# Optimizing a Trainium2 kernel written in Bass

```python
import jax, jax.numpy as jnp
from jax import lax
import numpy as np

D_MODEL = 1024
BATCH = 1
SEQ = 256
DEPTH = 2

CHUNK = 64
HG_HEADS = 4
HG_DK = 128
HG_W = HG_HEADS * HG_DK
RET_HEADS = 4
RET_DK = 128
RET_DV = 256
RET_QK = RET_HEADS * RET_DK
RET_V = RET_HEADS * RET_DV
ML_HEADS = 4
ML_DK = 128
ML_DV = 256
ML_QK = ML_HEADS * ML_DK
ML_V = ML_HEADS * ML_DV
CONV_W = 4
D_FF = 4 * D_MODEL
EPS = 1e-6
GATE_CAP = 15.0
ROPE_BASE = 10000.0
N_EVEN = (DEPTH + 1) // 2
N_ODD = DEPTH // 2
EVEN_IN = 4 * HG_W + 2 * RET_QK + 2 * RET_V
EVEN_OUT = HG_W + RET_V
ODD_IN = 2 * ML_QK + 2 * ML_V + 2 * ML_HEADS


def rmsnorm(x, g):
    xf = x.astype(jnp.float32)
    y = xf * lax.rsqrt(jnp.mean(xf * xf, axis=-1, keepdims=True) + EPS)
    return (y * g.astype(jnp.float32)).astype(x.dtype)

def head_rmsnorm(o, g, n_heads):
    b, s, w = o.shape
    return rmsnorm(o.reshape(b, s, n_heads, w // n_heads), g).reshape(b, s, w)

def to_chunks(x, n_heads):
    b, s, w = x.shape
    return x.reshape(b, s // CHUNK, CHUNK, n_heads, w // n_heads).transpose(1, 0, 3, 2, 4)

def gate_chunks(g):
    b, s, h = g.shape
    return g.reshape(b, s // CHUNK, CHUNK, h).transpose(1, 0, 3, 2)

def from_chunks(x):
    nc, b, h, c, d = x.shape
    return x.transpose(1, 0, 3, 2, 4).reshape(b, nc * c, h * d)

def rope(x, n_heads):
    b, s, w = x.shape
    dk = w // n_heads
    half = dk // 2
    xh = x.reshape(b, s, n_heads, dk)
    inv_freq = ROPE_BASE ** (-jnp.arange(half, dtype=jnp.float32) / half)
    ang = jnp.arange(s, dtype=jnp.float32)[:, None] * inv_freq[None, :]
    cos = jnp.cos(ang)[None, :, None, :]
    sin = jnp.sin(ang)[None, :, None, :]
    x1, x2 = xh[..., :half], xh[..., half:]
    return jnp.concatenate([x1 * cos - x2 * sin, x2 * cos + x1 * sin], axis=-1).reshape(b, s, w)

def hgrn2_scan(q, k, logf, v):
    nc, b, h, c, dk = q.shape
    dv = v.shape[-1]
    mask = jnp.tril(jnp.ones((c, c), dtype=bool))

    def step(state, inp):
        qc, kc, lfc, vc = inp
        bcum = jnp.cumsum(lfc, axis=2)
        diff = bcum[:, :, :, None, :] - bcum[:, :, None, :, :]
        decay = jnp.exp(jnp.where(mask[:, :, None], diff, -jnp.inf))
        scores = jnp.einsum('bhtd,bhsd,bhtsd->bhts', qc, kc, decay)
        out = jnp.einsum('bhts,bhsv->bhtv', scores, vc) \
            + jnp.einsum('bhtd,bhdv->bhtv', qc * jnp.exp(bcum), state)
        blast = bcum[:, :, -1, :]
        state = jnp.exp(blast)[..., None] * state \
            + jnp.einsum('bhsd,bhsv->bhdv', kc * jnp.exp(blast[:, :, None, :] - bcum), vc)
        return state, out

    init = jnp.zeros((b, h, dk, dv), jnp.float32)
    _, out = lax.scan(step, init, (q, k, logf, v))
    return out

def retention_scan(q, k, v):
    nc, b, h, c, dk = q.shape
    dv = v.shape[-1]
    mask = jnp.tril(jnp.ones((c, c), dtype=bool))
    lg = jnp.log1p(-jnp.exp2(-5.0 - jnp.arange(h, dtype=jnp.float32)))
    j = jnp.arange(c, dtype=jnp.float32)
    decay = jnp.where(mask, jnp.exp(lg[:, None, None] * (j[:, None] - j[None, :])), 0.0)
    q_decay = jnp.exp(lg[:, None] * (j + 1.0))[:, :, None]
    k_decay = jnp.exp(lg[:, None] * (c - 1.0 - j))[:, :, None]
    chunk_decay = jnp.exp(lg * c)[:, None, None]

    def step(state, inp):
        qc, kc, vc = inp
        scores = jnp.einsum('bhtd,bhsd->bhts', qc, kc) * decay
        out = jnp.einsum('bhts,bhsv->bhtv', scores, vc) \
            + jnp.einsum('bhtd,bhdv->bhtv', qc * q_decay, state)
        state = chunk_decay * state + jnp.einsum('bhsd,bhsv->bhdv', kc * k_decay, vc)
        return state, out

    init = jnp.zeros((b, h, dk, dv), jnp.float32)
    _, out = lax.scan(step, init, (q, k, v))
    return out

def mlstm_scan(q, k, v, lf, ig):
    nc, b, h, c, dk = q.shape
    dv = v.shape[-1]
    mask = jnp.tril(jnp.ones((c, c), dtype=bool))

    def step(carry, inp):
        cm, n, m = carry
        qc, kc, vc, lfc, igc = inp
        bcum = jnp.cumsum(lfc, axis=-1)
        logw = jnp.where(mask, bcum[..., :, None] - bcum[..., None, :] + igc[..., None, :], -jnp.inf)
        inter = bcum + m[..., None]
        m_row = jnp.maximum(inter, jnp.max(logw, axis=-1))
        w_intra = jnp.exp(logw - m_row[..., None])
        w_inter = jnp.exp(inter - m_row)
        scores = jnp.einsum('bhtd,bhsd->bhts', qc, kc) * w_intra
        num = jnp.einsum('bhts,bhsv->bhtv', scores, vc) \
            + w_inter[..., None] * jnp.einsum('bhtd,bhdv->bhtv', qc, cm)
        den = jnp.sum(scores, axis=-1) + w_inter * jnp.einsum('bhtd,bhd->bht', qc, n)
        out = num / jnp.maximum(jnp.abs(den), jnp.exp(-m_row))[..., None]
        blast = bcum[..., -1]
        logw_end = blast[..., None] - bcum + igc
        m_new = jnp.maximum(blast + m, jnp.max(logw_end, axis=-1))
        carry_scale = jnp.exp(blast + m - m_new)
        kw = kc * jnp.exp(logw_end - m_new[..., None])[..., None]
        cm = carry_scale[..., None, None] * cm + jnp.einsum('bhsd,bhsv->bhdv', kw, vc)
        n = carry_scale[..., None] * n + jnp.sum(kw, axis=2)
        return (cm, n, m_new), out

    init = (jnp.zeros((b, h, dk, dv), jnp.float32),
            jnp.zeros((b, h, dk), jnp.float32),
            jnp.zeros((b, h), jnp.float32))
    _, out = lax.scan(step, init, (q, k, v, lf, ig))
    return out

def causal_conv_silu(x, w, bias):
    s = x.shape[1]
    xp = jnp.pad(x, ((0, 0), (CONV_W - 1, 0), (0, 0)))
    y = sum(w[j].astype(jnp.float32) * xp[:, j:j + s, :] for j in range(CONV_W))
    return jax.nn.silu(y + bias.astype(jnp.float32))

def soft_cap(z):
    return GATE_CAP * jnp.tanh(z / GATE_CAP)

def even_mixer(h, w_in, lb, hg_norm_g, ret_norm_g, w_out):
    p = (h @ w_in).astype(jnp.float32)
    splits = [HG_W, 2 * HG_W, 3 * HG_W, 4 * HG_W, 4 * HG_W + RET_QK,
              4 * HG_W + 2 * RET_QK, 4 * HG_W + 2 * RET_QK + RET_V]
    hq, hf, hi, hgate, rq, rk, rv, rgate = jnp.split(p, splits, axis=-1)
    f = lb + (1.0 - lb) * jax.nn.sigmoid(hf)
    o_hg = from_chunks(hgrn2_scan(to_chunks(jax.nn.silu(hq), HG_HEADS), to_chunks(1.0 - f, HG_HEADS),
                                  to_chunks(jnp.log(f), HG_HEADS), to_chunks(hi, HG_HEADS)))
    o_hg = head_rmsnorm(o_hg, hg_norm_g, HG_HEADS) * jax.nn.silu(hgate)
    rq = rope(rq, RET_HEADS)
    rk = rope(rk, RET_HEADS) * RET_DK ** -0.5
    o_ret = from_chunks(retention_scan(to_chunks(rq, RET_HEADS), to_chunks(rk, RET_HEADS),
                                       to_chunks(rv, RET_HEADS)))
    o_ret = head_rmsnorm(o_ret, ret_norm_g, RET_HEADS) * jax.nn.silu(rgate)
    y = jnp.concatenate([o_hg, o_ret], axis=-1).astype(h.dtype)
    return y @ w_out

def odd_mixer(h, w_in, conv_w, conv_b, gate_b, ml_norm_g, w_out):
    p = (h @ w_in).astype(jnp.float32)
    splits = [2 * ML_QK, 2 * ML_QK + ML_V, 2 * ML_QK + 2 * ML_V, 2 * ML_QK + 2 * ML_V + ML_HEADS]
    qk, v, og, ig_pre, fg_pre = jnp.split(p, splits, axis=-1)
    qk = causal_conv_silu(qk, conv_w, conv_b)
    q, k = jnp.split(qk, 2, axis=-1)
    k = k * ML_DK ** -0.5
    gb = gate_b.astype(jnp.float32)
    ig = soft_cap(ig_pre + gb[0])
    lf = jax.nn.log_sigmoid(soft_cap(fg_pre + gb[1]))
    out = from_chunks(mlstm_scan(to_chunks(q, ML_HEADS), to_chunks(k, ML_HEADS), to_chunks(v, ML_HEADS),
                                 gate_chunks(lf), gate_chunks(ig)))
    y = (jax.nn.sigmoid(og) * head_rmsnorm(out, ml_norm_g, ML_HEADS)).astype(h.dtype)
    return y @ w_out

def sq_relu_mlp(h, w1, w2):
    return jnp.square(jax.nn.relu(h @ w1)) @ w2

def first_inputs(seed: int = 0) -> dict:
    key = jax.random.key(seed)
    ks = jax.random.split(key, 16)
    f32 = jnp.float32

    def nrm(k, shape, fan_in):
        return jax.random.normal(k, shape, f32) * fan_in ** -0.5

    x = jax.random.normal(ks[0], (BATCH, SEQ, D_MODEL), f32)
    norm_g = 1.0 + 0.05 * jax.random.normal(ks[1], (DEPTH, 4, D_MODEL), f32)
    hg_lower_bound = 0.5 * jax.random.normal(ks[2], (DEPTH + 1, HG_W), f32)
    ev_w_in = nrm(ks[3], (N_EVEN, D_MODEL, EVEN_IN), D_MODEL)
    ev_hg_norm_g = 1.0 + 0.05 * jax.random.normal(ks[4], (N_EVEN, HG_DK), f32)
    ev_ret_norm_g = 1.0 + 0.05 * jax.random.normal(ks[5], (N_EVEN, RET_DV), f32)
    ev_w_out = nrm(ks[6], (N_EVEN, EVEN_OUT, D_MODEL), EVEN_OUT)
    od_w_in = nrm(ks[7], (N_ODD, D_MODEL, ODD_IN), D_MODEL)
    od_conv_w = nrm(ks[8], (N_ODD, CONV_W, 2 * ML_QK), CONV_W)
    od_conv_b = 0.02 * jax.random.normal(ks[9], (N_ODD, 2 * ML_QK), f32)
    kg1, kg2 = jax.random.split(ks[10])
    i_bias = 0.1 * jax.random.normal(kg1, (N_ODD, ML_HEADS), f32)
    f_bias = jnp.linspace(3.0, 6.0, ML_HEADS, dtype=f32)[None, :] + 0.1 * jax.random.normal(kg2, (N_ODD, ML_HEADS), f32)
    od_gate_b = jnp.stack([i_bias, f_bias], axis=1)
    od_ml_norm_g = 1.0 + 0.05 * jax.random.normal(ks[11], (N_ODD, ML_DV), f32)
    od_w_out = nrm(ks[12], (N_ODD, ML_V, D_MODEL), ML_V)
    mlp_w1 = nrm(ks[13], (DEPTH, D_MODEL, D_FF), D_MODEL)
    mlp_w2 = nrm(ks[14], (DEPTH, D_FF, D_MODEL), D_FF)
    return {'x': x, 'norm_g': norm_g, 'hg_lower_bound': hg_lower_bound,
            'ev_w_in': ev_w_in, 'ev_hg_norm_g': ev_hg_norm_g, 'ev_ret_norm_g': ev_ret_norm_g,
            'ev_w_out': ev_w_out, 'od_w_in': od_w_in, 'od_conv_w': od_conv_w, 'od_conv_b': od_conv_b,
            'od_gate_b': od_gate_b, 'od_ml_norm_g': od_ml_norm_g, 'od_w_out': od_w_out,
            'mlp_w1': mlp_w1, 'mlp_w2': mlp_w2}

def first_block(x, norm_g, hg_lower_bound, ev_w_in, ev_hg_norm_g, ev_ret_norm_g, ev_w_out,
              od_w_in, od_conv_w, od_conv_b, od_gate_b, od_ml_norm_g, od_w_out, mlp_w1, mlp_w2):
    lower_bounds = jnp.cumsum(jax.nn.softmax(hg_lower_bound.astype(jnp.float32), axis=0), axis=0)
    for l in range(DEPTH):
        g = norm_g[l]
        h = rmsnorm(x, g[0])
        if l % 2 == 0:
            e = l // 2
            y = even_mixer(h, ev_w_in[e], lower_bounds[l], ev_hg_norm_g[e], ev_ret_norm_g[e], ev_w_out[e])
        else:
            o = l // 2
            y = odd_mixer(h, od_w_in[o], od_conv_w[o], od_conv_b[o], od_gate_b[o], od_ml_norm_g[o], od_w_out[o])
        x = x + rmsnorm(y, g[1])
        h = rmsnorm(x, g[2])
        x = x + rmsnorm(sq_relu_mlp(h, mlp_w1[l], mlp_w2[l]), g[3])
    return x


DEPTH_2 = 1

N_HEADS_ATTN = 8
HEAD_DIM = 64
ATTN_WIDTH = N_HEADS_ATTN * HEAD_DIM
MOBA_BLOCK = 256
MOBA_TOPK = 3
Q_CHUNK = 32
ROPE_THETA = 500000.0
ROT_DIM = HEAD_DIM // 4
CONV_WIDTH = 512
CONV_K = 3
N_BRANCH = 2
IN_COLS = 3 * ATTN_WIDTH + 3 * CONV_WIDTH + N_BRANCH * D_MODEL
N_GROUPS = 4
EXPERTS_PER_GROUP = 8
N_EXPERTS = N_GROUPS * EXPERTS_PER_GROUP
TOPK_IN_GROUP = 2
D_EXPERT = 512
MOE_BLOCK = 128
N_MOD = 6


def rms_norm(x, g):
    xf = x.astype(jnp.float32)
    y = xf * lax.rsqrt(jnp.mean(xf * xf, axis=-1, keepdims=True) + EPS)
    return (y * g.astype(jnp.float32)).astype(x.dtype)

def modulate(h, shift, scale):
    return h * (1 + scale[:, None, :]) + shift[:, None, :]

def rope_tables(seq_len, dtype):
    pos = jnp.arange(seq_len, dtype=jnp.float32)
    inv_freq = ROPE_THETA ** (-jnp.arange(0, ROT_DIM, 2, dtype=jnp.float32) / ROT_DIM)
    ang = pos[:, None] * inv_freq[None, :]
    return jnp.cos(ang).astype(dtype), jnp.sin(ang).astype(dtype)

def partial_rope(x, cos, sin):
    half = ROT_DIM // 2
    x1, x2, xp = x[..., :half], x[..., half:ROT_DIM], x[..., ROT_DIM:]
    return jnp.concatenate([x1 * cos - x2 * sin, x2 * cos + x1 * sin, xp], axis=-1)

def moba_attention(q, k, v):
    B, H, S, dh = q.shape
    nb = -(-S // MOBA_BLOCK)
    pad = nb * MOBA_BLOCK - S
    kb = jnp.pad(k, ((0, 0), (0, 0), (0, pad), (0, 0))).reshape(B, H, nb, MOBA_BLOCK, dh)
    vb = jnp.pad(v, ((0, 0), (0, 0), (0, pad), (0, 0))).reshape(B, H, nb, MOBA_BLOCK, dh)
    kmean = jnp.mean(kb.astype(jnp.float32), axis=3)
    topk = min(MOBA_TOPK, nb)
    scale = HEAD_DIM ** -0.5
    b_ix = jnp.arange(B)[:, None, None, None]
    h_ix = jnp.arange(H)[None, :, None, None]
    blk_ids = jnp.arange(nb)
    t_in_blk = jnp.arange(MOBA_BLOCK)

    def chunk(ci):
        q0 = ci * Q_CHUNK
        qc = lax.dynamic_slice_in_dim(q, q0, Q_CHUNK, axis=2)
        qpos = q0 + jnp.arange(Q_CHUNK)
        cur = q0 // MOBA_BLOCK
        gate = jnp.einsum('bhqd,bhnd->bhqn', qc.astype(jnp.float32), kmean)
        gate = jnp.where(blk_ids < cur, gate, -jnp.inf)
        _, sel = lax.top_k(gate, topk)
        sel_valid = jnp.arange(topk) < cur
        k_sel = kb[b_ix, h_ix, sel]
        v_sel = vb[b_ix, h_ix, sel]
        s_sel = jnp.einsum('bhqd,bhqntd->bhqnt', qc, k_sel).astype(jnp.float32) * scale
        s_sel = jnp.where(sel_valid[:, None], s_sel, -jnp.inf)
        k_own = lax.dynamic_index_in_dim(kb, cur, axis=2, keepdims=False)
        v_own = lax.dynamic_index_in_dim(vb, cur, axis=2, keepdims=False)
        s_own = jnp.einsum('bhqd,bhtd->bhqt', qc, k_own).astype(jnp.float32) * scale
        kpos = cur * MOBA_BLOCK + t_in_blk
        s_own = jnp.where(kpos[None, :] <= qpos[:, None], s_own, -jnp.inf)
        logits = jnp.concatenate([s_sel.reshape(B, H, Q_CHUNK, topk * MOBA_BLOCK), s_own], axis=-1)
        p = jax.nn.softmax(logits, axis=-1).astype(v.dtype)
        p_sel = p[..., :topk * MOBA_BLOCK].reshape(B, H, Q_CHUNK, topk, MOBA_BLOCK)
        p_own = p[..., topk * MOBA_BLOCK:]
        return (jnp.einsum('bhqnt,bhqntd->bhqd', p_sel, v_sel)
                + jnp.einsum('bhqt,bhtd->bhqd', p_own, v_own))

    out = lax.map(chunk, jnp.arange(S // Q_CHUNK))
    return out.transpose(1, 2, 0, 3, 4).reshape(B, H, S, dh)

def short_gated_conv(xb, bg, cg, conv_w, conv_b):
    u = cg * xb
    y = lax.conv_general_dilated(u, conv_w[:, None, :], window_strides=(1,), padding=[(CONV_K - 1, 0)],
                                 dimension_numbers=('NWC', 'WIO', 'NWC'), feature_group_count=CONV_WIDTH)
    return bg * (y + conv_b)

def hierarchical_moe(h, w_rg, b_rg, w_re, b_re, w1, w3, w2):
    B, S, D = h.shape
    T = B * S
    xt = h.reshape(T, D)
    g_logits = (xt @ w_rg).astype(jnp.float32) + b_rg.astype(jnp.float32)
    g_prob = jax.nn.softmax(g_logits, axis=-1)
    g_idx = jnp.argmax(g_logits, axis=-1)
    g_w = jnp.take_along_axis(g_prob, g_idx[:, None], axis=-1)
    e_logits = ((xt @ w_re).astype(jnp.float32) + b_re.astype(jnp.float32)).reshape(T, N_GROUPS, EXPERTS_PER_GROUP)
    e_logits = jnp.take_along_axis(e_logits, g_idx[:, None, None], axis=1)[:, 0]
    e_val, e_loc = lax.top_k(e_logits, TOPK_IN_GROUP)
    e_w = jax.nn.softmax(e_val, axis=-1) * g_w
    e_id = g_idx[:, None].astype(jnp.int32) * EXPERTS_PER_GROUP + e_loc.astype(jnp.int32)

    n_assign = T * TOPK_IN_GROUP
    flat_e = e_id.reshape(-1)
    flat_w = e_w.reshape(-1)
    order = jnp.argsort(flat_e)
    sorted_e = flat_e[order]
    counts = jnp.bincount(flat_e, length=N_EXPERTS)
    padded = (counts + MOE_BLOCK - 1) // MOE_BLOCK * MOE_BLOCK
    start = jnp.cumsum(counts) - counts
    pad_end = jnp.cumsum(padded)
    pad_start = pad_end - padded
    dest = pad_start[sorted_e] + (jnp.arange(n_assign) - start[sorted_e])
    n_pad = (-(-n_assign // MOE_BLOCK) + N_EXPERTS) * MOE_BLOCK
    n_blocks = n_pad // MOE_BLOCK
    tok = jnp.full((n_pad,), T, jnp.int32).at[dest].set((order // TOPK_IN_GROUP).astype(jnp.int32))
    wpad = jnp.zeros((n_pad,), jnp.float32).at[dest].set(flat_w[order])
    blk_start = jnp.arange(n_blocks) * MOE_BLOCK
    blk_expert = jnp.minimum(jnp.sum(pad_end[None, :] <= blk_start[:, None], axis=-1), N_EXPERTS - 1)
    x_ext = jnp.concatenate([xt, jnp.zeros((1, D), xt.dtype)], axis=0)
    xs = x_ext[tok].reshape(n_blocks, MOE_BLOCK, D)

    def expert_block(args):
        xb, e = args
        hid = jax.nn.silu(xb @ w1[e]) * (xb @ w3[e])
        return hid @ w2[e]

    ys = lax.map(expert_block, (xs, blk_expert)).reshape(n_pad, D)
    ys = ys * wpad[:, None].astype(ys.dtype)
    out = jnp.zeros((T + 1, D), ys.dtype).at[tok].add(ys)[:T]
    return out.reshape(B, S, D)

def second_inputs(seed: int = 0) -> dict:
    key = jax.random.key(seed)
    ks = jax.random.split(key, 24)
    L, D = DEPTH_2, D_MODEL
    f32 = jnp.float32
    nrm = lambda k, shape, s: jax.random.normal(k, shape, f32) * s
    return {
        "x": nrm(ks[0], (BATCH, SEQ, D), 1.0),
        "c": nrm(ks[1], (BATCH, D), 1.0),
        "w_ada": nrm(ks[2], (L, D, N_MOD * D), 0.5 * D ** -0.5),
        "b_ada": nrm(ks[3], (L, N_MOD * D), 0.02),
        "g_norm1": 1.0 + nrm(ks[4], (L, D), 0.02),
        "g_norm2": 1.0 + nrm(ks[5], (L, D), 0.02),
        "w_in": nrm(ks[6], (L, D, IN_COLS), D ** -0.5),
        "g_q": 1.0 + nrm(ks[7], (L, HEAD_DIM), 0.02),
        "g_k": 1.0 + nrm(ks[8], (L, HEAD_DIM), 0.02),
        "conv_w": nrm(ks[9], (L, CONV_K, CONV_WIDTH), CONV_K ** -0.5),
        "conv_b": nrm(ks[10], (L, CONV_WIDTH), 0.02),
        "w_pa": nrm(ks[11], (L, ATTN_WIDTH, D), ATTN_WIDTH ** -0.5),
        "w_pb": nrm(ks[12], (L, CONV_WIDTH, D), CONV_WIDTH ** -0.5),
        "w_o": nrm(ks[13], (L, D, D), D ** -0.5),
        "w_rg": nrm(ks[14], (L, D, N_GROUPS), D ** -0.5),
        "b_rg": nrm(ks[15], (L, N_GROUPS), 0.01),
        "w_re": nrm(ks[16], (L, D, N_EXPERTS), D ** -0.5),
        "b_re": nrm(ks[17], (L, N_EXPERTS), 0.01),
        "w1": nrm(ks[18], (L, N_EXPERTS, D, D_EXPERT), D ** -0.5),
        "w3": nrm(ks[19], (L, N_EXPERTS, D, D_EXPERT), D ** -0.5),
        "w2": nrm(ks[20], (L, N_EXPERTS, D_EXPERT, D), D_EXPERT ** -0.5),
    }

def second_block(x, c, w_ada, b_ada, g_norm1, g_norm2, w_in, g_q, g_k, conv_w, conv_b,
              w_pa, w_pb, w_o, w_rg, b_rg, w_re, b_re, w1, w3, w2):
    B, S, D = x.shape
    cos, sin = rope_tables(S, x.dtype)
    splits = [ATTN_WIDTH, 2 * ATTN_WIDTH, 3 * ATTN_WIDTH,
              3 * ATTN_WIDTH + CONV_WIDTH, 3 * ATTN_WIDTH + 2 * CONV_WIDTH, 3 * ATTN_WIDTH + 3 * CONV_WIDTH]
    for l in range(DEPTH_2):
        mod = jax.nn.silu(c) @ w_ada[l] + b_ada[l]
        sh1, sc1, ga1, sh2, sc2, ga2 = jnp.split(mod, N_MOD, axis=-1)

        h = modulate(rms_norm(x, g_norm1[l]), sh1, sc1)
        z = h @ w_in[l]
        q, k, v, xb, bg, cg, gates = jnp.split(z, splits, axis=-1)
        to_heads = lambda t: t.reshape(B, S, N_HEADS_ATTN, HEAD_DIM).transpose(0, 2, 1, 3)
        q = partial_rope(rms_norm(to_heads(q), g_q[l]), cos, sin)
        k = partial_rope(rms_norm(to_heads(k), g_k[l]), cos, sin)
        v = to_heads(v)
        y_a = moba_attention(q, k, v).transpose(0, 2, 1, 3).reshape(B, S, ATTN_WIDTH)
        y_b = short_gated_conv(xb, bg, cg, conv_w[l], conv_b[l])
        gate_a, gate_b = jnp.split(jax.nn.sigmoid(gates), N_BRANCH, axis=-1)
        merged = gate_a * (y_a @ w_pa[l]) + gate_b * (y_b @ w_pb[l])
        x = x + ga1[:, None, :] * (merged @ w_o[l])

        h2 = modulate(rms_norm(x, g_norm2[l]), sh2, sc2)
        x = x + ga2[:, None, :] * hierarchical_moe(h2, w_rg[l], b_rg[l], w_re[l], b_re[l], w1[l], w3[l], w2[l])
    return x


def setup_inputs(seed=0):
    out = dict(first_inputs(seed))
    for name, value in second_inputs(seed + 1).items():
        if name != "x":
            out[name + "_2"] = value
    return out


def reference(
    x, norm_g, hg_lower_bound, ev_w_in, ev_hg_norm_g, ev_ret_norm_g, ev_w_out, od_w_in,
    od_conv_w, od_conv_b, od_gate_b, od_ml_norm_g, od_w_out, mlp_w1, mlp_w2, c_2, w_ada_2,
    b_ada_2, g_norm1_2, g_norm2_2, w_in_2, g_q_2, g_k_2, conv_w_2, conv_b_2, w_pa_2, w_pb_2,
    w_o_2, w_rg_2, b_rg_2, w_re_2, b_re_2, w1_2, w3_2, w2_2,
):
    x = first_block(
        x, norm_g, hg_lower_bound, ev_w_in, ev_hg_norm_g, ev_ret_norm_g, ev_w_out, od_w_in,
        od_conv_w, od_conv_b, od_gate_b, od_ml_norm_g, od_w_out, mlp_w1, mlp_w2,
    )
    return second_block(
        x, c_2, w_ada_2, b_ada_2, g_norm1_2, g_norm2_2, w_in_2, g_q_2, g_k_2, conv_w_2,
        conv_b_2, w_pa_2, w_pb_2, w_o_2, w_rg_2, b_rg_2, w_re_2, b_re_2, w1_2, w3_2, w2_2,
    )


_drawn_inputs = setup_inputs


def setup_inputs(seed=0):
    import zlib

    import numpy as np

    out = dict(_drawn_inputs(seed))
    spreads = {}
    factors = {'hg_lower_bound': 2.865,
     'od_conv_b': 6.742,
     'b_ada_2': 5.265,
     'g_norm1_2': 8.0,
     'g_norm2_2': 35.877,
     'g_q_2': 64.0,
     'g_k_2': 64.0,
     'conv_b_2': 64.0,
     'b_rg_2': 64.0,
     'b_re_2': 64.0,
     'w_pa_2': 3.709}
    for name, (base, spread) in spreads.items():
        noise = np.random.default_rng([zlib.crc32(name.encode()), seed]).standard_normal(out[name].shape)
        drawn = base * np.exp(spread * noise) if base else spread * noise
        out[name] = __import__('jax').numpy.asarray(drawn.astype(out[name].dtype))
    for name, factor in factors.items():
        out[name] = (out[name] * factor).astype(out[name].dtype)
    return out
```

```python
from contextlib import ExitStack

import numpy as np

import concourse.bass as bass
from concourse import mybir

F32 = mybir.dt.float32
ALU = mybir.AluOpType
ACT = mybir.ActivationFunctionType
AX = mybir.AxisListType

P = 128
T = 256
TT = T // P
D = 1024
KT = D // P
FF = 4096
EPS = 1e-6
NB = 512
CH = 64
HG_H, HG_D = 4, 128
RV_H, RV_D = 4, 256
QK = 128
AH, AD = 8, 64
NE, NG, EG, DE = 32, 4, 8, 512
GCAP = 15.0
SLOTS = 4
BW = 4096
BIG = 1.0e30

EV_IN, ADA_A, EV_OUT = 10, 6, 3
MLP_B = 2 * (FF // NB)
OD_IN, ADA_B, OD_OUT = 6, 6, 2
IN2, PA, PB, WO = 10, 1, 1, 2
B_EV_IN = 0
B_ADA_A = B_EV_IN + EV_IN
B_EV_OUT = B_ADA_A + ADA_A
B_MLP0 = B_EV_OUT + EV_OUT
B_OD_IN = B_MLP0 + MLP_B
B_ADA_B = B_OD_IN + OD_IN
B_OD_OUT = B_ADA_B + ADA_B
B_MLP1 = B_OD_OUT + OD_OUT
B_IN2 = B_MLP1 + MLP_B
B_PA = B_IN2 + IN2
B_PB = B_PA + PA
B_WO = B_PB + PB
B_MOE = B_WO + WO

C_ID = 0
C_TRI = C_ID + P
C_CAU = C_TRI + P
C_NEG = C_CAU + P
C_SEL = C_NEG + 3 * P
C_CS2 = C_SEL + 4 * P
C_FIRST = C_CS2 + 4 * 8
C_ONE = C_FIRST + 8
C_KEEP = C_ONE + P
M_LEV = 0
M_DEC = M_LEV + 8 * P
M_CS = M_DEC + 4 * 3 * P
M_END = M_CS + 4 * 64

R_G = 0
R_CW = 32
R_CB = 64
R_G1, R_G2 = 72, 80
R_CW2 = 88
R_CB2 = 100
R_C = 104
R_END = 112


def shape_constants():
    i = np.arange(P)
    s, t = i[:, None], i[None, :]
    keep = np.zeros((P, C_KEEP), np.float32)
    keep[:, C_ID:C_ID + P] = s == t
    keep[:, C_TRI:C_TRI + P] = (s <= t) & (s // CH == t // CH)
    keep[:, C_CAU:C_CAU + P] = s <= t
    neg = np.where(t > s, -BIG, 0.0)
    keep[:, C_NEG:C_NEG + P] = neg
    keep[:, C_NEG + 2 * P:C_NEG + 3 * P] = neg
    for h in range(4):
        keep[h, C_SEL + h * P:C_SEL + (h + 1) * P] = 1.0
    pos = np.arange(T, dtype=np.float32)
    half = 8
    inv = (500000.0 ** (-np.arange(0, 2 * half, 2, dtype=np.float32) / np.float32(2 * half))).astype(np.float32)
    ang = (pos[:, None] * inv[None, :]).astype(np.float32)
    for tt in range(TT):
        keep[:, C_CS2 + tt * 8:C_CS2 + tt * 8 + 8] = np.cos(ang[tt * P:(tt + 1) * P])
        keep[:, C_CS2 + 16 + tt * 8:C_CS2 + 16 + tt * 8 + 8] = np.sin(ang[tt * P:(tt + 1) * P])
    keep[:, C_FIRST:C_FIRST + 8] = np.arange(8, 0, -1)
    keep[:, C_ONE:C_ONE + P] = 1.0
    mix = np.zeros((P, M_END), np.float32)
    mix[:, M_LEV:M_LEV + P] = s == t
    for n in range(7):
        m = 1 << n
        mix[:, M_LEV + (n + 1) * P:M_LEV + (n + 2) * P] = (
            (s // (2 * m) == t // (2 * m)) & (s // m % 2 == 0) & (t // m % 2 == 1))
    for h in range(4):
        lg = np.log1p(-np.exp2(-5.0 - h))
        at = M_DEC + h * 3 * P
        diag = np.where(s <= t, np.exp(lg * (t - s)), 0.0)
        mix[:, at:at + P] = diag
        mix[:, at + P:at + 2 * P] = np.exp(lg * (t + P - s))
        mix[:, at + 2 * P:at + 3 * P] = diag
    inv = (10000.0 ** (-np.arange(64, dtype=np.float32) / np.float32(64))).astype(np.float32)
    ang = (pos[:, None] * inv[None, :]).astype(np.float32)
    for tt in range(TT):
        mix[:, M_CS + tt * 64:M_CS + tt * 64 + 64] = np.cos(ang[tt * P:(tt + 1) * P])
        mix[:, M_CS + 128 + tt * 64:M_CS + 128 + tt * 64 + 64] = np.sin(ang[tt * P:(tt + 1) * P])
    return keep, mix


def block_program(nc, A, out, dump=None):
    ctx = ExitStack()
    with ctx:
        sems = {}

        def sem(name):
            if name not in sems:
                sems[name] = ctx.enter_context(nc.semaphore(name))
            return sems[name]

        def sb(name, *shape):
            return ctx.enter_context(nc.sbuf_tensor(name, list(shape), F32))

        X = sb("x_rows", P, TT, D)
        XN = sb("xn_rows", P, TT, D)
        HT = sb("h_cols", P, KT, T)
        PR = sb("proj_rows", P, TT, 10 * NB)
        W = sb("weights", P, SLOTS, BW)
        AR = sb("arena", P, 14592)
        GA = sb("ga_rows", P, 2, D)
        CK = sb("constants", P, C_KEEP)
        GC = sb("g_cols", P, R_END)
        BC = sb("b_ada_cols", P, 48)
        MC = sb("mod_cols", P, 4, KT)
        GM = sb("gain_cols", P, 2, KT)
        ST = sb("stats", P, 256)
        HN = sb("head_gains", P, 128 + 256 + 256 + 128)
        RB = sb("router_bias", P, NG + NE)
        WR = sb("router_weights", P, KT, NG + NE)
        WG = sb("gate_weights", P, KT, 8)
        G4 = sb("gate_bias", 4, 4)
        PS = ctx.enter_context(nc.psum_tensor("PS", [P, 8, NB], F32))

        GB = PR[:, 0, 0:D]

        def ar(at, *shape):
            n = int(np.prod(shape))
            v = AR[:, at:at + n]
            if len(shape) == 1:
                return v
            names = "abcd"[:len(shape)]
            return v.rearrange(f"p ({' '.join(names)}) -> p {' '.join(names)}",
                               **{c: k for c, k in zip(names[:-1], shape[:-1])})

        K1 = 1024
        QT, KTT, BT = ar(0, 4, T), ar(K1, 4, T), ar(2 * K1, 4, T)
        EX = [ar((3 + i) * K1, K1) for i in range(2)]
        QS = [ar((5 + i) * K1, 4, T) for i in range(2)]
        KS = [ar((7 + i) * K1, 4, T) for i in range(2)]
        SC = ar(9 * K1, 8, P)
        TMP = ar(10 * K1, K1)
        S01 = ar(11 * K1, 4, P)
        MX = ar(11 * K1 + 512, M_END)
        LB = ar(3 * K1, 3, 512)
        BO = ar(10 * K1, 512)
        LF = ar(5 * K1, 2, 512)
        RR = XN[:, :, :]
        RT = ar(0, 8, T)
        PT = ar(2 * K1, 4, 3 * P)
        HB = ar(4 * K1, 2 * K1)
        YT = ar(8 * K1, 12, T)
        CR = ar(11 * K1, 8 * (T + 3))
        CRv = CR.rearrange("p (a b) -> p a b", a=8)
        CT = ar(0, 8, T)
        HBW = ar(6 * K1, 4, 3 * P)
        GR = AR[0:4, 4 * K1:6 * K1].rearrange("p (a b) -> p a b", a=8)
        T2 = ar(0, 8, T)
        AS = ar(2 * K1, AH, 3 * P)
        APT = ar(5 * K1, 24, P)
        UT = ar(8 * K1, 4 * (T + 2))
        UTv = UT.rearrange("p (a b) -> p a b", a=4)
        BGT = ar(9 * K1 + 16, 4, T)
        YBT = ar(10 * K1 + 16, 4, T)
        YAT = ar(11 * K1 + 16, 4, T)
        YA = ar(12 * K1 + 16, 2, 512)
        MT = ar(0, 8, T)
        H1 = [ar(i * K1, 4, T) for i in range(2)]
        SG = [ar(2 * K1 + 512 * i, 2, T) for i in range(2)]
        SG2 = [ar(3 * K1 + 512 * i, 2, T) for i in range(2)]
        HR = [ar(2 * K1 + 512 * i, 2, T) for i in range(4)]
        CBE = PR[:, :, :].rearrange("p a b -> p (a b)")[:, 0:NE * T].rearrange("p (e t) -> p e t", e=NE)
        CWC = ar(8 * K1, TT, NE)

        CS = ST[:, 104:112]
        IDN = CK[:, C_ID:C_ID + P]
        ONE = CK[:, C_ONE:C_ONE + P]

        def colb(ap, n):
            return ap.unsqueeze(2).to_broadcast([P, ap.shape[1], n])

        def midb(ap, n):
            return ap.unsqueeze(1).to_broadcast([P, n, ap.shape[1]])

        def slot_of(b):
            return b % SLOTS

        def fulls(b):
            return 16 * (b // SLOTS + 1)

        def n_type(w, at):
            return w[:, bass.ds(at, NB)].rearrange("(k p) n -> p k n", p=P)

        def k_type(w, at):
            return w[bass.ds(at, NB), :].rearrange("(k p) n -> p k n", p=P)

        def wn(s):
            return W[:, s, :].rearrange("p (k n) -> p k n", k=KT)

        def wk(s):
            return W[:, s, :].rearrange("p (k n) -> p k n", k=4)

        block = ctx.enter_context(nc.Block())

        @block.sync
        def _(sp):
            def load(b, src):
                s = slot_of(b)
                if b >= SLOTS:
                    sp.wait_ge(sem("block_used"), b - SLOTS + 1)
                sp.dma_start(W[:, s, :].rearrange("p (k n) -> p k n", n=src.shape[2]), src)\
                  .then_inc(sem(f"slot{s}_full"), 16)

            for b in range(EV_IN):
                load(B_EV_IN + b, n_type(A["ev_w_in"][0], b * NB))
            for b in range(ADA_A):
                load(B_ADA_A + b, n_type(A["w_ada_2"][0], b * NB))
            for b in range(EV_OUT):
                load(B_EV_OUT + b, k_type(A["ev_w_out"][0], b * NB))

            def mlp_loads(l, base):
                with sp.Fori(0, FF // NB // 2) as i:
                    for c in range(4):
                        s = slot_of(base + c)
                        sp.wait_ge(sem("block_used"), i * 4 + (base + c - SLOTS + 1))
                        g = i * (2 * NB) + (c // 2) * NB
                        src = n_type(A["mlp_w1"][l], g) if c % 2 == 0 else k_type(A["mlp_w2"][l], g)
                        sp.dma_start(W[:, s, :].rearrange("p (k n) -> p k n", n=src.shape[2]), src)\
                          .then_inc(sem(f"slot{s}_full"), 16)

            mlp_loads(0, B_MLP0)
            for b in range(OD_IN):
                load(B_OD_IN + b, n_type(A["od_w_in"][0], b * NB))
            for b in range(ADA_B):
                load(B_ADA_B + b, n_type(A["w_ada_2"][0], (ADA_A + b) * NB))
            for b in range(OD_OUT):
                load(B_OD_OUT + b, k_type(A["od_w_out"][0], b * NB))
            mlp_loads(1, B_MLP1)
            for b in range(IN2):
                load(B_IN2 + b, n_type(A["w_in_2"][0], b * NB))
            load(B_PA, k_type(A["w_pa_2"][0], 0))
            load(B_PB, k_type(A["w_pb_2"][0], 0))
            for b in range(WO):
                load(B_WO + b, k_type(A["w_o_2"][0], b * NB))

            w1f = A["w1_2"][0].rearrange("e d f -> (e d) f")
            w3f = A["w3_2"][0].rearrange("e d f -> (e d) f")
            w2f = A["w2_2"][0].rearrange("e d f -> (e d) f")
            with sp.Fori(0, NE // 4) as i:
                for c in range(12):
                    e, kind = c // 3, c % 3
                    b = B_MOE + c
                    s = slot_of(b)
                    sp.wait_ge(sem("block_used"), i * 12 + (b - SLOTS + 1))
                    if kind < 2:
                        w = (w1f, w3f)[kind]
                        src = w[bass.ds(i * (4 * D) + e * D, D), :].rearrange("(k p) n -> p k n", p=P)
                    else:
                        src = w2f[bass.ds(i * (4 * DE) + e * DE, DE), :].rearrange("(k p) n -> p k n", p=P)
                    sp.dma_start(W[:, s, :].rearrange("p (k n) -> p k n", n=src.shape[2]), src)\
                      .then_inc(sem(f"slot{s}_full"), 16)

            for tt in range(TT):
                sp.wait_ge(sem("x_final"), tt + 1)
                sp.dma_start(out[0].rearrange("(t p) n -> p t n", p=P)[:, tt, :], X[:, tt, :])\
                  .then_inc(sem("out_stored"), 16)
            sp.wait_ge(sem("out_stored"), 32)
            if dump is not None:
                sp.dma_start(dump, X[:, :, :]).then_inc(sem("out_stored"), 16)
                sp.wait_ge(sem("out_stored"), 48)

        @block.gpsimd
        def _(pool):
            powers = [0]

            def power(a, b):
                powers[0] += 1
                pool.wait_ge(sem("mean_ready"), powers[0])
                nc.gpsimd.tensor_tensor(ST[:, a:b], ST[:, a:b], ST[:, 192:192 + b - a], ALU.pow)\
                    .then_inc(sem("rstd_ready"), 1)

            def gains(r, name, count):
                pool.wait_ge(sem(name), count)
                nc.gpsimd.dma_start(GB, A["norm_g"][r // 2, 1 + 2 * (r % 2)].partition_broadcast(P))\
                    .then_inc(sem("gain_in"), 16)

            nc.gpsimd.memset(ST[:, 192:224], -0.5).then_inc(sem("half_ready"), 1)
            pool.wait_ge(sem("half_ready"), 1)
            power(0, 2)
            pool.wait_ge(sem("hg_kT"), 2)
            for n in range(8):
                pool.wait_ge(sem("hg_exp"), n + 1)
                if n >= 2:
                    pool.wait_ge(sem("hg_prod"), n)
                nc.gpsimd.tensor_tensor(KS[n % 2], KTT, EX[n % 2].rearrange("p (a b) -> p a b", a=4),
                                        ALU.mult).then_inc(sem("hg_ks"), 1)
            power(16, 24)
            power(16, 24)
            gains(0, "mix_T", 6)
            power(2, 4)
            gains(1, "res_done", 1)
            power(0, 2)
            power(2, 4)
            power(0, 2)
            power(16, 24)
            gains(2, "mix_T", 10)
            power(2, 4)
            gains(3, "res_done", 3)
            power(0, 2)
            power(2, 4)
            power(0, 2)
            power(128, 160)
            power(0, 2)

        @block.tensor
        def _(pe):
            mm = nc.tensor.matmul

            def quad(bank, srcs):
                for j, s in enumerate(srcs):
                    last = nc.tensor.transpose(PS[:, bank, j * P:(j + 1) * P], s, IDN)
                return last

            def transpose_stream(n):
                for q in range(4):
                    tt, half = q // 2, q % 2
                    if half == 0:
                        pe.wait_ge(sem("xn_ready"), 2 * n + tt + 1)
                    quad(4 + q, [XN[:, tt, (4 * half + j) * P:(4 * half + j + 1) * P] for j in range(4)])\
                        .then_inc(sem("xT_ready"), 1)

            proj_n = [0]

            def proj_block(b, lhs=None):
                s, n = slot_of(b), proj_n[0]
                pe.wait_ge(sem(f"slot{s}_full"), fulls(b))
                if n >= 2:
                    pe.wait_ge(sem("proj_taken"), n - 1)
                for tt in range(TT):
                    for k in range(KT):
                        last = mm(PS[:, 2 * (n % 2) + tt, :], HT[:, k, tt * P:(tt + 1) * P], wn(s)[:, k, :],
                                  start=(k == 0), stop=(k == KT - 1))
                last.then_inc(sem("proj_ready"), 1)
                proj_n[0] += 1
                pe.wait_ge(sem("proj_ready"), proj_n[0])
                pe.sem_inc(sem("block_used"), 1)

            def ada(j):
                b = B_ADA_A + j if j < ADA_A else B_ADA_B + j - ADA_A
                s, bank = slot_of(b), 2 * (j % 2)
                pe.wait_ge(sem(f"slot{s}_full"), fulls(b))
                if j >= 2:
                    pe.wait_ge(sem("ada_taken"), j - 1)
                if j // 2 in (2, 5):
                    for k in range(KT):
                        last = mm(PS[:, bank, :], CS[:, k:k + 1].to_broadcast([P, P]), wn(s)[:, k, :],
                                  start=(k == 0), stop=(k == KT - 1))
                else:
                    for n in range(4):
                        for k in range(KT):
                            last = mm(PS[:, bank, n:n + 1], wn(s)[:, k, n * P:(n + 1) * P], CS[:, k:k + 1],
                                      start=(k == 0), stop=(k == KT - 1))
                last.then_inc(sem("ada_ready"), 1)
                pe.wait_ge(sem("ada_ready"), j + 1)
                pe.sem_inc(sem("block_used"), 1)

            def out_block(b, lhs, k0, first, last_k, bank=0):
                s = slot_of(b)
                pe.wait_ge(sem(f"slot{s}_full"), fulls(b))
                for kk in range(4):
                    for tt in range(TT):
                        for n in range(2):
                            last = mm(PS[:, bank + 2 * tt + n, :], lhs[:, k0 + kk, tt * P:(tt + 1) * P],
                                      wk(s)[:, kk, n * NB:(n + 1) * NB],
                                      start=(first and kk == 0), stop=(last_k and kk == 3))
                last.then_inc(sem("block_used"), 1)
                return last

            pe.wait_ge(sem("rows_in"), 16 * 12)
            pe.wait_ge(sem("const_in"), 16)
            nc.tensor.transpose(PS[:, 0, 0:R_END], AR[0:R_END, 0:P], IDN[0:R_END, 0:R_END])
            nc.tensor.transpose(PS[:, 1, 0:48], AR[0:48, P:2 * P], IDN[0:48, 0:48])\
                .then_inc(sem("cols_ready"), 1)

            transpose_stream(0)
            pe.wait_ge(sem("cols_taken"), 1)
            pe.wait_ge(sem("hT_ready"), 4)
            for b in range(2):
                proj_block(B_EV_IN + b)
            pe.wait_ge(sem("proj_taken"), 1)
            for tt in range(TT):
                last = quad(4 + tt, [PR[:, tt, h * P:(h + 1) * P] for h in range(4)])
            last.then_inc(sem("hg_qT_raw"), 1)
            proj_block(B_EV_IN + 2)
            pe.wait_ge(sem("hg_f"), 1)
            for tt in range(TT):
                last = quad(6 + tt, [PR[:, tt, NB + h * P:NB + (h + 1) * P] for h in range(4)])
            last.then_inc(sem("hg_fT_raw"), 1)
            pe.wait_ge(sem("hg_lf"), 1)
            pe.wait_ge(sem("hg_qT"), 2)
            for tt in range(TT):
                for h in range(4):
                    last = mm(PS[:, 4 + tt, h * P:(h + 1) * P], LF[:, tt, h * P:(h + 1) * P],
                              CK[:, C_TRI:C_TRI + P], start=True, stop=True)
            last.then_inc(sem("hg_b_raw"), 1)

            def level(n):
                if n == 0:
                    pe.wait_ge(sem("hg_kT"), 2)
                    q, k = QT, KTT
                    pe.wait_ge(sem("hg_bT"), 2)
                else:
                    pe.wait_ge(sem("hg_qs"), n)
                    pe.wait_ge(sem("hg_ks"), n)
                    q, k = QS[(n - 1) % 2], KS[(n - 1) % 2]
                if n >= 2:
                    pe.wait_ge(sem("hg_masked"), n - 1)
                bank = 4 + 2 * (n % 2)
                if n == 8:
                    for h in range(4):
                        last = mm(PS[:, bank, h * P:(h + 1) * P], k[:, h, 0:P], q[:, h, P:T],
                                  start=True, stop=True)
                else:
                    for tt in range(TT):
                        for h in range(4):
                            last = mm(PS[:, bank + tt, h * P:(h + 1) * P], k[:, h, tt * P:(tt + 1) * P],
                                      q[:, h, tt * P:(tt + 1) * P], start=True, stop=True)
                last.then_inc(sem("hg_prod"), 1)

            level(0)
            for n in range(1, 9):
                if n + 2 < EV_IN:
                    proj_block(B_EV_IN + n + 2)
                level(n)
            pe.wait_ge(sem("hg_masked"), 8)
            pe.wait_ge(sem("hg_s01"), 1)
            for tt in range(TT):
                for h in range(4):
                    o = PS[:, 6 + tt, h * P:(h + 1) * P]
                    last = mm(o, SC[:, 4 * tt + h, :], PR[:, tt, 2 * NB + h * P:2 * NB + (h + 1) * P],
                              start=True, stop=(tt == 0))
                    if tt:
                        last = mm(o, S01[:, h, :], PR[:, 0, 2 * NB + h * P:2 * NB + (h + 1) * P],
                                  start=False, stop=True)
            last.then_inc(sem("hg_out"), 1)
            pe.wait_ge(sem("c_silu"), 1)

            def retention():
                pe.wait_ge(sem("rope_done"), 1)
                pe.wait_ge(sem("hg_y"), 1)
                for q in range(4):
                    tt, half = q // 2, q % 2
                    last = quad(4 + q, [RR[:, tt, (4 * half + j) * P:(4 * half + j + 1) * P] for j in range(4)])
                    last.then_inc(sem("ret_T_raw"), 1)
                pe.wait_ge(sem("ret_T"), 4)
                for h in range(4):
                    mm(PS[:, 4 + h, 0:T], RT[:, 4 + h, 0:P], RT[:, h, 0:T], start=True, stop=True)
                    mm(PS[:, 4 + h, T:T + P], RT[:, 4 + h, P:T], RT[:, h, P:T], start=True, stop=True)\
                        .then_inc(sem("ret_s"), 1)

            def values(col, ready, n, dens=None):
                for tt in range(TT):
                    for h in range(4):
                        if tt == 0:
                            pe.wait_ge(sem(ready), h + 1)
                        v = slice(col + h * RV_D, col + (h + 1) * RV_D)
                        o = PS[:, 2 * tt + h // 2, (h % 2) * RV_D:(h % 2 + 1) * RV_D]
                        parts = [(PT[:, h, 0:P], 0)] if tt == 0 else [(PT[:, h, P:2 * P], 0), (PT[:, h, 2 * P:3 * P], 1)]
                        for i, (left, st) in enumerate(parts):
                            last = mm(o, left, PR[:, st, v], start=(i == 0), stop=(i == len(parts) - 1))
                        if dens is not None:
                            for i, (left, st) in enumerate(parts):
                                last = mm(dens[:, 4 * tt + h:4 * tt + h + 1], left, ONE[:, 0:1],
                                          start=(i == 0), stop=(i == len(parts) - 1))
                last.then_inc(sem(n), 1)

            def mixed_T(srcs, evac_name, ready, base, first_bank_wait=None):
                for q, (tt, col, wv) in enumerate(srcs):
                    pe.wait_ge(sem(ready), wv)
                    if q >= 4:
                        pe.wait_ge(sem(evac_name), base + q - 3)
                    quad(4 + q % 4, [PR[:, tt, col + j * P:col + (j + 1) * P] for j in range(4)])\
                        .then_inc(sem(evac_name + "_raw"), 1)

            retention()
            pe.wait_ge(sem("proj_taken"), EV_IN)
            for j in range(ADA_A):
                ada(j)
            pe.wait_ge(sem("ada_taken"), ADA_A)
            values(3072, "ret_p", "ret_out")
            mixed_T([(0, 1536, 1), (1, 1536, 1), (0, 4096, 2), (1, 4096, 2), (0, 4608, 2), (1, 4608, 2)],
                    "mix_T", "ev_y", 0)
            pe.wait_ge(sem("mix_T"), 6)
            for i in range(EV_OUT):
                last = out_block(B_EV_OUT + i, YT, 4 * i, i == 0, i == EV_OUT - 1)
            pe.wait_ge(sem("block_used"), B_EV_OUT + EV_OUT)
            pe.sem_inc(sem("y_ready"), 1)

            hidden_n = [0]

            def mlp(l, base, norm):
                transpose_stream(norm)
                pe.wait_ge(sem("hT_ready"), 4 * norm + 4)

                def up(s, full, h, first):
                    pe.wait_ge(sem(f"slot{s}_full"), full)
                    for j in range(4):
                        bank = 4 + 2 * h + j // 2
                        if j % 2 == 0 and not first:
                            pe.wait_ge(sem("hid_relu"), first_wait(j))
                        for k in range(KT):
                            last = mm(PS[:, bank, (j % 2) * T:(j % 2 + 1) * T],
                                      wn(s)[:, k, j * P:(j + 1) * P], HT[:, k, :],
                                      start=(k == 0), stop=(k == KT - 1))
                        if j % 2:
                            last.then_inc(sem("hid_raw"), 1)

                def first_wait(j):
                    return wait_base[0] + j // 2 + 1

                def down(s, full, h, hid, start, stop):
                    pe.wait_ge(sem(f"slot{s}_full"), full)
                    pe.wait_ge(sem("hid_ready"), hid)
                    for kk in range(4):
                        for tt in range(TT):
                            for n in range(2):
                                last = mm(PS[:, 2 * tt + n, :], H1[h][:, kk, tt * P:(tt + 1) * P],
                                          wk(s)[:, kk, n * NB:(n + 1) * NB],
                                          start=(start and kk == 0), stop=(stop and kk == 3))
                    last.then_inc(sem("block_used"), 1)

                H0 = l * 2 * (FF // NB)
                wait_base = [0]

                def group(g, i, c, start, stop):
                    h = (c // 2) % 2
                    s1, s2 = slot_of(base + c), slot_of(base + c + 1)
                    f1, f2 = fulls(base + c), fulls(base + c + 1)
                    f1 = i * 16 + f1
                    f2 = i * 16 + f2
                    up_wait = i * 4 + (H0 + c - 4)
                    wait_base[0] = up_wait
                    up(s1, f1, h, first=start)
                    last = None
                    pe.wait_ge(sem("hid_raw"), i * 4 + (H0 + c + 2))
                    pe.sem_inc(sem("block_used"), 1)
                    down(s2, f2, h, i * 4 + (H0 + c + 2), start, stop)

                wait_base[0] = 0
                for c in (0, 2):
                    h = c // 2
                    up(slot_of(base + c), fulls(base + c), h, first=True)
                    pe.wait_ge(sem("hid_raw"), H0 + c + 2)
                    pe.sem_inc(sem("block_used"), 1)
                    down(slot_of(base + c + 1), fulls(base + c + 1), h, H0 + c + 2, c == 0, False)
                with pe.Fori(1, FF // NB // 2 - 1) as i:
                    for c in (0, 2):
                        group(None, i, c, False, False)
                for c in (0, 2):
                    i = FF // NB // 2 - 1
                    h = c // 2
                    wait_base[0] = 4 * i + H0 + c - 4
                    up(slot_of(base + c), fulls(base + c) + 16 * i, h, first=False)
                    pe.wait_ge(sem("hid_raw"), H0 + 4 * i + c + 2)
                    pe.sem_inc(sem("block_used"), 1)
                    down(slot_of(base + c + 1), fulls(base + c + 1) + 16 * i, h, H0 + 4 * i + c + 2, False, c == 2)
                pe.wait_ge(sem("block_used"), base + MLP_B)
                pe.sem_inc(sem("y_ready"), 1)

            mlp(0, B_MLP0, 1)

            transpose_stream(2)
            pe.wait_ge(sem("hT_ready"), 12)
            for b in range(2):
                proj_block(B_OD_IN + b)
            pe.wait_ge(sem("gate_in"), 48)
            for g in range(2):
                for k in range(KT):
                    last = mm(PS[0:4, 7, g * T:(g + 1) * T], WG[:, k, 4 * g:4 * g + 4], HT[:, k, :],
                              start=(k == 0), stop=(k == KT - 1))
            last.then_inc(sem("gates_raw"), 1)
            for b in range(2, 4):
                proj_block(B_OD_IN + b)
            pe.wait_ge(sem("gates_taken"), 1)
            pe.wait_ge(sem("proj_taken"), EV_IN + 2)
            for q in range(4):
                tt, half = q // 2, q % 2
                quad(4 + q, [PR[:, tt, (4 * half + j) * P:(4 * half + j + 1) * P] for j in range(4)])\
                    .then_inc(sem("conv_T_raw"), 1)
            for b in range(4, 6):
                proj_block(B_OD_IN + b)
            pe.wait_ge(sem("conv_T"), 4)
            pe.wait_ge(sem("gates_done"), 1)
            for j, row in enumerate((3, 6)):
                for tt in range(TT):
                    last = mm(PS[:, 4, 8 * j + 4 * tt:8 * j + 4 * tt + 4], GR[:, row, tt * P:(tt + 1) * P],
                              IDN[0:4, 0:4], start=True, stop=True)
            last.then_inc(sem("acol_raw"), 1)
            for h in range(4):
                last = mm(PS[:, 5 + h // 2, (h % 2) * T:(h % 2 + 1) * T], CK[0:4, C_SEL + h * P:C_SEL + (h + 1) * P],
                          GR[:, 4, :], start=True, stop=True)
            last.then_inc(sem("mrow_raw"), 1)
            pe.wait_ge(sem("proj_taken"), EV_IN + OD_IN)
            for j in range(ADA_A, ADA_A + ADA_B // 2):
                ada(j)
            pe.wait_ge(sem("conv_done"), 1)
            pe.wait_ge(sem("wexp_in"), 1)
            for h in range(4):
                mm(PS[:, 4 + h, 0:T], CT[:, 4 + h, 0:P], CT[:, h, 0:T], start=True, stop=True)
                mm(PS[:, 4 + h, T:T + P], CT[:, 4 + h, P:T], CT[:, h, P:T], start=True, stop=True)\
                    .then_inc(sem("ml_s"), 1)
            for j in range(ADA_A + ADA_B // 2, ADA_A + ADA_B):
                ada(j)
            pe.wait_ge(sem("ada_taken"), ADA_A + ADA_B)
            pe.wait_ge(sem("ml_p"), 4)
            values(1024, "ml_p", "ml_out", dens=PS[:, 4, 0:8])
            pe.wait_ge(sem("ml_taken"), 1)
            mixed_T([(0, 2048, 1), (1, 2048, 1), (0, 2560, 1), (1, 2560, 1)], "mix_T", "od_y", 6)
            pe.wait_ge(sem("mix_T"), 10)
            for i in range(OD_OUT):
                out_block(B_OD_OUT + i, YT, 4 * i, i == 0, i == OD_OUT - 1)
            pe.wait_ge(sem("block_used"), B_OD_OUT + OD_OUT)
            pe.sem_inc(sem("y_ready"), 1)
            mlp(1, B_MLP1, 3)

            transpose_stream(4)
            pe.wait_ge(sem("hT_ready"), 20)
            E0 = EV_IN + OD_IN
            for b in range(6):
                proj_block(B_IN2 + b)
            pe.wait_ge(sem("qk_ready"), 1)
            for q in range(4):
                tt, half = q // 2, q % 2
                quad(4 + q, [PR[:, tt, (4 * half + j) * P:(4 * half + j + 1) * P] for j in range(4)])\
                    .then_inc(sem("qk_T_raw"), 1)
            proj_block(B_IN2 + 6)
            pe.wait_ge(sem("u_ready"), 1)
            pe.wait_ge(sem("qk_T"), 4)
            for q, col in enumerate((1536, 2048)):
                for tt in range(TT):
                    quad(4 + 2 * q + tt, [PR[:, tt, col + j * P:col + (j + 1) * P] for j in range(4)])\
                        .then_inc(sem("u_T_raw"), 1)
            proj_block(B_IN2 + 7)
            pe.wait_ge(sem("u_T"), 4)

            def logits(h):
                pr = slice(64 * (h % 2), 64 * (h % 2) + 64)
                bank = 4 + h % 4
                if h >= 4:
                    pe.wait_ge(sem("at_s"), h - 3)
                mm(PS[:, bank, 0:P], T2[pr, h // 2, 0:P], T2[pr, 4 + h // 2, 0:P], start=True, stop=True)
                mm(PS[:, bank, P:3 * P], T2[pr, h // 2, P:T], T2[pr, 4 + h // 2, 0:T], start=True, stop=True)\
                    .then_inc(sem("at_s_raw"), 1)

            for h in range(AH):
                logits(h)
            for b in range(8, 10):
                proj_block(B_IN2 + b)
            pe.wait_ge(sem("at_s"), 8)
            pe.wait_ge(sem("at_p"), 1)
            flat = AS.rearrange("p h (x s) -> p (h x) s", x=3)
            for q in range(6):
                if q >= 4:
                    pe.wait_ge(sem("at_pT"), q - 3)
                quad(4 + q % 4, [flat[:, 4 * q + j, :] for j in range(4)]).then_inc(sem("at_pT_raw"), 1)
            pe.wait_ge(sem("at_pT"), 6)
            for tt in range(TT):
                for h in range(AH):
                    o = PS[:, 6 + tt, h * AD:(h + 1) * AD]
                    v = slice(1024 + h * AD, 1024 + (h + 1) * AD)
                    for st in range(tt + 1):
                        last = mm(o, APT[:, 3 * h + tt + st, :], PR[:, st, v], start=(st == 0), stop=(st == tt))
            last.then_inc(sem("at_o"), 1)
            pe.wait_ge(sem("ya_ready"), 1)
            for tt in range(TT):
                quad(4 + tt, [YA[:, tt, j * P:(j + 1) * P] for j in range(4)]).then_inc(sem("ya_T_raw"), 1)
            pe.wait_ge(sem("ya_T"), 2)
            pe.wait_ge(sem("proj_taken"), E0 + IN2)
            out_block(B_PA, YAT, 0, True, True)
            pe.wait_ge(sem("block_used"), B_PA + 1)
            pe.sem_inc(sem("pa_ready"), 1)
            pe.wait_ge(sem("yb_ready"), 1)
            out_block(B_PB, YBT, 0, True, True, bank=4)
            pe.wait_ge(sem("block_used"), B_PB + 1)
            pe.sem_inc(sem("pb_ready"), 1)
            pe.wait_ge(sem("merged"), 1)
            for q in range(4):
                tt, half = q // 2, q % 2
                quad(4 + q, [PR[:, tt, 3072 + (4 * half + j) * P:3072 + (4 * half + j + 1) * P] for j in range(4)])\
                    .then_inc(sem("mg_T_raw"), 1)
            pe.wait_ge(sem("mg_T"), 4)
            for i in range(WO):
                out_block(B_WO + i, MT, 4 * i, i == 0, i == WO - 1)
            pe.wait_ge(sem("block_used"), B_WO + WO)
            pe.sem_inc(sem("y_ready"), 1)
            transpose_stream(5)
            pe.wait_ge(sem("hT_ready"), 24)
            pe.wait_ge(sem("router_in"), 64)
            for tt in range(TT):
                for k in range(KT):
                    last = mm(PS[:, 4, tt * 64:tt * 64 + NG + NE], HT[:, k, tt * P:(tt + 1) * P], WR[:, k, :],
                              start=(k == 0), stop=(k == KT - 1))
            last.then_inc(sem("router_raw"), 1)
            pe.wait_ge(sem("combine"), 1)
            for e in range(NE):
                if e % 2 == 0 and e >= 8:
                    pe.wait_ge(sem("cb_taken"), e // 2 - 3)
                for tt in range(TT):
                    last = mm(PS[:, 4 + e // 2 % 4, (e % 2) * T + tt * P:(e % 2) * T + (tt + 1) * P],
                              CWC[:, tt, e:e + 1].to_broadcast([P, P]), IDN, start=True, stop=True)
                if e % 2:
                    last.then_inc(sem("cb_raw"), 1)
            pe.wait_ge(sem("cb_taken"), NE // 2)

            def expert(i, x, start, stop):
                b = B_MOE + 3 * x
                for kind in range(2):
                    s = slot_of(b + kind)
                    pe.wait_ge(sem(f"slot{s}_full"), i * 48 + fulls(b + kind))
                    if not start:
                        if kind == 0:
                            pe.wait_ge(sem("ex_silu"), i * 8 + 2 * x)
                        else:
                            pe.wait_ge(sem("ex_hid"), i * 8 + 2 * x)
                    for j in range(4):
                        for k in range(KT):
                            last = mm(PS[:, 4 + 2 * kind + j // 2, (j % 2) * T:(j % 2 + 1) * T],
                                      wn(s)[:, k, j * P:(j + 1) * P], HT[:, k, :],
                                      start=(k == 0), stop=(k == KT - 1))
                        if j % 2:
                            last.then_inc(sem(f"ex_w{(1, 3)[kind]}"), 1)
                    pe.wait_ge(sem(f"ex_w{(1, 3)[kind]}"), i * 8 + 2 * x + 2)
                    pe.sem_inc(sem("block_used"), 1)
                s = slot_of(b + 2)
                pe.wait_ge(sem(f"slot{s}_full"), i * 48 + fulls(b + 2))
                pe.wait_ge(sem("ex_hid"), i * 8 + 2 * x + 2)
                for kk in range(4):
                    for tt in range(TT):
                        for n in range(2):
                            last = mm(PS[:, 2 * tt + n, :], H1[x % 2][:, kk, tt * P:(tt + 1) * P],
                                      wk(s)[:, kk, n * NB:(n + 1) * NB],
                                      start=(start and kk == 0), stop=(stop and kk == 3))
                last.then_inc(sem("block_used"), 1)

            for x in range(4):
                expert(0, x, x == 0, False)
            with pe.Fori(1, NE // 4 - 1) as i:
                for x in range(4):
                    expert(i, x, False, False)
            for x in range(4):
                expert(NE // 4 - 1, x, False, x == 3)
            pe.wait_ge(sem("block_used"), B_MOE + 3 * NE)
            pe.sem_inc(sem("y_ready"), 1)

        @block.scalar
        def _(act):
            a = nc.scalar.activation
            chain = [0]

            def link(ins):
                chain[0] += 1
                ins.then_inc(sem("act_step"), 1)
                act.wait_ge(sem("act_step"), chain[0])

            n_proj = [0]

            def evac(cols, func, scale=1.0, dst=None):
                n = n_proj[0]
                act.wait_ge(sem("proj_ready"), n + 1)
                src = PS[:, 2 * (n % 2):2 * (n % 2) + 2, :]
                a(PR[:, :, cols:cols + NB], src, func, scale=scale).then_inc(sem("proj_taken"), 1)
                n_proj[0] += 1
                act.wait_ge(sem("proj_taken"), n + 1)

            def ld(name, dst, src):
                nc.scalar.dma_start(dst, src).then_inc(sem(name), 16)

            ld("x_in", X[:, :, :], A["x"][0].rearrange("(t p) n -> p t n", p=P))
            ld("const_in", CK[:, :], A["keep"])
            for at, src in (
                (R_G, A["norm_g"][0, 0:3:2, :].rearrange("i (k p) -> i k p", p=P)),
                (R_G + 16, A["norm_g"][1, 0:3:2, :].rearrange("i (k p) -> i k p", p=P)),
            ):
                for i in range(2):
                    ld("rows_in", AR[at + 8 * i:at + 8 * i + 8, 0:P], src[i])
            ld("rows_in", AR[R_CW:R_CW + 32, 0:P], A["od_conv_w"][0].rearrange("j (k p) -> (j k) p", p=P))
            ld("rows_in", AR[R_CB:R_CB + 8, 0:P], A["od_conv_b"].rearrange("a (k p) -> (a k) p", p=P))
            ld("rows_in", AR[R_G1:R_G1 + 8, 0:P], A["g_norm1_2"].rearrange("a (k p) -> (a k) p", p=P))
            ld("rows_in", AR[R_G2:R_G2 + 8, 0:P], A["g_norm2_2"].rearrange("a (k p) -> (a k) p", p=P))
            ld("rows_in", AR[R_CW2:R_CW2 + 12, 0:P], A["conv_w_2"][0].rearrange("j (k p) -> (j k) p", p=P))
            ld("rows_in", AR[R_CB2:R_CB2 + 4, 0:P], A["conv_b_2"].rearrange("a (k p) -> (a k) p", p=P))
            ld("rows_in", AR[R_C:R_C + 8, 0:P], A["c_2"].rearrange("a (k p) -> (a k) p", p=P))
            ld("rows_in", AR[0:48, P:2 * P], A["b_ada_2"].rearrange("a (k p) -> (a k) p", p=P))
            ld("lb_in", LB, A["hg_lower_bound"].partition_broadcast(P))
            ld("mix_in", MX, A["mix"])
            ld("head_in", HN[:, 0:128], A["ev_hg_norm_g"][0].partition_broadcast(P))
            ld("head_in", HN[:, 128:384], A["ev_ret_norm_g"][0].partition_broadcast(P))
            ld("head_in", HN[:, 384:640], A["od_ml_norm_g"][0].partition_broadcast(P))
            ld("head_in", HN[:, 640:704], A["g_q_2"][0].partition_broadcast(P))
            ld("head_in", HN[:, 704:768], A["g_k_2"][0].partition_broadcast(P))
            ld("ga_in", GA[:, 0, :], A["b_ada_2"][0, 2 * D:3 * D].partition_broadcast(P))
            ld("ga_in", GA[:, 1, :], A["b_ada_2"][0, 5 * D:6 * D].partition_broadcast(P))
            ld("router_in", RB[:, 0:NG], A["b_rg_2"][0].partition_broadcast(P))
            ld("router_in", RB[:, NG:NG + NE], A["b_re_2"][0].partition_broadcast(P))
            ld("router_in", WR[:, :, 0:NG], A["w_rg_2"][0].rearrange("(k p) n -> p k n", p=P))
            ld("router_in", WR[:, :, NG:NG + NE], A["w_re_2"][0].rearrange("(k p) n -> p k n", p=P))
            ld("gate_in", WG[:, :, :], A["od_w_in"][0, :, 6 * NB:6 * NB + 8].rearrange("(k p) n -> p k n", p=P))
            for g in range(2):
                ld("gate_in", G4[:, g:g + 1], A["od_gate_b"][0, g].rearrange("(h a) -> h a", a=1))
            act.wait_ge(sem("cols_ready"), 1)
            link(a(GC[:, :], PS[:, 0, 0:R_END], ACT.Copy))
            a(BC[:, :], PS[:, 1, 0:48], ACT.Copy).then_inc(sem("cols_taken"), 1)
            a(CS, GC[:, R_C:R_C + 8], ACT.Silu).then_inc(sem("c_silu"), 1)
            act.wait_ge(sem("lb_shifted"), 1)
            a(LB, LB, ACT.Exp).then_inc(sem("lb_exp"), 1)
            evac(0, ACT.Silu)
            evac(NB, ACT.Sigmoid)
            act.wait_ge(sem("hg_qT_raw"), 1)
            for tt in range(TT):
                a(QT[:, :, tt * P:(tt + 1) * P], PS[:, 4 + tt, :].rearrange("p (h t) -> p h t", h=4), ACT.Copy)\
                    .then_inc(sem("hg_qT"), 1)
            evac(2 * NB, ACT.Copy)
            act.wait_ge(sem("hg_f"), 1)
            a(LF, PR[:, :, NB:2 * NB], ACT.Ln).then_inc(sem("hg_lf"), 1)
            act.wait_ge(sem("hg_b_raw"), 1)
            for tt in range(TT):
                a(BT[:, :, tt * P:(tt + 1) * P], PS[:, 4 + tt, :].rearrange("p (h t) -> p h t", h=4), ACT.Copy)\
                    .then_inc(sem("hg_bT"), 1)
            kinds = {3: (ACT.Silu, 1.0), 4: (ACT.Copy, 1.0), 5: (ACT.Copy, QK ** -0.5), 6: (ACT.Copy, 1.0),
                     7: (ACT.Copy, 1.0), 8: (ACT.Silu, 1.0), 9: (ACT.Silu, 1.0)}
            for n in range(1, 9):
                act.wait_ge(sem("hg_diff"), n)
                a(EX[(n - 1) % 2], EX[(n - 1) % 2], ACT.Exp).then_inc(sem("hg_exp"), 1)
                if n + 2 < EV_IN:
                    evac((n + 2) * NB, *kinds[n + 2])
            act.wait_ge(sem("hg_prod"), 9)
            a(S01, PS[:, 4, :].rearrange("p (h t) -> p h t", h=4), ACT.Copy).then_inc(sem("hg_s01"), 1)

            def squares(src, dst, wait, v, name):
                act.wait_ge(sem(wait), v)
                a(dst, src, ACT.Square).then_inc(sem(name), 1)

            squares(PS[:, 6:8, :], HB[:, 0:1024].rearrange("p (a b) -> p a b", a=2), "hg_out", 1, "hg_sq")
            act.wait_ge(sem("hg_y"), 1)
            for q in range(4):
                tt, half = q // 2, q % 2
                act.wait_ge(sem("ret_T_raw"), q + 1)
                a(RT[:, 4 * half:4 * half + 4, tt * P:(tt + 1) * P],
                  PS[:, 4 + q, :].rearrange("p (h t) -> p h t", h=4), ACT.Copy).then_inc(sem("ret_T"), 1)
            act.wait_ge(sem("ret_T"), 4)

            squares(PS[:, 0:4, :], HB.rearrange("p (a b) -> p a b", a=4), "ret_out", 1, "ret_sq")

            n_mix = [0]

            def mix_evac(dst, count):
                for q in range(count):
                    act.wait_ge(sem("mix_T_raw"), n_mix[0] + 1)
                    a(dst[:, 4 * (q // 2):4 * (q // 2) + 4, (q % 2) * P:(q % 2 + 1) * P],
                      PS[:, 4 + q % 4, :].rearrange("p (h t) -> p h t", h=4), ACT.Copy).then_inc(sem("mix_T"), 1)
                    n_mix[0] += 1

            mix_evac(YT, 6)

            def relus(H0, i, c, first):
                for j in range(2):
                    act.wait_ge(sem("hid_raw"), i * 4 + (H0 + c + j + 1))
                    if not first:
                        act.wait_ge(sem("hid_ready"), i * 4 + (H0 + c + j - 3))
                    a(HR[c + j], PS[:, 4 + c + j, :].rearrange("p (f t) -> p f t", f=2), ACT.Relu)\
                        .then_inc(sem("hid_relu"), 1)

            def mlp(l):
                H0 = 2 * (FF // NB) * l
                for c in (0, 2):
                    relus(H0, 0, c, True)
                with act.Fori(1, FF // NB // 2) as i:
                    for c in (0, 2):
                        relus(H0, i, c, False)

            n_y = [0]

            def y_square():
                n = n_y[0]
                act.wait_ge(sem("y_ready"), n + 1)
                for tt in range(TT):
                    a(XN[:, tt, :].rearrange("p (a b) -> p a b", a=2), PS[:, 2 * tt:2 * tt + 2, :], ACT.Square,
                      accum_out=ST[:, 2 + tt:3 + tt]).then_inc(sem("y_sq"), 1)
                n_y[0] += 1

            y_square()
            mlp(0)
            y_square()
            evac(0, ACT.Copy)
            evac(NB, ACT.Copy)
            act.wait_ge(sem("gates_raw"), 1)
            act.wait_ge(sem("gate_b"), 1)
            a(GR[:, 0, :], PS[0:4, 7, 0:T], ACT.Tanh, bias=G4[:, 2:3], scale=1.0 / GCAP).then_inc(sem("g_tanh"), 1)
            a(GR[:, 1, :], PS[0:4, 7, T:2 * T], ACT.Tanh, bias=G4[:, 3:4], scale=1.0 / GCAP)\
                .then_inc(sem("g_tanh"), 1)
            act.wait_ge(sem("g_tanh"), 2)
            act.sem_inc(sem("gates_taken"), 1)
            link(a(GR[:, 1, :], GR[:, 1, :], ACT.Exp, scale=-GCAP))
            a(GR[:, 2, :], GR[:, 1, :], ACT.Ln, bias=1.0).then_inc(sem("g_softplus"), 1)
            evac(2 * NB, ACT.Copy)
            evac(3 * NB, ACT.Copy)
            for q in range(4):
                tt, half = q // 2, q % 2
                act.wait_ge(sem("conv_T_raw"), q + 1)
                a(CRv[:, 4 * half:4 * half + 4, 3 + tt * P:3 + (tt + 1) * P],
                  PS[:, 4 + q, :].rearrange("p (h t) -> p h t", h=4), ACT.Copy).then_inc(sem("conv_T"), 1)
            act.wait_ge(sem("g_m"), 1)
            a(GR[:, 6, :], GR[:, 5, :], ACT.Exp, scale=-1.0).then_inc(sem("gates_done"), 1)
            evac(4 * NB, ACT.Sigmoid)
            evac(5 * NB, ACT.Sigmoid)
            act.wait_ge(sem("conv_sum"), 1)
            a(CT, CT, ACT.Silu).then_inc(sem("conv_done"), 1)
            act.wait_ge(sem("wexp_in"), 1)
            a(HBW, HBW, ACT.Exp, scale=-1.0).then_inc(sem("wexp"), 1)
            act.wait_ge(sem("ml_o"), 1)
            a(XN[:, :, :], HB.rearrange("p (a b) -> p a b", a=2), ACT.Square).then_inc(sem("ml_sq"), 1)
            mix_evac(YT, 4)
            y_square()
            mlp(1)
            y_square()

            for b in range(3):
                evac(b * NB, ACT.Copy)
            a(HB.rearrange("p (a b) -> p a b", a=2), PR[:, :, 0:1024], ACT.Square).then_inc(sem("qk_sq"), 1)
            for b in range(3, 6):
                evac(b * NB, ACT.Copy)
            for q in range(4):
                tt, half = q // 2, q % 2
                act.wait_ge(sem("qk_T_raw"), q + 1)
                a(T2[:, 4 * half:4 * half + 4, tt * P:(tt + 1) * P],
                  PS[:, 4 + q, :].rearrange("p (h t) -> p h t", h=4), ACT.Copy).then_inc(sem("qk_T"), 1)
            evac(6 * NB, ACT.Sigmoid)
            for q in range(2):
                for tt in range(TT):
                    act.wait_ge(sem("u_T_raw"), 2 * q + tt + 1)
                    dst = UTv[:, :, 2 + tt * P:2 + (tt + 1) * P] if q == 0 else BGT[:, :, tt * P:(tt + 1) * P]
                    a(dst, PS[:, 4 + 2 * q + tt, :].rearrange("p (h t) -> p h t", h=4), ACT.Copy)\
                        .then_inc(sem("u_T"), 1)
            for b in range(7, 10):
                evac(b * NB, ACT.Sigmoid)
            act.wait_ge(sem("at_max"), 1)
            for h in range(AH):
                a(AS[:, h, 0:P], AS[:, h, 0:P], ACT.Exp, bias=ST[:, 32 + h:33 + h], scale=AD ** -0.5,
                  accum_out=ST[:, 48 + h:49 + h]).then_inc(sem("at_exp"), 1)
                a(AS[:, h, P:3 * P], AS[:, h, P:3 * P], ACT.Exp, bias=ST[:, 40 + h:41 + h], scale=AD ** -0.5,
                  accum_out=ST[:, 56 + h:57 + h]).then_inc(sem("at_exp"), 1)
            act.wait_ge(sem("at_exp"), 2 * AH)
            act.sem_inc(sem("at_p"), 1)
            for q in range(6):
                act.wait_ge(sem("at_pT_raw"), q + 1)
                a(APT[:, 4 * q:4 * q + 4, :], PS[:, 4 + q % 4, :].rearrange("p (h t) -> p h t", h=4), ACT.Copy)\
                    .then_inc(sem("at_pT"), 1)
            for tt in range(TT):
                act.wait_ge(sem("ya_T_raw"), tt + 1)
                a(YAT[:, :, tt * P:(tt + 1) * P], PS[:, 4 + tt, :].rearrange("p (h t) -> p h t", h=4), ACT.Copy)\
                    .then_inc(sem("ya_T"), 1)
            for q in range(4):
                tt, half = q // 2, q % 2
                act.wait_ge(sem("mg_T_raw"), q + 1)
                a(MT[:, 4 * half:4 * half + 4, tt * P:(tt + 1) * P],
                  PS[:, 4 + q, :].rearrange("p (h t) -> p h t", h=4), ACT.Copy).then_inc(sem("mg_T"), 1)
            act.wait_ge(sem("r_shift"), 1)
            a(ST[:, 80:88], ST[:, 72:80], ACT.Exp).then_inc(sem("r_exp"), 1)
            act.wait_ge(sem("r_diff"), 1)
            a(ST[:, 98:100], ST[:, 96:98], ACT.Exp).then_inc(sem("r_exp"), 1)
            for q in range(NE // 2):
                act.wait_ge(sem("cb_raw"), q + 1)
                a(CBE[:, 2 * q:2 * q + 2, :], PS[:, 4 + q % 4, :].rearrange("p (e t) -> p e t", e=2), ACT.Copy)\
                    .then_inc(sem("cb_taken"), 1)

            def silus(i, x, first):
                for j in range(2):
                    act.wait_ge(sem("ex_w1"), i * 8 + (2 * x + j + 1))
                    if not first:
                        act.wait_ge(sem("ex_hid"), i * 8 + (2 * x + j - 1))
                    a(SG[j], PS[:, 4 + j, :].rearrange("p (f t) -> p f t", f=2), ACT.Silu)\
                        .then_inc(sem("ex_silu"), 1)

            for x in range(4):
                silus(0, x, x == 0)
            with act.Fori(1, NE // 4) as i:
                for x in range(4):
                    silus(i, x, False)

        @block.vector
        def _(dve):
            v = nc.vector
            chain = [0]

            def link(ins):
                chain[0] += 1
                ins.then_inc(sem("dve_step"), 1)
                dve.wait_ge(sem("dve_step"), chain[0])

            def tell(ins, name, value):
                ins.then_inc(sem(name), 1)
                dve.wait_ge(sem(name), value)

            rstd_n = [0]

            def rstd(dst, src, n):
                rstd_n[0] += 1
                v.tensor_scalar(dst, src, 1.0 / n, EPS, ALU.mult, ALU.add).then_inc(sem("mean_ready"), 1)
                dve.wait_ge(sem("rstd_ready"), rstd_n[0])

            norm_n = [0]

            def norm(gain, shift=None):
                n = norm_n[0]
                for tt in range(TT):
                    link(v.tensor_tensor_reduce(XN[:, tt, :], X[:, tt, :], X[:, tt, :], 1.0, 0.0,
                                                ALU.mult, ALU.add, ST[:, tt:tt + 1]))
                rstd(ST[:, 0:2], ST[:, 0:2], D)
                for tt in range(TT):
                    tell(v.tensor_scalar(XN[:, tt, :], X[:, tt, :], ST[:, tt:tt + 1], None, ALU.mult),
                         "xn_ready", 2 * n + tt + 1)
                if n == 0:
                    dve.wait_ge(sem("cols_taken"), 1)
                for q in range(4):
                    tt, half = q // 2, q % 2
                    dve.wait_ge(sem("xT_ready"), 4 * n + q + 1)
                    dst = HT[:, 4 * half:4 * half + 4, tt * P:(tt + 1) * P]
                    src = PS[:, 4 + q, :].rearrange("p (k t) -> p k t", k=4)
                    if shift is None:
                        tell(v.tensor_tensor(dst, src, colb(gain[:, 4 * half:4 * half + 4], P), ALU.mult),
                             "hT_ready", 4 * n + q + 1)
                    else:
                        link(v.tensor_tensor(dst, src, colb(gain[:, 4 * half:4 * half + 4], P), ALU.mult))
                        tell(v.tensor_tensor(dst, dst, colb(shift[:, 4 * half:4 * half + 4], P), ALU.add),
                             "hT_ready", 4 * n + q + 1)
                norm_n[0] += 1

            def residual(r):
                dve.wait_ge(sem("y_sq"), 2 * r + 2)
                dve.wait_ge(sem("gain_in"), 16 * (r + 1))
                rstd(ST[:, 2:4], ST[:, 2:4], D)
                for tt in range(TT):
                    y = PS[:, 2 * tt:2 * tt + 2, :]
                    xn = XN[:, tt, :].rearrange("p (a b) -> p a b", a=2)
                    link(v.scalar_tensor_tensor(xn, y, ST[:, 2 + tt:3 + tt],
                                                GB.rearrange("p (a b) -> p a b", a=2), ALU.mult, ALU.mult))
                    link(v.tensor_tensor(X[:, tt, :], X[:, tt, :], XN[:, tt, :], ALU.add))
                dve.sem_inc(sem("res_done"), 1)

            def head_norm(src, sq, groups, width, g, gate, tmp, name, value):
                link(v.tensor_reduce(ST[:, 16:16 + groups], sq, AX.X, ALU.add))
                rstd(ST[:, 16:16 + groups], ST[:, 16:16 + groups], width)
                link(v.tensor_tensor(tmp, src, colb(ST[:, 16:16 + groups], width), ALU.mult))
                link(v.tensor_tensor(tmp, tmp, midb(g, groups), ALU.mult))
                half = groups // 2
                for tt in range(TT):
                    tell(v.tensor_tensor(gate[tt], gate[tt], tmp[:, tt * half:(tt + 1) * half, :], ALU.mult),
                         name + "_half", 2 * (value - 1) + tt + 1)
                dve.sem_inc(sem(name), 1)

            dve.wait_ge(sem("x_in"), 16)
            norm(GC[:, R_G:R_G + 8])
            dve.wait_ge(sem("lb_in"), 16)
            link(v.tensor_tensor(BO, LB[:, 0, :], LB[:, 1, :], ALU.max))
            link(v.tensor_tensor(BO, BO, LB[:, 2, :], ALU.max))
            tell(v.tensor_tensor(LB, LB, midb(BO, 3), ALU.subtract), "lb_shifted", 1)
            dve.wait_ge(sem("lb_exp"), 1)
            link(v.tensor_tensor(BO, LB[:, 0, :], LB[:, 1, :], ALU.add))
            link(v.tensor_tensor(BO, BO, LB[:, 2, :], ALU.add))
            link(v.reciprocal(BO, BO))
            link(v.tensor_tensor(BO, BO, LB[:, 0, :], ALU.mult))
            link(v.tensor_scalar(LB[:, 1, :], BO, -1.0, 1.0, ALU.mult, ALU.add))
            dve.wait_ge(sem("proj_taken"), 2)
            F = PR[:, :, NB:2 * NB]
            link(v.tensor_tensor(F, F, midb(LB[:, 1, :], 2), ALU.mult))
            tell(v.tensor_tensor(F, F, midb(BO, 2), ALU.add), "hg_f", 1)
            dve.wait_ge(sem("hg_fT_raw"), 1)
            for tt in range(TT):
                tell(v.tensor_scalar(KTT[:, :, tt * P:(tt + 1) * P],
                                     PS[:, 6 + tt, :].rearrange("p (h t) -> p h t", h=4),
                                     -1.0, 1.0, ALU.mult, ALU.add), "hg_kT", tt + 1)
            dve.wait_ge(sem("hg_bT"), 2)
            dve.wait_ge(sem("hg_qT"), 2)
            dve.wait_ge(sem("mix_in"), 16)

            def diffs(n):
                ex = EX[(n - 1) % 2]
                if n >= 3:
                    dve.wait_ge(sem("hg_ks"), n - 2)
                if n <= 7:
                    m = 1 << (n - 1)
                    bv = BT.rearrange("p h (n x m) -> p (h n) x m", x=2, m=m)
                    ev = ex.rearrange("p (n x m) -> p n x m", x=2, m=m)
                    groups = 1024 // (2 * m)
                    ref = bv[:, :, 0, m - 1:m].to_broadcast([P, groups, m])
                    if n == 7:
                        link(v.tensor_copy(ev[:, :, 1, :], bv[:, :, 1, :]))
                    else:
                        link(v.tensor_tensor(ev[:, :, 1, :], bv[:, :, 1, :], ref, ALU.subtract))
                    tell(v.tensor_tensor(ev[:, :, 0, :], ref, bv[:, :, 0, :], ALU.subtract), "hg_diff", n)
                else:
                    bv = BT.rearrange("p h (c m) -> p h c m", c=4)
                    ev = ex.rearrange("p (h c m) -> p h c m", h=4, c=4)

                    def end(c):
                        return bv[:, :, c, CH - 1:CH].to_broadcast([P, 4, CH])

                    link(v.tensor_copy(ev[:, :, 2, :], bv[:, :, 2, :]))
                    link(v.tensor_tensor(ev[:, :, 3, :], bv[:, :, 3, :], end(2), ALU.add))
                    link(v.tensor_tensor(ev[:, :, 1, :], end(1), bv[:, :, 1, :], ALU.subtract))
                    link(v.tensor_tensor(ev[:, :, 0, :], end(0), bv[:, :, 0, :], ALU.subtract))
                    tell(v.tensor_tensor(ev[:, :, 0, :], ev[:, :, 0, :], end(1), ALU.add), "hg_diff", n)

            def masked(n):
                dve.wait_ge(sem("hg_prod"), n + 1)
                bank = 4 + 2 * (n % 2)
                src = PS[:, bank:bank + 2, :].rearrange("p b (h t) -> p (b h) t", h=4)
                mask = midb(MX[:, M_LEV + n * P:M_LEV + (n + 1) * P], 8)
                if n == 0:
                    tell(v.tensor_tensor(SC, src, mask, ALU.mult), "hg_masked", 1)
                else:
                    t = TMP.rearrange("p (g t) -> p g t", g=8)
                    link(v.tensor_tensor(t, src, mask, ALU.mult))
                    tell(v.tensor_tensor(SC, SC, t, ALU.add), "hg_masked", n + 1)

            diffs(1)
            diffs(2)
            masked(0)
            for n in range(1, 9):
                dve.wait_ge(sem("hg_exp"), n)
                if n >= 3:
                    dve.wait_ge(sem("hg_prod"), n - 1)
                tell(v.tensor_tensor(QS[(n - 1) % 2], QT, EX[(n - 1) % 2].rearrange("p (a b) -> p a b", a=4),
                                     ALU.mult), "hg_qs", n)
                if n + 2 <= 8:
                    diffs(n + 2)
                if n >= 2:
                    masked(n - 1)
            dve.wait_ge(sem("proj_taken"), 6)
            x = PR[:, :, 2048:3072].rearrange("p t (h x d) -> p t h x d", x=2, d=64)
            r = RR.rearrange("p t (h x d) -> p t h x d", x=2, d=64)
            dve.wait_ge(sem("hg_prod"), 9)
            for tt in range(TT):
                cos = midb(MX[:, M_CS + tt * 64:M_CS + tt * 64 + 64], 8)
                sin = midb(MX[:, M_CS + 128 + tt * 64:M_CS + 128 + tt * 64 + 64], 8)
                t1 = ar(5 * K1, 8, 64)
                t2 = ar(5 * K1 + 512, 8, 64)
                x1, x2 = x[:, tt, :, 0, :], x[:, tt, :, 1, :]
                link(v.tensor_tensor(t1, x1, cos, ALU.mult))
                link(v.tensor_tensor(t2, x2, sin, ALU.mult))
                link(v.tensor_tensor(r[:, tt, :, 0, :], t1, t2, ALU.subtract))
                link(v.tensor_tensor(t1, x2, cos, ALU.mult))
                link(v.tensor_tensor(t2, x1, sin, ALU.mult))
                link(v.tensor_tensor(r[:, tt, :, 1, :], t1, t2, ALU.add))
            dve.sem_inc(sem("rope_done"), 1)
            dve.wait_ge(sem("hg_sq"), 1)
            dve.wait_ge(sem("head_in"), 80)
            gate = [PR[:, tt, 1536:2048].rearrange("p (h d) -> p h d", h=4) for tt in range(TT)]
            dve.wait_ge(sem("proj_taken"), 4)
            head_norm(PS[:, 6:8, :].rearrange("p b (h d) -> p (b h) d", h=4),
                      HB[:, 0:1024].rearrange("p (g d) -> p g d", g=8), 8, HG_D, HN[:, 0:128], gate,
                      ar(6 * K1, 8, 128), "ev_y", 1)
            dve.sem_inc(sem("hg_y"), 1)
            for h in range(4):
                dve.wait_ge(sem("ret_s"), h + 1)
                tell(v.tensor_tensor(PT[:, h, :], PS[:, 4 + h, 0:3 * P],
                                     MX[:, M_DEC + h * 3 * P:M_DEC + (h + 1) * 3 * P], ALU.mult), "ret_p", h + 1)

            def ada_take(j):
                kind, half = j // 2, j % 2
                dve.wait_ge(sem("ada_ready"), j + 1)
                if kind in (2, 5):
                    dve.wait_ge(sem("ga_in"), 32)
                    g = GA[:, kind // 3, half * NB:(half + 1) * NB]
                    tell(v.tensor_tensor(g, g, PS[:, 2 * (j % 2), :], ALU.add), "ada_taken", j + 1)
                else:
                    c = (0, 1, None, 2, 3)[kind]
                    tell(v.tensor_tensor(MC[:, c, 4 * half:4 * half + 4], PS[:, 2 * (j % 2), 0:4],
                                         BC[:, 8 * kind + 4 * half:8 * kind + 4 * half + 4], ALU.add),
                         "ada_taken", j + 1)

            for j in range(ADA_A):
                ada_take(j)
            dve.wait_ge(sem("ret_sq"), 1)
            gate = [PR[:, tt, 4096:5120].rearrange("p (h d) -> p h d", h=4) for tt in range(TT)]
            dve.wait_ge(sem("proj_taken"), 10)
            head_norm(PS[:, 0:4, :].rearrange("p b (h d) -> p (b h) d", h=2),
                      HB.rearrange("p (g d) -> p g d", g=8), 8, RV_D, HN[:, 128:384], gate,
                      ar(6 * K1, 8, 256), "ev_y", 2)
            residual(0)
            norm(GC[:, R_G + 8:R_G + 16])

            def hidden(base, i, c, first):
                h = c // 2
                for j in range(2):
                    dve.wait_ge(sem("hid_relu"), i * 4 + (base + c + j + 1))
                    if j == 0 and not first:
                        dve.wait_ge(sem("block_used"), i * 4 + (base_b[0] + c - 2))
                    v.tensor_tensor(H1[h][:, 2 * j:2 * j + 2, :], HR[2 * h + j], HR[2 * h + j], ALU.mult)\
                        .then_inc(sem("hid_ready"), 1)

            base_b = [0]

            def mlp(l, base):
                H0 = 2 * (FF // NB) * l
                base_b[0] = base
                for c in (0, 2):
                    hidden(H0, 0, c, True)
                with dve.Fori(1, FF // NB // 2) as i:
                    for c in (0, 2):
                        hidden(H0, i, c, False)

            mlp(0, B_MLP0)
            residual(1)
            norm(GC[:, R_G + 16:R_G + 24])
            dve.wait_ge(sem("gate_in"), 48)
            tell(v.tensor_scalar(G4[:, 2:4], G4[:, 0:2], 1.0 / GCAP, None, ALU.mult), "gate_b", 1)
            tell(v.memset(CRv[:, :, 0:3], 0.0), "pad", 1)
            dve.wait_ge(sem("g_softplus"), 1)
            link(v.memset(GR[:, 7, :], 1.0))
            link(v.tensor_tensor_scan(GR[:, 1, :], GR[:, 7, :], GR[:, 2, :], 0.0, ALU.mult, ALU.subtract))
            link(v.scalar_tensor_tensor(GR[:, 3, :], GR[:, 0, :], GCAP, GR[:, 1, :], ALU.mult, ALU.subtract))
            link(v.tensor_tensor_scan(GR[:, 4, :], GR[:, 3, :], GR[:, 3, :], 0.0, ALU.max, ALU.max))
            tell(v.tensor_tensor(GR[:, 5, :], GR[:, 1, :], GR[:, 4, :], ALU.add), "g_m", 1)
            for c in range(8):
                if c % 4 == 0:
                    dve.wait_ge(sem("conv_T"), 3 + c // 4)

                def tap(j, c=c):
                    return GC[:, R_CW + 8 * j + c:R_CW + 8 * j + c + 1]
                link(v.tensor_scalar(CT[:, c, :], CRv[:, c, 0:T], tap(0), GC[:, R_CB + c:R_CB + c + 1],
                                     ALU.mult, ALU.add))
                for j in range(1, 4):
                    link(v.scalar_tensor_tensor(CT[:, c, :], CRv[:, c, j:j + T], tap(j), CT[:, c, :],
                                                ALU.mult, ALU.add))
            dve.sem_inc(sem("conv_sum"), 1)
            dve.wait_ge(sem("acol_raw"), 1)
            link(v.tensor_copy(ST[:, 112:128], PS[:, 4, 0:16]))
            dve.wait_ge(sem("mrow_raw"), 1)
            for h in range(4):
                m = PS[:, 5 + h // 2, (h % 2) * T:(h % 2 + 1) * T]
                link(v.tensor_scalar(HBW[:, h, 0:T], m, ST[:, 112 + h:113 + h], 0.0, ALU.subtract, ALU.max))
                link(v.tensor_scalar(HBW[:, h, T:3 * P], m[:, P:T], ST[:, 116 + h:117 + h], 0.0,
                                     ALU.subtract, ALU.max))
            dve.sem_inc(sem("wexp_in"), 1)
            dve.wait_ge(sem("wexp"), 1)
            for at in (0, T):
                link(v.tensor_tensor(HBW[:, :, at:at + P], HBW[:, :, at:at + P],
                                     midb(CK[:, C_CAU:C_CAU + P], 4), ALU.mult))
            for j in range(ADA_A, ADA_A + ADA_B // 2):
                ada_take(j)
            for h in range(4):
                dve.wait_ge(sem("ml_s"), h + 1)
                tell(v.scalar_tensor_tensor(PT[:, h, :], PS[:, 4 + h, 0:3 * P], QK ** -0.5, HBW[:, h, :],
                                            ALU.mult, ALU.mult), "ml_p", h + 1)
            for j in range(ADA_A + ADA_B // 2, ADA_A + ADA_B):
                ada_take(j)
            dve.wait_ge(sem("ml_out"), 1)
            link(v.scalar_tensor_tensor(ST[:, 128:136], PS[:, 4, 0:8], -1.0, ST[:, 120:128], ALU.mult, ALU.max))
            link(v.tensor_tensor(ST[:, 128:136], PS[:, 4, 0:8], ST[:, 128:136], ALU.max))
            link(v.reciprocal(ST[:, 128:136], ST[:, 128:136]))
            tell(v.tensor_tensor(HB.rearrange("p (g d) -> p g d", g=8),
                                 PS[:, 0:4, :].rearrange("p b (h d) -> p (b h) d", h=2),
                                 colb(ST[:, 128:136], RV_D), ALU.mult), "ml_o", 1)
            dve.sem_inc(sem("ml_taken"), 1)
            dve.wait_ge(sem("ml_sq"), 1)
            gate = [PR[:, tt, 2048:3072].rearrange("p (h d) -> p h d", h=4) for tt in range(TT)]
            dve.wait_ge(sem("proj_taken"), EV_IN + OD_IN)
            head_norm(HB.rearrange("p (g d) -> p g d", g=8),
                      XN[:, :, :].rearrange("p a (g d) -> p (a g) d", d=256), 8, RV_D, HN[:, 384:640], gate,
                      HB.rearrange("p (g d) -> p g d", g=8), "od_y", 1)
            residual(2)
            norm(GC[:, R_G + 24:R_G + 32])
            mlp(1, B_MLP1)
            residual(3)

            for i in range(2):
                link(v.scalar_tensor_tensor(GM[:, i, :], MC[:, 2 * i + 1, :], 1.0,
                                            GC[:, (R_G1, R_G2)[i]:(R_G1, R_G2)[i] + 8], ALU.add, ALU.mult))
            norm(GM[:, 0, :], MC[:, 0, :])
            dve.wait_ge(sem("qk_sq"), 1)
            link(v.tensor_reduce(ST[:, 128:160], HB.rearrange("p (g d) -> p g d", d=AD), AX.X, ALU.add))
            rstd(ST[:, 128:160], ST[:, 128:160], AD)
            for tt in range(TT):
                qk = PR[:, tt, 0:1024].rearrange("p (g d) -> p g d", d=AD)
                link(v.tensor_tensor(qk, qk, colb(ST[:, 128 + 16 * tt:144 + 16 * tt], AD), ALU.mult))
                for i in range(2):
                    link(v.tensor_tensor(qk[:, 8 * i:8 * i + 8, :], qk[:, 8 * i:8 * i + 8, :],
                                         midb(HN[:, 640 + 64 * i:704 + 64 * i], 8), ALU.mult))
                cos = midb(CK[:, C_CS2 + tt * 8:C_CS2 + tt * 8 + 8], 16)
                sin = midb(CK[:, C_CS2 + 16 + tt * 8:C_CS2 + 24 + tt * 8], 16)
                x1, x2 = qk[:, :, 0:8], qk[:, :, 8:16]
                t = [ar(6 * K1 + 128 * i, 16, 8) for i in range(4)]
                link(v.tensor_tensor(t[0], x1, cos, ALU.mult))
                link(v.tensor_tensor(t[1], x2, sin, ALU.mult))
                link(v.tensor_tensor(t[2], x2, cos, ALU.mult))
                link(v.tensor_tensor(t[3], x1, sin, ALU.mult))
                link(v.tensor_tensor(x1, t[0], t[1], ALU.subtract))
                link(v.tensor_tensor(x2, t[2], t[3], ALU.add))
            dve.sem_inc(sem("qk_ready"), 1)
            E0 = EV_IN + OD_IN
            dve.wait_ge(sem("proj_taken"), E0 + 6)
            link(v.memset(UTv[:, :, 0:2], 0.0))
            tell(v.tensor_tensor(PR[:, :, 1536:2048], PR[:, :, 1536:2048], PR[:, :, 2560:3072], ALU.mult),
                 "u_ready", 1)
            for h in range(AH):
                dve.wait_ge(sem("at_s_raw"), h + 1)
                tell(v.tensor_tensor(AS[:, h, :], PS[:, 4 + h % 4, 0:3 * P], CK[:, C_NEG:C_NEG + 3 * P], ALU.add),
                     "at_s", h + 1)
            link(v.tensor_reduce(ST[:, 32:40], AS[:, :, 0:P], AX.X, ALU.max))
            link(v.tensor_reduce(ST[:, 40:48], AS[:, :, P:3 * P], AX.X, ALU.max))
            tell(v.tensor_scalar(ST[:, 32:48], ST[:, 32:48], -(AD ** -0.5), None, ALU.mult), "at_max", 1)
            dve.wait_ge(sem("u_T"), 4)
            for c in range(4):
                def tap2(j, c=c):
                    return GC[:, R_CW2 + 4 * j + c:R_CW2 + 4 * j + c + 1]
                y = YBT[:, c, :]
                link(v.tensor_scalar(y, UTv[:, c, 0:T], tap2(0), GC[:, R_CB2 + c:R_CB2 + c + 1],
                                     ALU.mult, ALU.add))
                for j in range(1, 3):
                    link(v.scalar_tensor_tensor(y, UTv[:, c, j:j + T], tap2(j), y, ALU.mult, ALU.add))
                link(v.tensor_tensor(y, y, BGT[:, c, :], ALU.mult))
            dve.sem_inc(sem("yb_ready"), 1)
            dve.wait_ge(sem("at_exp"), 2 * AH)
            link(v.reciprocal(ST[:, 48:64], ST[:, 48:64]))
            dve.wait_ge(sem("at_o"), 1)
            tell(v.tensor_tensor(YA.rearrange("p t (h d) -> p (t h) d", h=AH),
                                 PS[:, 6:8, :].rearrange("p b (h d) -> p (b h) d", h=AH),
                                 colb(ST[:, 48:64], AD), ALU.mult), "ya_ready", 1)
            dve.wait_ge(sem("pa_ready"), 1)
            ga, gb = PR[:, :, 3072:4096], PR[:, :, 4096:5120]
            dve.wait_ge(sem("proj_taken"), E0 + 10)
            for tt in range(TT):
                y = PS[:, 2 * tt:2 * tt + 2, :].rearrange("p a b -> p (a b)")
                link(v.tensor_tensor(ga[:, tt, :], ga[:, tt, :], y, ALU.mult))
            dve.wait_ge(sem("pb_ready"), 1)
            for tt in range(TT):
                y = PS[:, 4 + 2 * tt:6 + 2 * tt, :].rearrange("p a b -> p (a b)")
                link(v.tensor_tensor(gb[:, tt, :], gb[:, tt, :], y, ALU.mult))
                link(v.tensor_tensor(ga[:, tt, :], ga[:, tt, :], gb[:, tt, :], ALU.add))
            dve.sem_inc(sem("merged"), 1)

            def gated_residual(i, r):
                dve.wait_ge(sem("y_ready"), r)
                for tt in range(TT):
                    y = PS[:, 2 * tt:2 * tt + 2, :].rearrange("p a b -> p (a b)")
                    link(v.tensor_tensor(XN[:, tt, :], y, GA[:, i, :], ALU.mult))
                    link(v.tensor_tensor(X[:, tt, :], X[:, tt, :], XN[:, tt, :], ALU.add))
                    if i:
                        dve.sem_inc(sem("x_final"), 1)

            gated_residual(0, 5)
            norm(GM[:, 1, :], MC[:, 2, :])
            dve.wait_ge(sem("router_raw"), 1)
            L = ar(8 * K1 + 512, TT, NG + NE)
            link(v.tensor_tensor(L, PS[:, 4, 0:128].rearrange("p (t n) -> p t n", t=2)[:, :, 0:NG + NE],
                                 midb(RB[:, :], TT), ALU.add))
            gl = L[:, :, 0:NG]
            el = L[:, :, NG:NG + NE].rearrange("p t (g e) -> p t g e", g=NG)

            def st(at, *shape):
                n = int(np.prod(shape))
                w = ar(9 * K1 + at, *shape) if len(shape) > 1 else ar(9 * K1 + at, n)
                return w

            def first_max(x, width, mx, hot):
                link(v.tensor_reduce(mx, x, AX.X, ALU.max))
                link(v.tensor_tensor(hot, x, colb(mx, width), ALU.is_equal))
                link(v.tensor_tensor(hot, hot, midb(CK[:, C_FIRST:C_FIRST + width], TT), ALU.mult))
                link(v.tensor_reduce(ST[:, 140:142], hot, AX.X, ALU.max))
                link(v.tensor_tensor(hot, hot, colb(ST[:, 140:142], width), ALU.is_equal))

            hg = st(0, TT, NG)
            first_max(gl, NG, ST[:, 64:66], hg)
            tell(v.tensor_tensor(ST[:, 72:80].rearrange("p (t g) -> p t g", t=TT), gl, colb(ST[:, 64:66], NG),
                                 ALU.subtract), "r_shift", 1)
            sel = st(64, TT, EG, NG)
            for tt in range(TT):
                link(v.tensor_tensor(sel[:, tt, :, :], el[:, tt, :, :].rearrange("p g e -> p e g"), midb(hg[:, tt, :], EG), ALU.mult))
            le = st(192, TT, EG)
            link(v.tensor_reduce(le, sel, AX.X, ALU.add))
            h1, h2 = st(256, TT, EG), st(320, TT, EG)
            first_max(le, EG, ST[:, 66:68], h1)
            link(v.scalar_tensor_tensor(le, h1, -BIG, le, ALU.mult, ALU.add))
            first_max(le, EG, ST[:, 68:70], h2)
            tell(v.tensor_tensor(ST[:, 96:98], ST[:, 68:70], ST[:, 66:68], ALU.subtract), "r_diff", 1)
            dve.wait_ge(sem("r_exp"), 2)
            link(v.tensor_reduce(ST[:, 100:102], ST[:, 80:88].rearrange("p (t g) -> p t g", t=TT), AX.X, ALU.add))
            link(v.tensor_scalar(ST[:, 102:104], ST[:, 98:100], 1.0, None, ALU.add))
            link(v.tensor_tensor(ST[:, 102:104], ST[:, 102:104], ST[:, 100:102], ALU.mult))
            link(v.reciprocal(ST[:, 102:104], ST[:, 102:104]))
            link(v.tensor_tensor(ST[:, 98:100], ST[:, 98:100], ST[:, 102:104], ALU.mult))
            link(v.tensor_tensor(h1, h1, colb(ST[:, 102:104], EG), ALU.mult))
            link(v.tensor_tensor(h2, h2, colb(ST[:, 98:100], EG), ALU.mult))
            link(v.tensor_tensor(h1, h1, h2, ALU.add))
            for tt in range(TT):
                link(v.tensor_tensor(CWC[:, tt, :].rearrange("p (g e) -> p g e", g=NG), colb(hg[:, tt, :], EG),
                                     midb(h1[:, tt, :], NG), ALU.mult))
            dve.sem_inc(sem("combine"), 1)

            def expert(i, x, first):
                for j in range(2):
                    dve.wait_ge(sem("ex_silu"), i * 8 + (2 * x + j + 1))
                    dve.wait_ge(sem("ex_w3"), i * 8 + (2 * x + j + 1))
                    if j == 0 and not first:
                        dve.wait_ge(sem("block_used"), i * 12 + (B_MOE + 3 * x - 3))
                    src = PS[:, 6 + j, :].rearrange("p (f t) -> p f t", f=2)
                    v.tensor_tensor(SG2[j], SG[j], src, ALU.mult).then_inc(sem("ex_mul"), 1)
                    dve.wait_ge(sem("ex_mul"), i * 8 + (2 * x + j + 1))
                    cb = CBE[:, bass.ds(i * 4 + x, 1), :].to_broadcast([P, 2, T])
                    v.tensor_tensor(H1[x % 2][:, 2 * j:2 * j + 2, :], SG2[j], cb, ALU.mult)\
                        .then_inc(sem("ex_hid"), 1)

            dve.wait_ge(sem("cb_taken"), NE // 2)
            for x in range(4):
                expert(0, x, x < 2)
            with dve.Fori(1, NE // 4) as i:
                for x in range(4):
                    expert(i, x, False)
            gated_residual(1, 6)


_IN = ["x", "norm_g", "hg_lower_bound", "ev_w_in", "ev_hg_norm_g", "ev_ret_norm_g", "ev_w_out", "od_w_in",
       "od_conv_w", "od_conv_b", "od_gate_b", "od_ml_norm_g", "od_w_out", "mlp_w1", "mlp_w2", "c_2", "w_ada_2",
       "b_ada_2", "g_norm1_2", "g_norm2_2", "w_in_2", "g_q_2", "g_k_2", "conv_w_2", "conv_b_2", "w_pa_2",
       "w_pb_2", "w_o_2", "w_rg_2", "b_rg_2", "w_re_2", "b_re_2", "w1_2", "w3_2", "w2_2"]


def kernel(**inputs):
    import concourse.bacc as bacc
    from concourse.bass_utils import run_bass_kernel_spmd

    nc = bacc.Bacc("TRN2", target_bir_lowering=False, num_devices=1)
    keep, mix = shape_constants()
    arrays, A = {}, {}
    for name in _IN:
        arrays[f"in_{name}"] = np.ascontiguousarray(inputs[name])
    arrays["in_keep"], arrays["in_mix"] = keep, mix
    for name, a in arrays.items():
        A[name[3:]] = nc.dram_tensor(name, a.shape, F32, kind="ExternalInput").ap()
    out = nc.dram_tensor("out", (1, T, D), F32, kind="ExternalOutput").ap()
    block_program(nc, A, out)
    r = run_bass_kernel_spmd(nc, [arrays], core_ids=[0])
    return r.results[0]["out"]
```

```python
from contextlib import ExitStack

import numpy as np

import concourse.bass as bass
from concourse import mybir

F32 = mybir.dt.float32
ALU = mybir.AluOpType
ACT = mybir.ActivationFunctionType
AX = mybir.AxisListType

P = 128
T = 256
TT = T // P
D = 1024
KT = D // P
FF = 4096
EPS = 1e-6
NB = 512
CH = 64
HG_H, HG_D = 4, 128
RV_H, RV_D = 4, 256
QK = 128
AH, AD = 8, 64
NE, NG, EG, DE = 32, 4, 8, 512
GCAP = 15.0
SLOTS = 4
BW = 4096
BIG = 1.0e30

EV_IN, ADA_A, EV_OUT = 10, 6, 3
MLP_B = 2 * (FF // NB)
OD_IN, ADA_B, OD_OUT = 6, 6, 2
IN2, PA, PB, WO = 10, 1, 1, 2
B_EV_IN = 0
B_ADA_A = B_EV_IN + EV_IN
B_EV_OUT = B_ADA_A + ADA_A
B_MLP0 = B_EV_OUT + EV_OUT
B_OD_IN = B_MLP0 + MLP_B
B_ADA_B = B_OD_IN + OD_IN
B_OD_OUT = B_ADA_B + ADA_B
B_MLP1 = B_OD_OUT + OD_OUT
B_IN2 = B_MLP1 + MLP_B
B_PA = B_IN2 + IN2
B_PB = B_PA + PA
B_WO = B_PB + PB
B_MOE = B_WO + WO

C_ID = 0
C_TRI = C_ID + P
C_CAU = C_TRI + P
C_NEG = C_CAU + P
C_SEL = C_NEG + 3 * P
C_CS2 = C_SEL + 4 * P
C_FIRST = C_CS2 + 4 * 8
C_ONE = C_FIRST + 8
C_PLACE = C_ONE + P
C_KEEP = C_PLACE + 64
M_LEV = 0
M_DEC = M_LEV + 8 * P
M_CS = M_DEC + 4 * 3 * P
M_END = M_CS + 4 * 64

R_G = 0
R_CW = 32
R_CB = 64
R_G1, R_G2 = 72, 80
R_CW2 = 88
R_CB2 = 100
R_C = 104
R_END = 112


PROJ_BLOCKS = ([B_EV_IN + b for b in range(EV_IN)] + [B_OD_IN + b for b in range(OD_IN)]
               + [B_IN2 + b for b in range(IN2)])
Y_BLOCKS = [B_EV_OUT + EV_OUT - 1, B_MLP0 + MLP_B - 1, B_OD_OUT + OD_OUT - 1, B_MLP1 + MLP_B - 1]
NGRP = FF // NB
CAP = 64
PAIRS = NE // 2
SLOT_MOE = (4, 5, 3, 0, 1, 2)


def ada_block(j):
    return B_ADA_A + j if j < ADA_A else B_ADA_B + j - ADA_A


def moe_fulls(c):
    s = SLOT_MOE[c]
    return len([b for b in range(B_MOE) if b % SLOTS == s]) if s < SLOTS else 0


def shape_constants():
    i = np.arange(P)
    s, t = i[:, None], i[None, :]
    keep = np.zeros((P, C_KEEP), np.float32)
    keep[:, C_ID:C_ID + P] = s == t
    keep[:, C_TRI:C_TRI + P] = (s <= t) & (s // CH == t // CH)
    keep[:, C_CAU:C_CAU + P] = s <= t
    neg = np.where(t > s, -BIG, 0.0)
    keep[:, C_NEG:C_NEG + P] = neg
    keep[:, C_NEG + 2 * P:C_NEG + 3 * P] = neg
    for h in range(4):
        keep[h, C_SEL + h * P:C_SEL + (h + 1) * P] = 1.0
    pos = np.arange(T, dtype=np.float32)
    half = 8
    inv = (500000.0 ** (-np.arange(0, 2 * half, 2, dtype=np.float32) / np.float32(2 * half))).astype(np.float32)
    ang = (pos[:, None] * inv[None, :]).astype(np.float32)
    for tt in range(TT):
        keep[:, C_CS2 + tt * 8:C_CS2 + tt * 8 + 8] = np.cos(ang[tt * P:(tt + 1) * P])
        keep[:, C_CS2 + 16 + tt * 8:C_CS2 + 16 + tt * 8 + 8] = np.sin(ang[tt * P:(tt + 1) * P])
    keep[:, C_FIRST:C_FIRST + 8] = np.arange(8, 0, -1)
    keep[:, C_ONE:C_ONE + P] = 1.0
    keep[:, C_PLACE:C_PLACE + 64] = np.arange(1, 65)
    mix = np.zeros((P, M_END), np.float32)
    mix[:, M_LEV:M_LEV + P] = s == t
    for n in range(7):
        m = 1 << n
        mix[:, M_LEV + (n + 1) * P:M_LEV + (n + 2) * P] = (
            (s // (2 * m) == t // (2 * m)) & (s // m % 2 == 0) & (t // m % 2 == 1))
    for h in range(4):
        lg = np.log1p(-np.exp2(-5.0 - h))
        at = M_DEC + h * 3 * P
        diag = np.where(s <= t, np.exp(lg * (t - s)), 0.0)
        mix[:, at:at + P] = diag
        mix[:, at + P:at + 2 * P] = np.exp(lg * (t + P - s))
        mix[:, at + 2 * P:at + 3 * P] = diag
    inv = (10000.0 ** (-np.arange(64, dtype=np.float32) / np.float32(64))).astype(np.float32)
    ang = (pos[:, None] * inv[None, :]).astype(np.float32)
    for tt in range(TT):
        mix[:, M_CS + tt * 64:M_CS + tt * 64 + 64] = np.cos(ang[tt * P:(tt + 1) * P])
        mix[:, M_CS + 128 + tt * 64:M_CS + 128 + tt * 64 + 64] = np.sin(ang[tt * P:(tt + 1) * P])
    return keep, mix


def block_program(nc, A, out, dump=None):
    ctx = ExitStack()
    with ctx:
        sems = {}

        def sem(name):
            if name not in sems:
                sems[name] = ctx.enter_context(nc.semaphore(name))
            return sems[name]

        def sb(name, *shape):
            return ctx.enter_context(nc.sbuf_tensor(name, list(shape), F32))

        def sb_i(name, *shape):
            return ctx.enter_context(nc.sbuf_tensor(name, list(shape), mybir.dt.int32))

        X = sb("x_rows", P, TT, D)
        XN = sb("xn_rows", P, TT, D)
        HT = sb("h_cols", P, KT, T)
        PR = sb("proj_rows", P, TT, 10 * NB)
        W = sb("weights", P, SLOTS, BW)
        AR = sb("arena", P, 14592)
        GA = sb("ga_rows", P, 2, D)
        CK = sb("constants", P, C_KEEP)
        GC = sb("g_cols", P, R_END)
        BC = sb("b_ada_cols", P, 48)
        MC = sb("mod_cols", P, 4, KT)
        GM = sb("gain_cols", P, 2, KT)
        ST = sb("stats", P, 256)
        HN = sb("head_gains", P, 128 + 256 + 256 + 128)
        RB = sb("router_bias", P, NG + NE)
        WR = sb("router_weights", P, KT, NG + NE)
        WG = sb("gate_weights", P, KT, 8)
        G4 = sb("gate_bias", 4, 4)
        PS = ctx.enter_context(nc.psum_tensor("PS", [P, 8, NB], F32))

        GB = PR[:, 0, 0:D]

        def ar(at, *shape):
            n = int(np.prod(shape))
            v = AR[:, at:at + n]
            if len(shape) == 1:
                return v
            names = "abcd"[:len(shape)]
            return v.rearrange(f"p ({' '.join(names)}) -> p {' '.join(names)}",
                               **{c: k for c, k in zip(names[:-1], shape[:-1])})

        K1 = 1024
        QT, KTT, BT = ar(0, 4, T), ar(K1, 4, T), ar(2 * K1, 4, T)
        EX = [ar((3 + i) * K1, K1) for i in range(2)]
        QS = [ar((5 + i) * K1, 4, T) for i in range(2)]
        KS = [ar((7 + i) * K1, 4, T) for i in range(2)]
        SC = ar(9 * K1, 8, P)
        TMP = ar(10 * K1, K1)
        S01 = ar(11 * K1, 4, P)
        MX = ar(11 * K1 + 512, M_END)
        LB = ar(3 * K1, 3, 512)
        BO = ar(10 * K1, 512)
        LF = ar(5 * K1, 2, 512)
        RR = XN[:, :, :]
        RT = ar(0, 8, T)
        PT = ar(2 * K1, 4, 3 * P)
        HB = ar(4 * K1, 2 * K1)
        YT = ar(8 * K1, 12, T)
        CR = ar(11 * K1, 8 * (T + 3))
        CRv = CR.rearrange("p (a b) -> p a b", a=8)
        CT = ar(0, 8, T)
        HBW = ar(6 * K1, 4, 3 * P)
        GR = AR[0:4, 4 * K1:6 * K1].rearrange("p (a b) -> p a b", a=8)
        T2 = ar(0, 8, T)
        AS = ar(2 * K1, AH, 3 * P)
        APT = ar(5 * K1, 24, P)
        UT = ar(8 * K1, 4 * (T + 2))
        UTv = UT.rearrange("p (a b) -> p a b", a=4)
        BGT = ar(9 * K1 + 16, 4, T)
        YBT = ar(10 * K1 + 16, 4, T)
        YAT = ar(11 * K1 + 16, 4, T)
        YA = ar(12 * K1 + 16, 2, 512)
        MT = ar(0, 8, T)
        H1 = [ar(i * K1, 4, T) for i in range(2)]
        HR = [ar(2 * K1 + 512 * i, 2, T) for i in range(4)]
        PRF = PR[:, :, :].rearrange("p a b -> p (a b)")
        CWC = ar(8 * K1, TT, NE)
        SEL = ar(8 * K1 + 64, TT, NE)
        RK = ar(8 * K1 + 128, TT, NE)
        H2R = ar(0, TT, D)
        XG = ar(2 * K1, KT, P)
        SGU = ar(3 * K1, NB)
        HIDR = ar(3 * K1 + 512, NB)
        HIDT = ar(4 * K1, 4, P)
        SWT = ar(4 * K1 + 512, T)
        SEL1 = ar(4 * K1 + 768, TT, 2, CAP)
        SELW = ar(5 * K1, TT, 2, CAP)
        YSB = ar(5 * K1 + 512, D)
        ZERO = ar(6 * K1 + 512, NB)
        CNT = ar(7 * K1, NE)
        RNDS = sb_i("rounds", P, 1)
        CS = ST[:, 104:112]
        IDN = CK[:, C_ID:C_ID + P]
        ONE = CK[:, C_ONE:C_ONE + P]

        def colb(ap, n):
            return ap.unsqueeze(2).to_broadcast([P, ap.shape[1], n])

        def midb(ap, n):
            return ap.unsqueeze(1).to_broadcast([P, n, ap.shape[1]])

        def moe_slot(c):
            s = SLOT_MOE[c]
            return W[:, s, :] if s < SLOTS else PRF[:, (s - SLOTS) * BW:(s - SLOTS + 1) * BW]

        def rounds(eng):
            eng.wait_ge(sem("rounds"), 1)
            return eng.value_load(RNDS[0:1, 0:1], min_val=1, max_val=T // CAP)

        def slot_of(b):
            return b % SLOTS

        def fulls(b):
            return 16 * (b // SLOTS + 1)

        def n_type(w, at):
            return w[:, bass.ds(at, NB)].rearrange("(k p) n -> p k n", p=P)

        def k_type(w, at):
            return w[bass.ds(at, NB), :].rearrange("(k p) n -> p k n", p=P)

        def wn(s):
            return W[:, s, :].rearrange("p (k n) -> p k n", k=KT)

        def wk(s):
            return W[:, s, :].rearrange("p (k n) -> p k n", k=4)

        block = ctx.enter_context(nc.Block())

        @block.sync
        def _(sp):
            def load(b, src):
                s = slot_of(b)
                if b >= SLOTS:
                    sp.wait_ge(sem("block_used"), b - SLOTS + 1)
                sp.dma_start(W[:, s, :].rearrange("p (k n) -> p k n", n=src.shape[2]), src)\
                  .then_inc(sem(f"slot{s}_full"), 16)

            for b in range(EV_IN):
                load(B_EV_IN + b, n_type(A["ev_w_in"][0], b * NB))
            for b in range(ADA_A):
                load(B_ADA_A + b, n_type(A["w_ada_2"][0], b * NB))
            for b in range(EV_OUT):
                load(B_EV_OUT + b, k_type(A["ev_w_out"][0], b * NB))

            def mlp_loads(l, base):
                w1, w2 = A["mlp_w1"][l], A["mlp_w2"][l]
                load(base, n_type(w1, 0))
                load(base + 1, n_type(w1, NB))
                load(base + 2, k_type(w2, 0))
                with sp.Fori(0, (NGRP - 2) // 2) as i:
                    for c in range(4):
                        b = base + 3 + c
                        s = slot_of(b)
                        sp.wait_ge(sem("block_used"), i * 4 + (b - SLOTS + 1))
                        g = 1 + c // 2
                        src = n_type(w1, i * (2 * NB) + (g + 1) * NB) if c % 2 == 0 else k_type(w2, i * (2 * NB) + g * NB)
                        sp.dma_start(W[:, s, :].rearrange("p (k n) -> p k n", n=src.shape[2]), src)\
                          .then_inc(sem(f"slot{s}_full"), 16)
                load(base + MLP_B - 1, k_type(w2, (NGRP - 1) * NB))

            mlp_loads(0, B_MLP0)
            for b in range(OD_IN):
                load(B_OD_IN + b, n_type(A["od_w_in"][0], b * NB))
            for b in range(ADA_B):
                load(B_ADA_B + b, n_type(A["w_ada_2"][0], (ADA_A + b) * NB))
            for b in range(OD_OUT):
                load(B_OD_OUT + b, k_type(A["od_w_out"][0], b * NB))
            mlp_loads(1, B_MLP1)
            for b in range(IN2):
                load(B_IN2 + b, n_type(A["w_in_2"][0], b * NB))
            load(B_PA, k_type(A["w_pa_2"][0], 0))
            load(B_PB, k_type(A["w_pb_2"][0], 0))
            for b in range(WO):
                load(B_WO + b, k_type(A["w_o_2"][0], b * NB))

            w1f = A["w1_2"][0].rearrange("e d f -> (e d) f")
            w3f = A["w3_2"][0].rearrange("e d f -> (e d) f")
            w2f = A["w2_2"][0].rearrange("e d f -> (e d) f")
            sp.wait_ge(sem("mg_T"), 4)
            n_rounds = rounds(sp)
            with sp.Fori(0, n_rounds) as r:
                with sp.Fori(0, PAIRS) as i:
                    for c in range(6):
                        kind, x = c // 2, c % 2
                        sp.wait_ge(sem("block_used"), r * (6 * PAIRS) + i * 6 + (B_MOE + c - 5))
                        if kind < 2:
                            w = (w1f, w3f)[kind]
                            src = w[bass.ds(i * (2 * D) + x * D, D), :].rearrange("(k p) n -> p k n", p=P)
                        else:
                            src = w2f[bass.ds(i * (2 * DE) + x * DE, DE), :].rearrange("(k p) n -> p k n", p=P)
                        sp.dma_start(moe_slot(c).rearrange("p (k n) -> p k n", n=src.shape[2]), src)\
                          .then_inc(sem(f"slot{SLOT_MOE[c]}_full"), 16)

            for tt in range(TT):
                sp.wait_ge(sem("x_final"), tt + 1)
                sp.dma_start(out[0].rearrange("(t p) n -> p t n", p=P)[:, tt, :], X[:, tt, :])\
                  .then_inc(sem("out_stored"), 16)
            sp.wait_ge(sem("out_stored"), 32)
            if dump is not None:
                sp.dma_start(dump, X[:, :, :]).then_inc(sem("out_stored"), 16)
                sp.wait_ge(sem("out_stored"), 48)

        @block.gpsimd
        def _(pool):
            powers = [0]

            def power(a, b):
                powers[0] += 1
                pool.wait_ge(sem("mean_ready"), powers[0])
                nc.gpsimd.tensor_tensor(ST[:, a:b], ST[:, a:b], ST[:, 192:192 + b - a], ALU.pow)\
                    .then_inc(sem("rstd_ready"), 1)

            def gains(r, name, count):
                pool.wait_ge(sem(name), count)
                nc.gpsimd.dma_start(GB, A["norm_g"][r // 2, 1 + 2 * (r % 2)].partition_broadcast(P))\
                    .then_inc(sem("gain_in"), 16)

            nc.gpsimd.memset(ST[:, 192:224], -0.5).then_inc(sem("half_ready"), 1)
            pool.wait_ge(sem("half_ready"), 1)
            power(0, 2)
            pool.wait_ge(sem("hg_kT"), 2)
            for n in range(8):
                pool.wait_ge(sem("hg_exp"), n + 1)
                if n >= 2:
                    pool.wait_ge(sem("hg_prod"), n)
                nc.gpsimd.tensor_tensor(KS[n % 2], KTT, EX[n % 2].rearrange("p (a b) -> p a b", a=4),
                                        ALU.mult).then_inc(sem("hg_ks"), 1)
            power(16, 24)
            power(16, 24)
            gains(0, "mix_T", 6)
            power(2, 4)
            gains(1, "res_done", 1)
            power(0, 2)
            power(2, 4)
            power(0, 2)
            power(16, 24)
            gains(2, "mix_T", 10)
            power(2, 4)
            gains(3, "res_done", 3)
            power(0, 2)
            power(2, 4)
            power(0, 2)
            power(128, 160)
            power(0, 2)

        @block.tensor
        def _(pe):
            mm = nc.tensor.matmul

            def quad(bank, srcs):
                for j, s in enumerate(srcs):
                    last = nc.tensor.transpose(PS[:, bank, j * P:(j + 1) * P], s, IDN)
                return last

            def transpose_stream(n):
                for q in range(4):
                    tt, half = q // 2, q % 2
                    if half == 0:
                        pe.wait_ge(sem("xn_ready"), 2 * n + tt + 1)
                    quad(4 + q, [XN[:, tt, (4 * half + j) * P:(4 * half + j + 1) * P] for j in range(4)])\
                        .then_inc(sem("xT_ready"), 1)

            proj_n = [0]

            def proj_block(b):
                s, n = slot_of(b), proj_n[0]
                pe.wait_ge(sem(f"slot{s}_full"), fulls(b))
                if n >= 2:
                    pe.wait_ge(sem("proj_taken"), n - 1)
                for tt in range(TT):
                    for k in range(KT):
                        last = mm(PS[:, 2 * (n % 2) + tt, :], HT[:, k, tt * P:(tt + 1) * P], wn(s)[:, k, :],
                                  start=(k == 0), stop=(k == KT - 1))
                last.then_inc(sem("block_used"), 1)
                proj_n[0] += 1

            def ada(j):
                b = ada_block(j)
                s, bank = slot_of(b), 2 * (j % 2)
                pe.wait_ge(sem(f"slot{s}_full"), fulls(b))
                if j >= 2:
                    pe.wait_ge(sem("ada_taken"), j - 1)
                if j // 2 in (2, 5):
                    for k in range(KT):
                        last = mm(PS[:, bank, :], CS[:, k:k + 1].to_broadcast([P, P]), wn(s)[:, k, :],
                                  start=(k == 0), stop=(k == KT - 1))
                else:
                    for n in range(4):
                        for k in range(KT):
                            last = mm(PS[:, bank, n:n + 1], wn(s)[:, k, n * P:(n + 1) * P], CS[:, k:k + 1],
                                      start=(k == 0), stop=(k == KT - 1))
                last.then_inc(sem("block_used"), 1)

            def out_block(b, lhs, k0, first, last_k, bank=0):
                s = slot_of(b)
                pe.wait_ge(sem(f"slot{s}_full"), fulls(b))
                for kk in range(4):
                    for tt in range(TT):
                        for n in range(2):
                            last = mm(PS[:, bank + 2 * tt + n, :], lhs[:, k0 + kk, tt * P:(tt + 1) * P],
                                      wk(s)[:, kk, n * NB:(n + 1) * NB],
                                      start=(first and kk == 0), stop=(last_k and kk == 3))
                last.then_inc(sem("block_used"), 1)
                return last

            pe.wait_ge(sem("rows_in"), 16 * 12)
            pe.wait_ge(sem("const_in"), 16)
            nc.tensor.transpose(PS[:, 0, 0:R_END], AR[0:R_END, 0:P], IDN[0:R_END, 0:R_END])
            nc.tensor.transpose(PS[:, 1, 0:48], AR[0:48, P:2 * P], IDN[0:48, 0:48])\
                .then_inc(sem("cols_ready"), 1)

            transpose_stream(0)
            pe.wait_ge(sem("cols_taken"), 1)
            pe.wait_ge(sem("hT_ready"), 4)
            for b in range(2):
                proj_block(B_EV_IN + b)
            pe.wait_ge(sem("proj_taken"), 1)
            for tt in range(TT):
                last = quad(4 + tt, [PR[:, tt, h * P:(h + 1) * P] for h in range(4)])
            last.then_inc(sem("hg_qT_raw"), 1)
            proj_block(B_EV_IN + 2)
            pe.wait_ge(sem("hg_f"), 1)
            for tt in range(TT):
                last = quad(6 + tt, [PR[:, tt, NB + h * P:NB + (h + 1) * P] for h in range(4)])
            last.then_inc(sem("hg_fT_raw"), 1)
            pe.wait_ge(sem("hg_lf"), 1)
            pe.wait_ge(sem("hg_qT"), 2)
            for tt in range(TT):
                for h in range(4):
                    last = mm(PS[:, 4 + tt, h * P:(h + 1) * P], LF[:, tt, h * P:(h + 1) * P],
                              CK[:, C_TRI:C_TRI + P], start=True, stop=True)
            last.then_inc(sem("hg_b_raw"), 1)

            def level(n):
                if n == 0:
                    pe.wait_ge(sem("hg_kT"), 2)
                    q, k = QT, KTT
                    pe.wait_ge(sem("hg_bT"), 2)
                else:
                    pe.wait_ge(sem("hg_qs"), n)
                    pe.wait_ge(sem("hg_ks"), n)
                    q, k = QS[(n - 1) % 2], KS[(n - 1) % 2]
                if n >= 2:
                    pe.wait_ge(sem("hg_masked"), n - 1)
                bank = 4 + 2 * (n % 2)
                if n == 8:
                    for h in range(4):
                        last = mm(PS[:, bank, h * P:(h + 1) * P], k[:, h, 0:P], q[:, h, P:T],
                                  start=True, stop=True)
                else:
                    for tt in range(TT):
                        for h in range(4):
                            last = mm(PS[:, bank + tt, h * P:(h + 1) * P], k[:, h, tt * P:(tt + 1) * P],
                                      q[:, h, tt * P:(tt + 1) * P], start=True, stop=True)
                last.then_inc(sem("hg_prod"), 1)

            level(0)
            for n in range(1, 9):
                if n + 2 < EV_IN:
                    proj_block(B_EV_IN + n + 2)
                level(n)
            pe.wait_ge(sem("hg_masked"), 8)
            pe.wait_ge(sem("hg_s01"), 1)
            for tt in range(TT):
                for h in range(4):
                    o = PS[:, 6 + tt, h * P:(h + 1) * P]
                    last = mm(o, SC[:, 4 * tt + h, :], PR[:, tt, 2 * NB + h * P:2 * NB + (h + 1) * P],
                              start=True, stop=(tt == 0))
                    if tt:
                        last = mm(o, S01[:, h, :], PR[:, 0, 2 * NB + h * P:2 * NB + (h + 1) * P],
                                  start=False, stop=True)
            last.then_inc(sem("hg_out"), 1)
            pe.wait_ge(sem("c_silu"), 1)

            def retention():
                pe.wait_ge(sem("rope_done"), 1)
                pe.wait_ge(sem("hg_y"), 1)
                for q in range(4):
                    tt, half = q // 2, q % 2
                    last = quad(4 + q, [RR[:, tt, (4 * half + j) * P:(4 * half + j + 1) * P] for j in range(4)])
                    last.then_inc(sem("ret_T_raw"), 1)
                pe.wait_ge(sem("ret_T"), 4)
                for h in range(4):
                    mm(PS[:, 4 + h, 0:T], RT[:, 4 + h, 0:P], RT[:, h, 0:T], start=True, stop=True)
                    mm(PS[:, 4 + h, T:T + P], RT[:, 4 + h, P:T], RT[:, h, P:T], start=True, stop=True)\
                        .then_inc(sem("ret_s"), 1)

            def values(col, ready, n, dens=None):
                for tt in range(TT):
                    for h in range(4):
                        if tt == 0:
                            pe.wait_ge(sem(ready), h + 1)
                        v = slice(col + h * RV_D, col + (h + 1) * RV_D)
                        o = PS[:, 2 * tt + h // 2, (h % 2) * RV_D:(h % 2 + 1) * RV_D]
                        parts = [(PT[:, h, 0:P], 0)] if tt == 0 else [(PT[:, h, P:2 * P], 0), (PT[:, h, 2 * P:3 * P], 1)]
                        for i, (left, st) in enumerate(parts):
                            last = mm(o, left, PR[:, st, v], start=(i == 0), stop=(i == len(parts) - 1))
                        if dens is not None:
                            for i, (left, st) in enumerate(parts):
                                last = mm(dens[:, 4 * tt + h:4 * tt + h + 1], left, ONE[:, 0:1],
                                          start=(i == 0), stop=(i == len(parts) - 1))
                last.then_inc(sem(n), 1)

            def mixed_T(srcs, evac_name, ready, base, first_bank_wait=None):
                for q, (tt, col, wv) in enumerate(srcs):
                    pe.wait_ge(sem(ready), wv)
                    if q >= 4:
                        pe.wait_ge(sem(evac_name), base + q - 3)
                    quad(4 + q % 4, [PR[:, tt, col + j * P:col + (j + 1) * P] for j in range(4)])\
                        .then_inc(sem(evac_name + "_raw"), 1)

            retention()
            pe.wait_ge(sem("proj_taken"), EV_IN)
            for j in range(ADA_A):
                ada(j)
            pe.wait_ge(sem("ada_taken"), ADA_A)
            values(3072, "ret_p", "ret_out")
            mixed_T([(0, 1536, 1), (1, 1536, 1), (0, 4096, 2), (1, 4096, 2), (0, 4608, 2), (1, 4608, 2)],
                    "mix_T", "ev_y", 0)
            pe.wait_ge(sem("mix_T"), 6)
            for i in range(EV_OUT):
                last = out_block(B_EV_OUT + i, YT, 4 * i, i == 0, i == EV_OUT - 1)

            def mlp(l, base, norm):
                transpose_stream(norm)
                pe.wait_ge(sem("hT_ready"), 4 * norm + 4)

                def up(s, full, h):
                    pe.wait_ge(sem(f"slot{s}_full"), full)
                    for j in range(4):
                        for k in range(KT):
                            last = mm(PS[:, 4 + 2 * h + j // 2, (j % 2) * T:(j % 2 + 1) * T],
                                      wn(s)[:, k, j * P:(j + 1) * P], HT[:, k, :],
                                      start=(k == 0), stop=(k == KT - 1))
                        if j == 1:
                            last.then_inc(sem("hid_raw"), 1)
                    last.then_inc(sem("block_used"), 1)

                def down(s, full, h, hid, start, stop):
                    pe.wait_ge(sem(f"slot{s}_full"), full)
                    pe.wait_ge(sem("hid_ready"), hid)
                    for kk in range(4):
                        for tt in range(TT):
                            for n in range(2):
                                last = mm(PS[:, 2 * tt + n, :], H1[h][:, kk, tt * P:(tt + 1) * P],
                                          wk(s)[:, kk, n * NB:(n + 1) * NB],
                                          start=(start and kk == 0), stop=(stop and kk == 3))
                    last.then_inc(sem("block_used"), 1)

                H0 = l * 2 * NGRP
                up(slot_of(base), fulls(base), 0)
                up(slot_of(base + 1), fulls(base + 1), 1)
                down(slot_of(base + 2), fulls(base + 2), 0, H0 + 2, True, False)
                with pe.Fori(0, (NGRP - 2) // 2) as i:
                    for g in (1, 2):
                        b = base + 1 + 2 * g
                        up(slot_of(b), i * 16 + fulls(b), (g + 1) % 2)
                        down(slot_of(b + 1), i * 16 + fulls(b + 1), g % 2, i * 4 + (H0 + 2 * g + 2), False, False)
                b = base + MLP_B - 1
                down(slot_of(b), fulls(b), (NGRP - 1) % 2, H0 + 2 * NGRP, False, True)

            mlp(0, B_MLP0, 1)

            transpose_stream(2)
            pe.wait_ge(sem("hT_ready"), 12)
            for b in range(2):
                proj_block(B_OD_IN + b)
            pe.wait_ge(sem("gate_in"), 48)
            for g in range(2):
                for k in range(KT):
                    last = mm(PS[0:4, 7, g * T:(g + 1) * T], WG[:, k, 4 * g:4 * g + 4], HT[:, k, :],
                              start=(k == 0), stop=(k == KT - 1))
            last.then_inc(sem("gates_raw"), 1)
            for b in range(2, 4):
                proj_block(B_OD_IN + b)
            pe.wait_ge(sem("gates_taken"), 1)
            pe.wait_ge(sem("proj_taken"), EV_IN + 2)
            for q in range(4):
                tt, half = q // 2, q % 2
                quad(4 + q, [PR[:, tt, (4 * half + j) * P:(4 * half + j + 1) * P] for j in range(4)])\
                    .then_inc(sem("conv_T_raw"), 1)
            for b in range(4, 6):
                proj_block(B_OD_IN + b)
            pe.wait_ge(sem("conv_T"), 4)
            pe.wait_ge(sem("gates_done"), 1)
            for j, row in enumerate((3, 6)):
                for tt in range(TT):
                    last = mm(PS[:, 4, 8 * j + 4 * tt:8 * j + 4 * tt + 4], GR[:, row, tt * P:(tt + 1) * P],
                              IDN[0:4, 0:4], start=True, stop=True)
            last.then_inc(sem("acol_raw"), 1)
            for h in range(4):
                last = mm(PS[:, 5 + h // 2, (h % 2) * T:(h % 2 + 1) * T], CK[0:4, C_SEL + h * P:C_SEL + (h + 1) * P],
                          GR[:, 4, :], start=True, stop=True)
            last.then_inc(sem("mrow_raw"), 1)
            pe.wait_ge(sem("proj_taken"), EV_IN + OD_IN)
            for j in range(ADA_A, ADA_A + ADA_B // 2):
                ada(j)
            pe.wait_ge(sem("conv_done"), 1)
            pe.wait_ge(sem("wexp_in"), 1)
            for h in range(4):
                mm(PS[:, 4 + h, 0:T], CT[:, 4 + h, 0:P], CT[:, h, 0:T], start=True, stop=True)
                mm(PS[:, 4 + h, T:T + P], CT[:, 4 + h, P:T], CT[:, h, P:T], start=True, stop=True)\
                    .then_inc(sem("ml_s"), 1)
            for j in range(ADA_A + ADA_B // 2, ADA_A + ADA_B):
                ada(j)
            pe.wait_ge(sem("ada_taken"), ADA_A + ADA_B)
            pe.wait_ge(sem("ml_p"), 4)
            values(1024, "ml_p", "ml_out", dens=PS[:, 4, 0:8])
            pe.wait_ge(sem("ml_taken"), 1)
            mixed_T([(0, 2048, 1), (1, 2048, 1), (0, 2560, 1), (1, 2560, 1)], "mix_T", "od_y", 6)
            pe.wait_ge(sem("mix_T"), 10)
            for i in range(OD_OUT):
                out_block(B_OD_OUT + i, YT, 4 * i, i == 0, i == OD_OUT - 1)
            mlp(1, B_MLP1, 3)

            transpose_stream(4)
            pe.wait_ge(sem("hT_ready"), 20)
            E0 = EV_IN + OD_IN
            for b in range(6):
                proj_block(B_IN2 + b)
            pe.wait_ge(sem("qk_ready"), 1)
            for q in range(4):
                tt, half = q // 2, q % 2
                quad(4 + q, [PR[:, tt, (4 * half + j) * P:(4 * half + j + 1) * P] for j in range(4)])\
                    .then_inc(sem("qk_T_raw"), 1)
            proj_block(B_IN2 + 6)
            pe.wait_ge(sem("u_ready"), 1)
            pe.wait_ge(sem("qk_T"), 4)
            for q, col in enumerate((1536, 2048)):
                for tt in range(TT):
                    quad(4 + 2 * q + tt, [PR[:, tt, col + j * P:col + (j + 1) * P] for j in range(4)])\
                        .then_inc(sem("u_T_raw"), 1)
            proj_block(B_IN2 + 7)
            pe.wait_ge(sem("u_T"), 4)

            def logits(h):
                pr = slice(64 * (h % 2), 64 * (h % 2) + 64)
                bank = 4 + h % 4
                if h >= 4:
                    pe.wait_ge(sem("at_s"), h - 3)
                mm(PS[:, bank, 0:P], T2[pr, h // 2, 0:P], T2[pr, 4 + h // 2, 0:P], start=True, stop=True)
                mm(PS[:, bank, P:3 * P], T2[pr, h // 2, P:T], T2[pr, 4 + h // 2, 0:T], start=True, stop=True)\
                    .then_inc(sem("at_s_raw"), 1)

            for h in range(AH):
                logits(h)
            for b in range(8, 10):
                proj_block(B_IN2 + b)
            pe.wait_ge(sem("at_s"), 8)
            pe.wait_ge(sem("at_p"), 1)
            flat = AS.rearrange("p h (x s) -> p (h x) s", x=3)
            for q in range(6):
                if q >= 4:
                    pe.wait_ge(sem("at_pT"), q - 3)
                quad(4 + q % 4, [flat[:, 4 * q + j, :] for j in range(4)]).then_inc(sem("at_pT_raw"), 1)
            pe.wait_ge(sem("at_pT"), 6)
            for tt in range(TT):
                for h in range(AH):
                    o = PS[:, 6 + tt, h * AD:(h + 1) * AD]
                    v = slice(1024 + h * AD, 1024 + (h + 1) * AD)
                    for st in range(tt + 1):
                        last = mm(o, APT[:, 3 * h + tt + st, :], PR[:, st, v], start=(st == 0), stop=(st == tt))
            last.then_inc(sem("at_o"), 1)
            pe.wait_ge(sem("ya_ready"), 1)
            for tt in range(TT):
                quad(4 + tt, [YA[:, tt, j * P:(j + 1) * P] for j in range(4)]).then_inc(sem("ya_T_raw"), 1)
            pe.wait_ge(sem("ya_T"), 2)
            pe.wait_ge(sem("proj_taken"), E0 + IN2)
            out_block(B_PA, YAT, 0, True, True)
            pe.wait_ge(sem("yb_ready"), 1)
            out_block(B_PB, YBT, 0, True, True, bank=4)
            pe.wait_ge(sem("merged"), 1)
            for q in range(4):
                tt, half = q // 2, q % 2
                quad(4 + q, [PR[:, tt, 3072 + (4 * half + j) * P:3072 + (4 * half + j + 1) * P] for j in range(4)])\
                    .then_inc(sem("mg_T_raw"), 1)
            pe.wait_ge(sem("mg_T"), 4)
            for i in range(WO):
                out_block(B_WO + i, MT, 4 * i, i == 0, i == WO - 1)
            transpose_stream(5)
            pe.wait_ge(sem("hT_ready"), 24)
            pe.wait_ge(sem("router_in"), 64)
            for tt in range(TT):
                for k in range(KT):
                    last = mm(PS[:, 4, tt * 64:tt * 64 + NG + NE], HT[:, k, tt * P:(tt + 1) * P], WR[:, k, :],
                              start=(k == 0), stop=(k == KT - 1))
            last.then_inc(sem("router_raw"), 1)
            pe.wait_ge(sem("router_taken"), 1)
            for q in range(4):
                tt, half = q // 2, q % 2
                quad(4 + q, [HT[:, 4 * half + j, tt * P:(tt + 1) * P] for j in range(4)]).then_inc(sem("h2_raw"), 1)
            pe.wait_ge(sem("chosen"), 1)
            mm(PS[:, 0, 0:NE], CK[:, C_CAU:C_CAU + P], SEL[:, 0, :], start=True, stop=True)
            mm(PS[:, 0, NE:2 * NE], ONE, SEL[:, 0, :], start=True, stop=False)
            mm(PS[:, 0, NE:2 * NE], CK[:, C_CAU:C_CAU + P], SEL[:, 1, :], start=False, stop=True)
            mm(PS[:, 0, 64:64 + NE], ONE, SEL[:, 0, :], start=True, stop=False)
            mm(PS[:, 0, 64:64 + NE], ONE, SEL[:, 1, :], start=False, stop=True).then_inc(sem("places_raw"), 1)
            pe.wait_ge(sem("h2_rows"), 4)
            n_rounds = rounds(pe)
            for bank in range(4):
                mm(PS[:, bank, :], ZERO[:, 0:P], ZERO, start=True, stop=False, skip_group_check=True)

            def gather():
                for dt in range(KT):
                    for tt in range(TT):
                        last = mm(PS[:, 6 + dt // 4, (dt % 4) * P:(dt % 4 + 1) * P], H2R[:, tt, dt * P:(dt + 1) * P],
                                  SEL1[:, tt, :, :], start=(tt == 0), stop=(tt == TT - 1))
                    if dt % 4 == 3:
                        last.then_inc(sem("ex_gather"), 1)

            def scatter():
                for tt in range(TT):
                    for n in range(2):
                        mm(PS[:, 2 * tt + n, :], SWT[:, tt * P:(tt + 1) * P], YSB[:, n * NB:(n + 1) * NB],
                           start=False, stop=False, skip_group_check=True)

            def pair(n, i, first, last_pair):
                def arrived(c):
                    s = SLOT_MOE[c]
                    pe.wait_ge(sem(f"slot{s}_full"), n * 16 + 16 * (moe_fulls(c) + 1))

                pe.wait_ge(sem("ex_xg0"), n + 1)
                pe.wait_ge(sem("ex_xg1"), n + 1)
                for kind in range(2):
                    arrived(2 * kind)
                    arrived(2 * kind + 1)
                    if not first:
                        pe.wait_ge(sem(("ex_hT", "ex_swT")[kind]), n)
                    for k in range(KT):
                        for x in range(2):
                            w = moe_slot(2 * kind + x).rearrange("p (k n) -> p k n", k=KT)
                            last = mm(PS[CAP * x:CAP * (x + 1), 4 + kind, :], XG[:, k, CAP * x:CAP * (x + 1)],
                                      w[:, k, :], start=(k == 0), stop=(k == KT - 1))
                    last.then_inc(sem("block_used"), 2)
                if not first:
                    pe.wait_ge(sem("ex_y0"), n)
                    pe.wait_ge(sem("ex_y1"), n)
                    scatter()
                pe.wait_ge(sem("ex_hid"), n + 1)
                for j in range(4):
                    last = nc.tensor.transpose(PS[:, 4, j * P:(j + 1) * P], HIDR[:, j * P:(j + 1) * P], IDN)
                last.then_inc(sem("ex_T"), 1)
                pe.wait_ge(sem("ex_weights"), n + 1)
                for tt in range(TT):
                    last = nc.tensor.transpose(PS[:, 5, tt * P:(tt + 1) * P],
                                               SELW[:, tt, :, :].rearrange("p e c -> p (e c)"), IDN)
                last.then_inc(sem("ex_swT_raw"), 1)
                if not last_pair:
                    pe.wait_ge(sem("ex_places"), n + 2)
                    gather()
                pe.wait_ge(sem("ex_hT"), n + 1)
                arrived(4)
                arrived(5)
                for half in range(2):
                    if not last_pair:
                        pe.wait_ge(sem(("ex_xg0", "ex_xg1")[half]), n + 2)
                    for kk in range(4):
                        for x in range(2):
                            w = moe_slot(4 + x).rearrange("p (k n) -> p k n", k=4)
                            last = mm(PS[CAP * x:CAP * (x + 1), 6 + half, :], HIDT[:, kk, CAP * x:CAP * (x + 1)],
                                      w[:, kk, half * NB:(half + 1) * NB], start=(kk == 0), stop=(kk == 3))
                    if half == 0:
                        last.then_inc(sem("ex_y_raw"), 1)
                last.then_inc(sem("block_used"), 2)

            with pe.Fori(0, n_rounds) as r:
                pe.wait_ge(sem("ex_places"), r * PAIRS + 1)
                gather()
                pair(r * PAIRS, 0, True, False)
                with pe.Fori(1, PAIRS - 1) as i:
                    pair(r * PAIRS + i, i, False, False)
                pair(r * PAIRS + (PAIRS - 1), PAIRS - 1, False, True)
                pe.wait_ge(sem("ex_y0"), r * PAIRS + PAIRS)
                pe.wait_ge(sem("ex_y1"), r * PAIRS + PAIRS)
                pe.wait_ge(sem("ex_swT"), r * PAIRS + PAIRS)
                scatter()
            for bank in range(4):
                last = mm(PS[:, bank, :], ZERO[:, 0:P], ZERO, start=False, stop=True, skip_group_check=True)
            last.then_inc(sem("moe_rows"), 1)

        @block.scalar
        def _(act):
            a = nc.scalar.activation
            chain = [0]

            def link(ins):
                chain[0] += 1
                ins.then_inc(sem("act_step"), 1)
                act.wait_ge(sem("act_step"), chain[0])

            n_proj = [0]

            def evac(cols, func, scale=1.0):
                n = n_proj[0]
                act.wait_ge(sem("block_used"), PROJ_BLOCKS[n] + 1)
                src = PS[:, 2 * (n % 2):2 * (n % 2) + 2, :]
                a(PR[:, :, cols:cols + NB], src, func, scale=scale).then_inc(sem("proj_taken"), 1)
                n_proj[0] += 1
                act.wait_ge(sem("proj_taken"), n + 1)

            def ld(name, dst, src):
                nc.scalar.dma_start(dst, src).then_inc(sem(name), 16)

            ld("x_in", X[:, :, :], A["x"][0].rearrange("(t p) n -> p t n", p=P))
            ld("const_in", CK[:, :], A["keep"])
            for at, src in (
                (R_G, A["norm_g"][0, 0:3:2, :].rearrange("i (k p) -> i k p", p=P)),
                (R_G + 16, A["norm_g"][1, 0:3:2, :].rearrange("i (k p) -> i k p", p=P)),
            ):
                for i in range(2):
                    ld("rows_in", AR[at + 8 * i:at + 8 * i + 8, 0:P], src[i])
            ld("rows_in", AR[R_CW:R_CW + 32, 0:P], A["od_conv_w"][0].rearrange("j (k p) -> (j k) p", p=P))
            ld("rows_in", AR[R_CB:R_CB + 8, 0:P], A["od_conv_b"].rearrange("a (k p) -> (a k) p", p=P))
            ld("rows_in", AR[R_G1:R_G1 + 8, 0:P], A["g_norm1_2"].rearrange("a (k p) -> (a k) p", p=P))
            ld("rows_in", AR[R_G2:R_G2 + 8, 0:P], A["g_norm2_2"].rearrange("a (k p) -> (a k) p", p=P))
            ld("rows_in", AR[R_CW2:R_CW2 + 12, 0:P], A["conv_w_2"][0].rearrange("j (k p) -> (j k) p", p=P))
            ld("rows_in", AR[R_CB2:R_CB2 + 4, 0:P], A["conv_b_2"].rearrange("a (k p) -> (a k) p", p=P))
            ld("rows_in", AR[R_C:R_C + 8, 0:P], A["c_2"].rearrange("a (k p) -> (a k) p", p=P))
            ld("rows_in", AR[0:48, P:2 * P], A["b_ada_2"].rearrange("a (k p) -> (a k) p", p=P))
            ld("lb_in", LB, A["hg_lower_bound"].partition_broadcast(P))
            ld("mix_in", MX, A["mix"])
            ld("head_in", HN[:, 0:128], A["ev_hg_norm_g"][0].partition_broadcast(P))
            ld("head_in", HN[:, 128:384], A["ev_ret_norm_g"][0].partition_broadcast(P))
            ld("head_in", HN[:, 384:640], A["od_ml_norm_g"][0].partition_broadcast(P))
            ld("head_in", HN[:, 640:704], A["g_q_2"][0].partition_broadcast(P))
            ld("head_in", HN[:, 704:768], A["g_k_2"][0].partition_broadcast(P))
            ld("ga_in", GA[:, 0, :], A["b_ada_2"][0, 2 * D:3 * D].partition_broadcast(P))
            ld("ga_in", GA[:, 1, :], A["b_ada_2"][0, 5 * D:6 * D].partition_broadcast(P))
            ld("router_in", RB[:, 0:NG], A["b_rg_2"][0].partition_broadcast(P))
            ld("router_in", RB[:, NG:NG + NE], A["b_re_2"][0].partition_broadcast(P))
            ld("router_in", WR[:, :, 0:NG], A["w_rg_2"][0].rearrange("(k p) n -> p k n", p=P))
            ld("router_in", WR[:, :, NG:NG + NE], A["w_re_2"][0].rearrange("(k p) n -> p k n", p=P))
            ld("gate_in", WG[:, :, :], A["od_w_in"][0, :, 6 * NB:6 * NB + 8].rearrange("(k p) n -> p k n", p=P))
            for g in range(2):
                ld("gate_in", G4[:, g:g + 1], A["od_gate_b"][0, g].rearrange("(h a) -> h a", a=1))
            act.wait_ge(sem("cols_ready"), 1)
            link(a(GC[:, :], PS[:, 0, 0:R_END], ACT.Copy))
            a(BC[:, :], PS[:, 1, 0:48], ACT.Copy).then_inc(sem("cols_taken"), 1)
            a(CS, GC[:, R_C:R_C + 8], ACT.Silu).then_inc(sem("c_silu"), 1)
            act.wait_ge(sem("lb_shifted"), 1)
            a(LB, LB, ACT.Exp).then_inc(sem("lb_exp"), 1)
            evac(0, ACT.Silu)
            evac(NB, ACT.Sigmoid)
            act.wait_ge(sem("hg_qT_raw"), 1)
            for tt in range(TT):
                a(QT[:, :, tt * P:(tt + 1) * P], PS[:, 4 + tt, :].rearrange("p (h t) -> p h t", h=4), ACT.Copy)\
                    .then_inc(sem("hg_qT"), 1)
            evac(2 * NB, ACT.Copy)
            act.wait_ge(sem("hg_f"), 1)
            a(LF, PR[:, :, NB:2 * NB], ACT.Ln).then_inc(sem("hg_lf"), 1)
            act.wait_ge(sem("hg_b_raw"), 1)
            for tt in range(TT):
                a(BT[:, :, tt * P:(tt + 1) * P], PS[:, 4 + tt, :].rearrange("p (h t) -> p h t", h=4), ACT.Copy)\
                    .then_inc(sem("hg_bT"), 1)
            kinds = {3: (ACT.Silu, 1.0), 4: (ACT.Copy, 1.0), 5: (ACT.Copy, QK ** -0.5), 6: (ACT.Copy, 1.0),
                     7: (ACT.Copy, 1.0), 8: (ACT.Silu, 1.0), 9: (ACT.Silu, 1.0)}
            for n in range(1, 9):
                act.wait_ge(sem("hg_diff"), n)
                a(EX[(n - 1) % 2], EX[(n - 1) % 2], ACT.Exp).then_inc(sem("hg_exp"), 1)
                if n + 2 < EV_IN:
                    evac((n + 2) * NB, *kinds[n + 2])
            act.wait_ge(sem("hg_prod"), 9)
            a(S01, PS[:, 4, :].rearrange("p (h t) -> p h t", h=4), ACT.Copy).then_inc(sem("hg_s01"), 1)

            def squares(src, dst, wait, v, name):
                act.wait_ge(sem(wait), v)
                a(dst, src, ACT.Square).then_inc(sem(name), 1)

            squares(PS[:, 6:8, :], HB[:, 0:1024].rearrange("p (a b) -> p a b", a=2), "hg_out", 1, "hg_sq")
            act.wait_ge(sem("hg_y"), 1)
            for q in range(4):
                tt, half = q // 2, q % 2
                act.wait_ge(sem("ret_T_raw"), q + 1)
                a(RT[:, 4 * half:4 * half + 4, tt * P:(tt + 1) * P],
                  PS[:, 4 + q, :].rearrange("p (h t) -> p h t", h=4), ACT.Copy).then_inc(sem("ret_T"), 1)
            act.wait_ge(sem("ret_T"), 4)

            squares(PS[:, 0:4, :], HB.rearrange("p (a b) -> p a b", a=4), "ret_out", 1, "ret_sq")

            n_mix = [0]

            def mix_evac(dst, count):
                for q in range(count):
                    act.wait_ge(sem("mix_T_raw"), n_mix[0] + 1)
                    a(dst[:, 4 * (q // 2):4 * (q // 2) + 4, (q % 2) * P:(q % 2 + 1) * P],
                      PS[:, 4 + q % 4, :].rearrange("p (h t) -> p h t", h=4), ACT.Copy).then_inc(sem("mix_T"), 1)
                    n_mix[0] += 1

            mix_evac(YT, 6)

            def relus(l, base, i, g):
                h = g % 2
                for j in range(2):
                    if j == 0:
                        act.wait_ge(sem("hid_raw"), i * 2 + (NGRP * l + g + 1))
                    else:
                        act.wait_ge(sem("block_used"), i * 4 + (base + max(1, 2 * g)))
                    a(HR[2 * h + j], PS[:, 4 + 2 * h + j, :].rearrange("p (f t) -> p f t", f=2), ACT.Relu)\
                        .then_inc(sem("hid_relu"), 1)

            def mlp(l, base):
                for g in (0, 1):
                    relus(l, base, 0, g)
                with act.Fori(0, (NGRP - 2) // 2) as i:
                    for g in (2, 3):
                        relus(l, base, i, g)

            n_y = [0]

            def y_square():
                n = n_y[0]
                act.wait_ge(sem("block_used"), Y_BLOCKS[n] + 1)
                for tt in range(TT):
                    a(XN[:, tt, :].rearrange("p (a b) -> p a b", a=2), PS[:, 2 * tt:2 * tt + 2, :], ACT.Square,
                      accum_out=ST[:, 2 + tt:3 + tt]).then_inc(sem("y_sq"), 1)
                n_y[0] += 1

            y_square()
            mlp(0, B_MLP0)
            y_square()
            evac(0, ACT.Copy)
            evac(NB, ACT.Copy)
            act.wait_ge(sem("gates_raw"), 1)
            act.wait_ge(sem("gate_b"), 1)
            a(GR[:, 0, :], PS[0:4, 7, 0:T], ACT.Tanh, bias=G4[:, 2:3], scale=1.0 / GCAP).then_inc(sem("g_tanh"), 1)
            a(GR[:, 1, :], PS[0:4, 7, T:2 * T], ACT.Tanh, bias=G4[:, 3:4], scale=1.0 / GCAP)\
                .then_inc(sem("g_tanh"), 1)
            act.wait_ge(sem("g_tanh"), 2)
            act.sem_inc(sem("gates_taken"), 1)
            link(a(GR[:, 1, :], GR[:, 1, :], ACT.Exp, scale=-GCAP))
            a(GR[:, 2, :], GR[:, 1, :], ACT.Ln, bias=1.0).then_inc(sem("g_softplus"), 1)
            evac(2 * NB, ACT.Copy)
            evac(3 * NB, ACT.Copy)
            for q in range(4):
                tt, half = q // 2, q % 2
                act.wait_ge(sem("conv_T_raw"), q + 1)
                a(CRv[:, 4 * half:4 * half + 4, 3 + tt * P:3 + (tt + 1) * P],
                  PS[:, 4 + q, :].rearrange("p (h t) -> p h t", h=4), ACT.Copy).then_inc(sem("conv_T"), 1)
            act.wait_ge(sem("g_m"), 1)
            a(GR[:, 6, :], GR[:, 5, :], ACT.Exp, scale=-1.0).then_inc(sem("gates_done"), 1)
            evac(4 * NB, ACT.Sigmoid)
            evac(5 * NB, ACT.Sigmoid)
            act.wait_ge(sem("conv_sum"), 1)
            a(CT, CT, ACT.Silu).then_inc(sem("conv_done"), 1)
            act.wait_ge(sem("wexp_in"), 1)
            a(HBW, HBW, ACT.Exp, scale=-1.0).then_inc(sem("wexp"), 1)
            act.wait_ge(sem("ml_o"), 1)
            a(XN[:, :, :], HB.rearrange("p (a b) -> p a b", a=2), ACT.Square).then_inc(sem("ml_sq"), 1)
            mix_evac(YT, 4)
            y_square()
            mlp(1, B_MLP1)
            y_square()

            for b in range(3):
                evac(b * NB, ACT.Copy)
            a(HB.rearrange("p (a b) -> p a b", a=2), PR[:, :, 0:1024], ACT.Square).then_inc(sem("qk_sq"), 1)
            for b in range(3, 6):
                evac(b * NB, ACT.Copy)
            for q in range(4):
                tt, half = q // 2, q % 2
                act.wait_ge(sem("qk_T_raw"), q + 1)
                a(T2[:, 4 * half:4 * half + 4, tt * P:(tt + 1) * P],
                  PS[:, 4 + q, :].rearrange("p (h t) -> p h t", h=4), ACT.Copy).then_inc(sem("qk_T"), 1)
            evac(6 * NB, ACT.Sigmoid)
            for q in range(2):
                for tt in range(TT):
                    act.wait_ge(sem("u_T_raw"), 2 * q + tt + 1)
                    dst = UTv[:, :, 2 + tt * P:2 + (tt + 1) * P] if q == 0 else BGT[:, :, tt * P:(tt + 1) * P]
                    a(dst, PS[:, 4 + 2 * q + tt, :].rearrange("p (h t) -> p h t", h=4), ACT.Copy)\
                        .then_inc(sem("u_T"), 1)
            for b in range(7, 10):
                evac(b * NB, ACT.Sigmoid)
            act.wait_ge(sem("at_max"), 1)
            for h in range(AH):
                a(AS[:, h, 0:P], AS[:, h, 0:P], ACT.Exp, bias=ST[:, 32 + h:33 + h], scale=AD ** -0.5,
                  accum_out=ST[:, 48 + h:49 + h]).then_inc(sem("at_exp"), 1)
                a(AS[:, h, P:3 * P], AS[:, h, P:3 * P], ACT.Exp, bias=ST[:, 40 + h:41 + h], scale=AD ** -0.5,
                  accum_out=ST[:, 56 + h:57 + h]).then_inc(sem("at_exp"), 1)
            act.wait_ge(sem("at_exp"), 2 * AH)
            act.sem_inc(sem("at_p"), 1)
            for q in range(6):
                act.wait_ge(sem("at_pT_raw"), q + 1)
                a(APT[:, 4 * q:4 * q + 4, :], PS[:, 4 + q % 4, :].rearrange("p (h t) -> p h t", h=4), ACT.Copy)\
                    .then_inc(sem("at_pT"), 1)
            for tt in range(TT):
                act.wait_ge(sem("ya_T_raw"), tt + 1)
                a(YAT[:, :, tt * P:(tt + 1) * P], PS[:, 4 + tt, :].rearrange("p (h t) -> p h t", h=4), ACT.Copy)\
                    .then_inc(sem("ya_T"), 1)
            for q in range(4):
                tt, half = q // 2, q % 2
                act.wait_ge(sem("mg_T_raw"), q + 1)
                a(MT[:, 4 * half:4 * half + 4, tt * P:(tt + 1) * P],
                  PS[:, 4 + q, :].rearrange("p (h t) -> p h t", h=4), ACT.Copy).then_inc(sem("mg_T"), 1)
            for q in range(4):
                tt, half = q // 2, q % 2
                act.wait_ge(sem("h2_raw"), q + 1)
                a(H2R[:, tt, half * NB:(half + 1) * NB], PS[:, 4 + q, :], ACT.Copy).then_inc(sem("h2_rows"), 1)
            act.wait_ge(sem("r_shift"), 1)
            a(ST[:, 80:88], ST[:, 72:80], ACT.Exp).then_inc(sem("r_exp"), 1)
            act.wait_ge(sem("r_diff"), 1)
            a(ST[:, 98:100], ST[:, 96:98], ACT.Exp).then_inc(sem("r_exp"), 1)
            n_rounds = rounds(act)

            def take_gather(n):
                act.wait_ge(sem("ex_gather"), n * 2 + 1)
                a(XG[:, 0:4, :], PS[:, 6, :].rearrange("p (k t) -> p k t", k=4), ACT.Copy).then_inc(sem("ex_xg0"), 1)

            def pair(n, last_pair):
                act.wait_ge(sem("block_used"), n * 6 + (B_MOE + 2))
                a(SGU, PS[:, 4, :], ACT.Silu).then_inc(sem("ex_silu"), 1)
                act.wait_ge(sem("ex_T"), n + 1)
                a(HIDT, PS[:, 4, :].rearrange("p (k t) -> p k t", k=4), ACT.Copy).then_inc(sem("ex_hT"), 1)
                if not last_pair:
                    take_gather(n + 1)
                act.wait_ge(sem("ex_y_raw"), n + 1)
                a(YSB[:, 0:NB], PS[:, 6, :], ACT.Copy).then_inc(sem("ex_y0"), 1)

            with act.Fori(0, n_rounds) as r:
                take_gather(r * PAIRS)
                with act.Fori(0, PAIRS - 1) as i:
                    pair(r * PAIRS + i, False)
                pair(r * PAIRS + (PAIRS - 1), True)

        @block.vector
        def _(dve):
            v = nc.vector
            chain = [0]

            def link(ins):
                chain[0] += 1
                ins.then_inc(sem("dve_step"), 1)
                dve.wait_ge(sem("dve_step"), chain[0])

            def tell(ins, name, value):
                ins.then_inc(sem(name), 1)
                dve.wait_ge(sem(name), value)

            rstd_n = [0]

            def rstd(dst, src, n):
                rstd_n[0] += 1
                v.tensor_scalar(dst, src, 1.0 / n, EPS, ALU.mult, ALU.add).then_inc(sem("mean_ready"), 1)
                dve.wait_ge(sem("rstd_ready"), rstd_n[0])

            norm_n = [0]

            def norm(gain, shift=None):
                n = norm_n[0]
                for tt in range(TT):
                    link(v.tensor_tensor_reduce(XN[:, tt, :], X[:, tt, :], X[:, tt, :], 1.0, 0.0,
                                                ALU.mult, ALU.add, ST[:, tt:tt + 1]))
                rstd(ST[:, 0:2], ST[:, 0:2], D)
                for tt in range(TT):
                    tell(v.tensor_scalar(XN[:, tt, :], X[:, tt, :], ST[:, tt:tt + 1], None, ALU.mult),
                         "xn_ready", 2 * n + tt + 1)
                if n == 0:
                    dve.wait_ge(sem("cols_taken"), 1)
                for q in range(4):
                    tt, half = q // 2, q % 2
                    dve.wait_ge(sem("xT_ready"), 4 * n + q + 1)
                    dst = HT[:, 4 * half:4 * half + 4, tt * P:(tt + 1) * P]
                    src = PS[:, 4 + q, :].rearrange("p (k t) -> p k t", k=4)
                    if shift is None:
                        tell(v.tensor_tensor(dst, src, colb(gain[:, 4 * half:4 * half + 4], P), ALU.mult),
                             "hT_ready", 4 * n + q + 1)
                    else:
                        link(v.tensor_tensor(dst, src, colb(gain[:, 4 * half:4 * half + 4], P), ALU.mult))
                        tell(v.tensor_tensor(dst, dst, colb(shift[:, 4 * half:4 * half + 4], P), ALU.add),
                             "hT_ready", 4 * n + q + 1)
                norm_n[0] += 1

            def residual(r):
                dve.wait_ge(sem("y_sq"), 2 * r + 2)
                dve.wait_ge(sem("gain_in"), 16 * (r + 1))
                rstd(ST[:, 2:4], ST[:, 2:4], D)
                for tt in range(TT):
                    y = PS[:, 2 * tt:2 * tt + 2, :]
                    xn = XN[:, tt, :].rearrange("p (a b) -> p a b", a=2)
                    link(v.scalar_tensor_tensor(xn, y, ST[:, 2 + tt:3 + tt],
                                                GB.rearrange("p (a b) -> p a b", a=2), ALU.mult, ALU.mult))
                    link(v.tensor_tensor(X[:, tt, :], X[:, tt, :], XN[:, tt, :], ALU.add))
                dve.sem_inc(sem("res_done"), 1)

            def head_norm(src, sq, groups, width, g, gate, tmp, name, value):
                link(v.tensor_reduce(ST[:, 16:16 + groups], sq, AX.X, ALU.add))
                rstd(ST[:, 16:16 + groups], ST[:, 16:16 + groups], width)
                link(v.tensor_tensor(tmp, src, colb(ST[:, 16:16 + groups], width), ALU.mult))
                link(v.tensor_tensor(tmp, tmp, midb(g, groups), ALU.mult))
                half = groups // 2
                for tt in range(TT):
                    tell(v.tensor_tensor(gate[tt], gate[tt], tmp[:, tt * half:(tt + 1) * half, :], ALU.mult),
                         name + "_half", 2 * (value - 1) + tt + 1)
                dve.sem_inc(sem(name), 1)

            dve.wait_ge(sem("x_in"), 16)
            norm(GC[:, R_G:R_G + 8])
            dve.wait_ge(sem("lb_in"), 16)
            link(v.tensor_tensor(BO, LB[:, 0, :], LB[:, 1, :], ALU.max))
            link(v.tensor_tensor(BO, BO, LB[:, 2, :], ALU.max))
            tell(v.tensor_tensor(LB, LB, midb(BO, 3), ALU.subtract), "lb_shifted", 1)
            dve.wait_ge(sem("lb_exp"), 1)
            link(v.tensor_tensor(BO, LB[:, 0, :], LB[:, 1, :], ALU.add))
            link(v.tensor_tensor(BO, BO, LB[:, 2, :], ALU.add))
            link(v.reciprocal(BO, BO))
            link(v.tensor_tensor(BO, BO, LB[:, 0, :], ALU.mult))
            link(v.tensor_scalar(LB[:, 1, :], BO, -1.0, 1.0, ALU.mult, ALU.add))
            dve.wait_ge(sem("proj_taken"), 2)
            F = PR[:, :, NB:2 * NB]
            link(v.tensor_tensor(F, F, midb(LB[:, 1, :], 2), ALU.mult))
            tell(v.tensor_tensor(F, F, midb(BO, 2), ALU.add), "hg_f", 1)
            dve.wait_ge(sem("hg_fT_raw"), 1)
            for tt in range(TT):
                tell(v.tensor_scalar(KTT[:, :, tt * P:(tt + 1) * P],
                                     PS[:, 6 + tt, :].rearrange("p (h t) -> p h t", h=4),
                                     -1.0, 1.0, ALU.mult, ALU.add), "hg_kT", tt + 1)
            dve.wait_ge(sem("hg_bT"), 2)
            dve.wait_ge(sem("hg_qT"), 2)
            dve.wait_ge(sem("mix_in"), 16)

            def diffs(n):
                ex = EX[(n - 1) % 2]
                if n >= 3:
                    dve.wait_ge(sem("hg_ks"), n - 2)
                if n <= 7:
                    m = 1 << (n - 1)
                    bv = BT.rearrange("p h (n x m) -> p (h n) x m", x=2, m=m)
                    ev = ex.rearrange("p (n x m) -> p n x m", x=2, m=m)
                    groups = 1024 // (2 * m)
                    ref = bv[:, :, 0, m - 1:m].to_broadcast([P, groups, m])
                    if n == 7:
                        link(v.tensor_copy(ev[:, :, 1, :], bv[:, :, 1, :]))
                    else:
                        link(v.tensor_tensor(ev[:, :, 1, :], bv[:, :, 1, :], ref, ALU.subtract))
                    tell(v.tensor_tensor(ev[:, :, 0, :], ref, bv[:, :, 0, :], ALU.subtract), "hg_diff", n)
                else:
                    bv = BT.rearrange("p h (c m) -> p h c m", c=4)
                    ev = ex.rearrange("p (h c m) -> p h c m", h=4, c=4)

                    def end(c):
                        return bv[:, :, c, CH - 1:CH].to_broadcast([P, 4, CH])

                    link(v.tensor_copy(ev[:, :, 2, :], bv[:, :, 2, :]))
                    link(v.tensor_tensor(ev[:, :, 3, :], bv[:, :, 3, :], end(2), ALU.add))
                    link(v.tensor_tensor(ev[:, :, 1, :], end(1), bv[:, :, 1, :], ALU.subtract))
                    link(v.tensor_tensor(ev[:, :, 0, :], end(0), bv[:, :, 0, :], ALU.subtract))
                    tell(v.tensor_tensor(ev[:, :, 0, :], ev[:, :, 0, :], end(1), ALU.add), "hg_diff", n)

            def masked(n):
                dve.wait_ge(sem("hg_prod"), n + 1)
                bank = 4 + 2 * (n % 2)
                src = PS[:, bank:bank + 2, :].rearrange("p b (h t) -> p (b h) t", h=4)
                mask = midb(MX[:, M_LEV + n * P:M_LEV + (n + 1) * P], 8)
                if n == 0:
                    tell(v.tensor_tensor(SC, src, mask, ALU.mult), "hg_masked", 1)
                else:
                    t = TMP.rearrange("p (g t) -> p g t", g=8)
                    link(v.tensor_tensor(t, src, mask, ALU.mult))
                    tell(v.tensor_tensor(SC, SC, t, ALU.add), "hg_masked", n + 1)

            diffs(1)
            diffs(2)
            masked(0)
            for n in range(1, 9):
                dve.wait_ge(sem("hg_exp"), n)
                if n >= 3:
                    dve.wait_ge(sem("hg_prod"), n - 1)
                tell(v.tensor_tensor(QS[(n - 1) % 2], QT, EX[(n - 1) % 2].rearrange("p (a b) -> p a b", a=4),
                                     ALU.mult), "hg_qs", n)
                if n + 2 <= 8:
                    diffs(n + 2)
                if n >= 2:
                    masked(n - 1)
            dve.wait_ge(sem("proj_taken"), 6)
            x = PR[:, :, 2048:3072].rearrange("p t (h x d) -> p t h x d", x=2, d=64)
            r = RR.rearrange("p t (h x d) -> p t h x d", x=2, d=64)
            dve.wait_ge(sem("hg_prod"), 9)
            for tt in range(TT):
                cos = midb(MX[:, M_CS + tt * 64:M_CS + tt * 64 + 64], 8)
                sin = midb(MX[:, M_CS + 128 + tt * 64:M_CS + 128 + tt * 64 + 64], 8)
                t1 = ar(5 * K1, 8, 64)
                t2 = ar(5 * K1 + 512, 8, 64)
                x1, x2 = x[:, tt, :, 0, :], x[:, tt, :, 1, :]
                link(v.tensor_tensor(t1, x1, cos, ALU.mult))
                link(v.tensor_tensor(t2, x2, sin, ALU.mult))
                link(v.tensor_tensor(r[:, tt, :, 0, :], t1, t2, ALU.subtract))
                link(v.tensor_tensor(t1, x2, cos, ALU.mult))
                link(v.tensor_tensor(t2, x1, sin, ALU.mult))
                link(v.tensor_tensor(r[:, tt, :, 1, :], t1, t2, ALU.add))
            dve.sem_inc(sem("rope_done"), 1)
            dve.wait_ge(sem("hg_sq"), 1)
            dve.wait_ge(sem("head_in"), 80)
            gate = [PR[:, tt, 1536:2048].rearrange("p (h d) -> p h d", h=4) for tt in range(TT)]
            dve.wait_ge(sem("proj_taken"), 4)
            head_norm(PS[:, 6:8, :].rearrange("p b (h d) -> p (b h) d", h=4),
                      HB[:, 0:1024].rearrange("p (g d) -> p g d", g=8), 8, HG_D, HN[:, 0:128], gate,
                      ar(6 * K1, 8, 128), "ev_y", 1)
            dve.sem_inc(sem("hg_y"), 1)
            for h in range(4):
                dve.wait_ge(sem("ret_s"), h + 1)
                tell(v.tensor_tensor(PT[:, h, :], PS[:, 4 + h, 0:3 * P],
                                     MX[:, M_DEC + h * 3 * P:M_DEC + (h + 1) * 3 * P], ALU.mult), "ret_p", h + 1)

            def ada_take(j):
                kind, half = j // 2, j % 2
                dve.wait_ge(sem("block_used"), ada_block(j) + 1)
                if kind in (2, 5):
                    dve.wait_ge(sem("ga_in"), 32)
                    g = GA[:, kind // 3, half * NB:(half + 1) * NB]
                    tell(v.tensor_tensor(g, g, PS[:, 2 * (j % 2), :], ALU.add), "ada_taken", j + 1)
                else:
                    c = (0, 1, None, 2, 3)[kind]
                    tell(v.tensor_tensor(MC[:, c, 4 * half:4 * half + 4], PS[:, 2 * (j % 2), 0:4],
                                         BC[:, 8 * kind + 4 * half:8 * kind + 4 * half + 4], ALU.add),
                         "ada_taken", j + 1)

            for j in range(ADA_A):
                ada_take(j)
            dve.wait_ge(sem("ret_sq"), 1)
            gate = [PR[:, tt, 4096:5120].rearrange("p (h d) -> p h d", h=4) for tt in range(TT)]
            dve.wait_ge(sem("proj_taken"), 10)
            head_norm(PS[:, 0:4, :].rearrange("p b (h d) -> p (b h) d", h=2),
                      HB.rearrange("p (g d) -> p g d", g=8), 8, RV_D, HN[:, 128:384], gate,
                      ar(6 * K1, 8, 256), "ev_y", 2)
            residual(0)
            norm(GC[:, R_G + 8:R_G + 16])

            def hidden(l, i, g):
                h = g % 2
                for j in range(2):
                    dve.wait_ge(sem("hid_relu"), i * 4 + (2 * NGRP * l + 2 * g + j + 1))
                    v.tensor_tensor(H1[h][:, 2 * j:2 * j + 2, :], HR[2 * h + j], HR[2 * h + j], ALU.mult)\
                        .then_inc(sem("hid_ready"), 1)

            def mlp(l):
                for g in (0, 1):
                    hidden(l, 0, g)
                with dve.Fori(0, (NGRP - 2) // 2) as i:
                    for g in (2, 3):
                        hidden(l, i, g)

            mlp(0)
            residual(1)
            norm(GC[:, R_G + 16:R_G + 24])
            dve.wait_ge(sem("gate_in"), 48)
            tell(v.tensor_scalar(G4[:, 2:4], G4[:, 0:2], 1.0 / GCAP, None, ALU.mult), "gate_b", 1)
            tell(v.memset(CRv[:, :, 0:3], 0.0), "pad", 1)
            dve.wait_ge(sem("g_softplus"), 1)
            link(v.memset(GR[:, 7, :], 1.0))
            link(v.tensor_tensor_scan(GR[:, 1, :], GR[:, 7, :], GR[:, 2, :], 0.0, ALU.mult, ALU.subtract))
            link(v.scalar_tensor_tensor(GR[:, 3, :], GR[:, 0, :], GCAP, GR[:, 1, :], ALU.mult, ALU.subtract))
            link(v.tensor_tensor_scan(GR[:, 4, :], GR[:, 3, :], GR[:, 3, :], 0.0, ALU.max, ALU.max))
            tell(v.tensor_tensor(GR[:, 5, :], GR[:, 1, :], GR[:, 4, :], ALU.add), "g_m", 1)
            for c in range(8):
                if c % 4 == 0:
                    dve.wait_ge(sem("conv_T"), 3 + c // 4)

                def tap(j, c=c):
                    return GC[:, R_CW + 8 * j + c:R_CW + 8 * j + c + 1]
                link(v.tensor_scalar(CT[:, c, :], CRv[:, c, 0:T], tap(0), GC[:, R_CB + c:R_CB + c + 1],
                                     ALU.mult, ALU.add))
                for j in range(1, 4):
                    link(v.scalar_tensor_tensor(CT[:, c, :], CRv[:, c, j:j + T], tap(j), CT[:, c, :],
                                                ALU.mult, ALU.add))
            dve.sem_inc(sem("conv_sum"), 1)
            dve.wait_ge(sem("acol_raw"), 1)
            link(v.tensor_copy(ST[:, 112:128], PS[:, 4, 0:16]))
            dve.wait_ge(sem("mrow_raw"), 1)
            for h in range(4):
                m = PS[:, 5 + h // 2, (h % 2) * T:(h % 2 + 1) * T]
                link(v.tensor_scalar(HBW[:, h, 0:T], m, ST[:, 112 + h:113 + h], 0.0, ALU.subtract, ALU.max))
                link(v.tensor_scalar(HBW[:, h, T:3 * P], m[:, P:T], ST[:, 116 + h:117 + h], 0.0,
                                     ALU.subtract, ALU.max))
            dve.sem_inc(sem("wexp_in"), 1)
            dve.wait_ge(sem("wexp"), 1)
            for at in (0, T):
                link(v.tensor_tensor(HBW[:, :, at:at + P], HBW[:, :, at:at + P],
                                     midb(CK[:, C_CAU:C_CAU + P], 4), ALU.mult))
            for j in range(ADA_A, ADA_A + ADA_B // 2):
                ada_take(j)
            for h in range(4):
                dve.wait_ge(sem("ml_s"), h + 1)
                tell(v.scalar_tensor_tensor(PT[:, h, :], PS[:, 4 + h, 0:3 * P], QK ** -0.5, HBW[:, h, :],
                                            ALU.mult, ALU.mult), "ml_p", h + 1)
            for j in range(ADA_A + ADA_B // 2, ADA_A + ADA_B):
                ada_take(j)
            dve.wait_ge(sem("ml_out"), 1)
            link(v.scalar_tensor_tensor(ST[:, 128:136], PS[:, 4, 0:8], -1.0, ST[:, 120:128], ALU.mult, ALU.max))
            link(v.tensor_tensor(ST[:, 128:136], PS[:, 4, 0:8], ST[:, 128:136], ALU.max))
            link(v.reciprocal(ST[:, 128:136], ST[:, 128:136]))
            tell(v.tensor_tensor(HB.rearrange("p (g d) -> p g d", g=8),
                                 PS[:, 0:4, :].rearrange("p b (h d) -> p (b h) d", h=2),
                                 colb(ST[:, 128:136], RV_D), ALU.mult), "ml_o", 1)
            dve.sem_inc(sem("ml_taken"), 1)
            dve.wait_ge(sem("ml_sq"), 1)
            gate = [PR[:, tt, 2048:3072].rearrange("p (h d) -> p h d", h=4) for tt in range(TT)]
            dve.wait_ge(sem("proj_taken"), EV_IN + OD_IN)
            head_norm(HB.rearrange("p (g d) -> p g d", g=8),
                      XN[:, :, :].rearrange("p a (g d) -> p (a g) d", d=256), 8, RV_D, HN[:, 384:640], gate,
                      HB.rearrange("p (g d) -> p g d", g=8), "od_y", 1)
            residual(2)
            norm(GC[:, R_G + 24:R_G + 32])
            mlp(1)
            residual(3)

            for i in range(2):
                link(v.scalar_tensor_tensor(GM[:, i, :], MC[:, 2 * i + 1, :], 1.0,
                                            GC[:, (R_G1, R_G2)[i]:(R_G1, R_G2)[i] + 8], ALU.add, ALU.mult))
            norm(GM[:, 0, :], MC[:, 0, :])
            dve.wait_ge(sem("qk_sq"), 1)
            link(v.tensor_reduce(ST[:, 128:160], HB.rearrange("p (g d) -> p g d", d=AD), AX.X, ALU.add))
            rstd(ST[:, 128:160], ST[:, 128:160], AD)
            for tt in range(TT):
                qk = PR[:, tt, 0:1024].rearrange("p (g d) -> p g d", d=AD)
                link(v.tensor_tensor(qk, qk, colb(ST[:, 128 + 16 * tt:144 + 16 * tt], AD), ALU.mult))
                for i in range(2):
                    link(v.tensor_tensor(qk[:, 8 * i:8 * i + 8, :], qk[:, 8 * i:8 * i + 8, :],
                                         midb(HN[:, 640 + 64 * i:704 + 64 * i], 8), ALU.mult))
                cos = midb(CK[:, C_CS2 + tt * 8:C_CS2 + tt * 8 + 8], 16)
                sin = midb(CK[:, C_CS2 + 16 + tt * 8:C_CS2 + 24 + tt * 8], 16)
                x1, x2 = qk[:, :, 0:8], qk[:, :, 8:16]
                t = [ar(6 * K1 + 128 * i, 16, 8) for i in range(4)]
                link(v.tensor_tensor(t[0], x1, cos, ALU.mult))
                link(v.tensor_tensor(t[1], x2, sin, ALU.mult))
                link(v.tensor_tensor(t[2], x2, cos, ALU.mult))
                link(v.tensor_tensor(t[3], x1, sin, ALU.mult))
                link(v.tensor_tensor(x1, t[0], t[1], ALU.subtract))
                link(v.tensor_tensor(x2, t[2], t[3], ALU.add))
            dve.sem_inc(sem("qk_ready"), 1)
            E0 = EV_IN + OD_IN
            dve.wait_ge(sem("proj_taken"), E0 + 6)
            link(v.memset(UTv[:, :, 0:2], 0.0))
            tell(v.tensor_tensor(PR[:, :, 1536:2048], PR[:, :, 1536:2048], PR[:, :, 2560:3072], ALU.mult),
                 "u_ready", 1)
            for h in range(AH):
                dve.wait_ge(sem("at_s_raw"), h + 1)
                tell(v.tensor_tensor(AS[:, h, :], PS[:, 4 + h % 4, 0:3 * P], CK[:, C_NEG:C_NEG + 3 * P], ALU.add),
                     "at_s", h + 1)
            link(v.tensor_reduce(ST[:, 32:40], AS[:, :, 0:P], AX.X, ALU.max))
            link(v.tensor_reduce(ST[:, 40:48], AS[:, :, P:3 * P], AX.X, ALU.max))
            tell(v.tensor_scalar(ST[:, 32:48], ST[:, 32:48], -(AD ** -0.5), None, ALU.mult), "at_max", 1)
            dve.wait_ge(sem("u_T"), 4)
            for c in range(4):
                def tap2(j, c=c):
                    return GC[:, R_CW2 + 4 * j + c:R_CW2 + 4 * j + c + 1]
                y = YBT[:, c, :]
                link(v.tensor_scalar(y, UTv[:, c, 0:T], tap2(0), GC[:, R_CB2 + c:R_CB2 + c + 1],
                                     ALU.mult, ALU.add))
                for j in range(1, 3):
                    link(v.scalar_tensor_tensor(y, UTv[:, c, j:j + T], tap2(j), y, ALU.mult, ALU.add))
                link(v.tensor_tensor(y, y, BGT[:, c, :], ALU.mult))
            dve.sem_inc(sem("yb_ready"), 1)
            dve.wait_ge(sem("at_exp"), 2 * AH)
            link(v.reciprocal(ST[:, 48:64], ST[:, 48:64]))
            dve.wait_ge(sem("at_o"), 1)
            tell(v.tensor_tensor(YA.rearrange("p t (h d) -> p (t h) d", h=AH),
                                 PS[:, 6:8, :].rearrange("p b (h d) -> p (b h) d", h=AH),
                                 colb(ST[:, 48:64], AD), ALU.mult), "ya_ready", 1)
            dve.wait_ge(sem("block_used"), B_PA + 1)
            ga, gb = PR[:, :, 3072:4096], PR[:, :, 4096:5120]
            dve.wait_ge(sem("proj_taken"), E0 + 10)
            for tt in range(TT):
                y = PS[:, 2 * tt:2 * tt + 2, :].rearrange("p a b -> p (a b)")
                link(v.tensor_tensor(ga[:, tt, :], ga[:, tt, :], y, ALU.mult))
            dve.wait_ge(sem("block_used"), B_PB + 1)
            for tt in range(TT):
                y = PS[:, 4 + 2 * tt:6 + 2 * tt, :].rearrange("p a b -> p (a b)")
                link(v.tensor_tensor(gb[:, tt, :], gb[:, tt, :], y, ALU.mult))
                link(v.tensor_tensor(ga[:, tt, :], ga[:, tt, :], gb[:, tt, :], ALU.add))
            dve.sem_inc(sem("merged"), 1)

            def gated_residual(i, name, value):
                dve.wait_ge(sem(name), value)
                for tt in range(TT):
                    y = PS[:, 2 * tt:2 * tt + 2, :].rearrange("p a b -> p (a b)")
                    link(v.tensor_tensor(XN[:, tt, :], y, GA[:, i, :], ALU.mult))
                    link(v.tensor_tensor(X[:, tt, :], X[:, tt, :], XN[:, tt, :], ALU.add))
                    if i:
                        dve.sem_inc(sem("x_final"), 1)

            gated_residual(0, "block_used", B_WO + WO)
            norm(GM[:, 1, :], MC[:, 2, :])
            dve.wait_ge(sem("router_raw"), 1)
            L = ar(8 * K1 + 512, TT, NG + NE)
            link(v.tensor_tensor(L, PS[:, 4, 0:128].rearrange("p (t n) -> p t n", t=2)[:, :, 0:NG + NE],
                                 midb(RB[:, :], TT), ALU.add))
            dve.sem_inc(sem("router_taken"), 1)
            gl = L[:, :, 0:NG]
            el = L[:, :, NG:NG + NE].rearrange("p t (g e) -> p t g e", g=NG)

            def st(at, *shape):
                n = int(np.prod(shape))
                w = ar(9 * K1 + at, *shape) if len(shape) > 1 else ar(9 * K1 + at, n)
                return w

            def first_max(x, width, mx, hot):
                link(v.tensor_reduce(mx, x, AX.X, ALU.max))
                link(v.tensor_tensor(hot, x, colb(mx, width), ALU.is_equal))
                link(v.tensor_tensor(hot, hot, midb(CK[:, C_FIRST:C_FIRST + width], TT), ALU.mult))
                link(v.tensor_reduce(ST[:, 140:142], hot, AX.X, ALU.max))
                link(v.tensor_tensor(hot, hot, colb(ST[:, 140:142], width), ALU.is_equal))

            hg = st(0, TT, NG)
            first_max(gl, NG, ST[:, 64:66], hg)
            tell(v.tensor_tensor(ST[:, 72:80].rearrange("p (t g) -> p t g", t=TT), gl, colb(ST[:, 64:66], NG),
                                 ALU.subtract), "r_shift", 1)
            sel = st(64, TT, EG, NG)
            for tt in range(TT):
                link(v.tensor_tensor(sel[:, tt, :, :], el[:, tt, :, :].rearrange("p g e -> p e g"), midb(hg[:, tt, :], EG), ALU.mult))
            le = st(192, TT, EG)
            link(v.tensor_reduce(le, sel, AX.X, ALU.add))
            h1, h2 = st(256, TT, EG), st(320, TT, EG)
            first_max(le, EG, ST[:, 66:68], h1)
            link(v.scalar_tensor_tensor(le, h1, -BIG, le, ALU.mult, ALU.add))
            first_max(le, EG, ST[:, 68:70], h2)
            tell(v.tensor_tensor(ST[:, 96:98], ST[:, 68:70], ST[:, 66:68], ALU.subtract), "r_diff", 1)
            link(v.tensor_tensor(st(384, TT, EG), h1, h2, ALU.add))
            for tt in range(TT):
                link(v.tensor_tensor(SEL[:, tt, :].rearrange("p (g e) -> p g e", g=NG), colb(hg[:, tt, :], EG),
                                     midb(st(384, TT, EG)[:, tt, :], NG), ALU.mult))
            dve.sem_inc(sem("chosen"), 1)
            dve.wait_ge(sem("r_exp"), 2)
            link(v.tensor_reduce(ST[:, 100:102], ST[:, 80:88].rearrange("p (t g) -> p t g", t=TT), AX.X, ALU.add))
            link(v.tensor_scalar(ST[:, 102:104], ST[:, 98:100], 1.0, None, ALU.add))
            link(v.tensor_tensor(ST[:, 102:104], ST[:, 102:104], ST[:, 100:102], ALU.mult))
            link(v.reciprocal(ST[:, 102:104], ST[:, 102:104]))
            link(v.tensor_tensor(ST[:, 98:100], ST[:, 98:100], ST[:, 102:104], ALU.mult))
            link(v.tensor_tensor(h1, h1, colb(ST[:, 102:104], EG), ALU.mult))
            link(v.tensor_tensor(h2, h2, colb(ST[:, 98:100], EG), ALU.mult))
            link(v.tensor_tensor(h1, h1, h2, ALU.add))
            for tt in range(TT):
                link(v.tensor_tensor(CWC[:, tt, :].rearrange("p (g e) -> p g e", g=NG), colb(hg[:, tt, :], EG),
                                     midb(h1[:, tt, :], NG), ALU.mult))
            link(v.memset(ZERO, 0.0))
            dve.wait_ge(sem("places_raw"), 1)
            link(v.tensor_tensor(RK, PS[:, 0, 0:2 * NE].rearrange("p (t e) -> p t e", t=TT), SEL, ALU.mult))
            link(v.tensor_reduce(ST[:, 0:1], PS[:, 0, 64:64 + NE], AX.X, ALU.max))
            link(v.tensor_scalar(ST[:, 1:2], ST[:, 0:1], float(CAP) + 0.5, 1.0, ALU.is_gt, ALU.add))
            for m in range(2, T // CAP):
                link(v.tensor_scalar(ST[:, 2:3], ST[:, 0:1], m * CAP + 0.5, None, ALU.is_gt))
                link(v.tensor_tensor(ST[:, 1:2], ST[:, 1:2], ST[:, 2:3], ALU.add))
            link(v.tensor_copy(RNDS[:, :], ST[:, 1:2]))
            dve.sem_inc(sem("rounds"), 1)
            n_rounds = rounds(dve)

            PLACE = CK[:, C_PLACE:C_PLACE + CAP].unsqueeze(1).unsqueeze(1).to_broadcast([P, TT, 2, CAP])

            def of_pair(table, i):
                return table[:, :, bass.ds(i * 2, 2)].unsqueeze(3).to_broadcast([P, TT, 2, CAP])

            def places(i):
                v.tensor_tensor(SEL1, PLACE, of_pair(RK, i), ALU.is_equal).then_inc(sem("ex_places"), 1)

            def weights(n, i):
                dve.wait_ge(sem("ex_places"), n + 1)
                v.tensor_tensor(SELW, SEL1, of_pair(CWC, i), ALU.mult).then_inc(sem("ex_weights"), 1)

            def take_gather(n):
                dve.wait_ge(sem("ex_gather"), n * 2 + 2)
                v.tensor_copy(XG[:, 4:8, :], PS[:, 7, :].rearrange("p (k t) -> p k t", k=4))\
                    .then_inc(sem("ex_xg1"), 1)

            def pair(n, i, last_pair):
                dve.wait_ge(sem("ex_silu"), n + 1)
                dve.wait_ge(sem("block_used"), n * 6 + (B_MOE + 4))
                v.tensor_tensor(HIDR, SGU, PS[:, 5, :], ALU.mult).then_inc(sem("ex_hid"), 1)
                if not last_pair:
                    dve.wait_ge(sem("ex_weights"), n + 1)
                    places(i + 1)
                dve.wait_ge(sem("ex_swT_raw"), n + 1)
                v.tensor_copy(SWT, PS[:, 5, 0:T]).then_inc(sem("ex_swT"), 1)
                if not last_pair:
                    weights(n + 1, i + 1)
                    take_gather(n + 1)
                dve.wait_ge(sem("block_used"), n * 6 + (B_MOE + 6))
                v.tensor_copy(YSB[:, NB:D], PS[:, 7, :]).then_inc(sem("ex_y1"), 1)

            with dve.Fori(0, n_rounds) as r:
                places(0)
                weights(r * PAIRS, 0)
                take_gather(r * PAIRS)
                with dve.Fori(0, PAIRS - 1) as i:
                    pair(r * PAIRS + i, i, False)
                pair(r * PAIRS + (PAIRS - 1), PAIRS - 1, True)
                v.tensor_scalar(RK, RK, -float(CAP), None, ALU.add).then_inc(sem("next_places"), 1)
                dve.wait_ge(sem("next_places"), r + 1)
            gated_residual(1, "moe_rows", 1)


_IN = ["x", "norm_g", "hg_lower_bound", "ev_w_in", "ev_hg_norm_g", "ev_ret_norm_g", "ev_w_out", "od_w_in",
       "od_conv_w", "od_conv_b", "od_gate_b", "od_ml_norm_g", "od_w_out", "mlp_w1", "mlp_w2", "c_2", "w_ada_2",
       "b_ada_2", "g_norm1_2", "g_norm2_2", "w_in_2", "g_q_2", "g_k_2", "conv_w_2", "conv_b_2", "w_pa_2",
       "w_pb_2", "w_o_2", "w_rg_2", "b_rg_2", "w_re_2", "b_re_2", "w1_2", "w3_2", "w2_2"]


def kernel(**inputs):
    import concourse.bacc as bacc
    from concourse.bass_utils import run_bass_kernel_spmd

    nc = bacc.Bacc("TRN2", target_bir_lowering=False, num_devices=1)
    keep, mix = shape_constants()
    arrays, A = {}, {}
    for name in _IN:
        arrays[f"in_{name}"] = np.ascontiguousarray(inputs[name])
    arrays["in_keep"], arrays["in_mix"] = keep, mix
    for name, a in arrays.items():
        A[name[3:]] = nc.dram_tensor(name, a.shape, F32, kind="ExternalInput").ap()
    out = nc.dram_tensor("out", (1, T, D), F32, kind="ExternalOutput").ap()
    block_program(nc, A, out)
    r = run_bass_kernel_spmd(nc, [arrays], core_ids=[0])
    return r.results[0]["out"]
```

```python
from contextlib import ExitStack

import numpy as np

import concourse.bass as bass
from concourse import mybir

F32 = mybir.dt.float32
ALU = mybir.AluOpType
ACT = mybir.ActivationFunctionType
AX = mybir.AxisListType

P = 128
T = 256
TT = T // P
D = 1024
KT = D // P
FF = 4096
EPS = 1e-6
NB = 512
CH = 64
HG_D = 128
RV_D = 256
QK = 128
AH, AD = 8, 64
NE, NG, EG, DE = 32, 4, 8, 512
GCAP = 15.0
SLOTS = 4
BW = 4096
BIG = 1.0e30

EV_IN, EV_OUT = 10, 3
MLP_B = 2 * (FF // NB)
OD_IN, OD_OUT = 6, 2
IN2, PA, PB, WO = 10, 1, 1, 2
B_EV_IN = 0
B_EV_OUT = B_EV_IN + EV_IN
B_MLP0 = B_EV_OUT + EV_OUT
B_OD_IN = B_MLP0 + MLP_B
B_OD_OUT = B_OD_IN + OD_IN
B_MLP1 = B_OD_OUT + OD_OUT
B_IN2 = B_MLP1 + MLP_B
B_PA = B_IN2 + 8
B_PB = B_IN2 + 10
B_IN2_AT = [B_IN2 + b for b in (0, 1, 2, 3, 4, 5, 6, 7, 9, 11)]
B_WO = B_IN2 + IN2 + PA + PB
B_MOE = B_WO + WO

ADA = 6

C_ID = 0
C_TRI = C_ID + P
C_CAU = C_TRI + P
C_NEG = C_CAU + P
C_SEL = C_NEG + 3 * P
C_CS2 = C_SEL + 4 * P
C_FIRST = C_CS2 + 4 * 8
C_ONE = C_FIRST + 8
C_PLACE = C_ONE + P
C_STEP = C_PLACE + 64
C_KEEP = C_STEP + 4
M_LEV = 0
M_DEC = M_LEV + 8 * P
M_CS = M_DEC + 4 * 3 * P
M_END = M_CS + 4 * 64

R_G = 0
R_CW = 32
R_CB = 64
R_G1, R_G2 = 72, 80
R_CW2 = 88
R_CB2 = 100
R_C = 104
R_END = 112


PROJ_BLOCKS = ([B_EV_IN + b for b in range(EV_IN)] + [B_OD_IN + b for b in range(OD_IN)]
               + B_IN2_AT)
MIX_EV = [(6, 0, 1536, 0), (7, 1, 1536, 0), (4, 0, 4096, 4), (5, 0, 4608, 8), (6, 1, 4096, 4), (7, 1, 4608, 8)]
MIX_OD = [(4, 0, 2048, 0), (5, 0, 2560, 4), (6, 1, 2048, 0), (7, 1, 2560, 4)]
Y_BLOCKS = [B_EV_OUT + EV_OUT - 1, B_MLP0 + MLP_B - 1, B_OD_OUT + OD_OUT - 1, B_MLP1 + MLP_B - 1]
NGRP = FF // NB
AR_END = 14592
CAP = 64
PAIRS = NE // 2
SLOT_MOE = ((6, 7, 3, 0, 4, 5), (1, 2, 8, 0, 4, 5))


def ring_fulls(s):
    return len([b for b in range(B_MOE) if b % SLOTS == s]) if s < SLOTS else 0


def shape_constants():
    i = np.arange(P)
    s, t = i[:, None], i[None, :]
    keep = np.zeros((P, C_KEEP), np.float32)
    keep[:, C_ID:C_ID + P] = s == t
    keep[:, C_TRI:C_TRI + P] = (s <= t) & (s // CH == t // CH)
    keep[:, C_CAU:C_CAU + P] = s <= t
    neg = np.where(t > s, -BIG, 0.0)
    keep[:, C_NEG:C_NEG + P] = neg
    keep[:, C_NEG + 2 * P:C_NEG + 3 * P] = neg
    for h in range(4):
        keep[h, C_SEL + h * P:C_SEL + (h + 1) * P] = 1.0
    pos = np.arange(T, dtype=np.float32)
    half = 8
    inv = (500000.0 ** (-np.arange(0, 2 * half, 2, dtype=np.float32) / np.float32(2 * half))).astype(np.float32)
    ang = (pos[:, None] * inv[None, :]).astype(np.float32)
    for tt in range(TT):
        keep[:, C_CS2 + tt * 8:C_CS2 + tt * 8 + 8] = np.cos(ang[tt * P:(tt + 1) * P])
        keep[:, C_CS2 + 16 + tt * 8:C_CS2 + 16 + tt * 8 + 8] = np.sin(ang[tt * P:(tt + 1) * P])
    keep[:, C_FIRST:C_FIRST + 8] = np.arange(8, 0, -1)
    keep[:, C_ONE:C_ONE + P] = 1.0
    keep[:, C_PLACE:C_PLACE + 64] = np.arange(1, 65)
    keep[:, C_STEP:C_STEP + T // CAP] = np.arange(T // CAP) * CAP + 0.5
    mix = np.zeros((P, M_END), np.float32)
    mix[:, M_LEV:M_LEV + P] = s == t
    for n in range(7):
        m = 1 << n
        mix[:, M_LEV + (n + 1) * P:M_LEV + (n + 2) * P] = (
            (s // (2 * m) == t // (2 * m)) & (s // m % 2 == 0) & (t // m % 2 == 1))
    for h in range(4):
        lg = np.log1p(-np.exp2(-5.0 - h))
        at = M_DEC + h * 3 * P
        diag = np.where(s <= t, np.exp(lg * (t - s)), 0.0)
        mix[:, at:at + P] = diag
        mix[:, at + P:at + 2 * P] = np.exp(lg * (t + P - s))
        mix[:, at + 2 * P:at + 3 * P] = diag
    inv = (10000.0 ** (-np.arange(64, dtype=np.float32) / np.float32(64))).astype(np.float32)
    ang = (pos[:, None] * inv[None, :]).astype(np.float32)
    for tt in range(TT):
        mix[:, M_CS + tt * 64:M_CS + tt * 64 + 64] = np.cos(ang[tt * P:(tt + 1) * P])
        mix[:, M_CS + 128 + tt * 64:M_CS + 128 + tt * 64 + 64] = np.sin(ang[tt * P:(tt + 1) * P])
    return keep, mix


def block_program(nc, A, out):
    ctx = ExitStack()
    with ctx:
        sems = {}

        def sem(name):
            if name not in sems:
                sems[name] = ctx.enter_context(nc.semaphore(name))
            return sems[name]

        def sb(name, *shape):
            return ctx.enter_context(nc.sbuf_tensor(name, list(shape), F32))

        def sb_i(name, *shape):
            return ctx.enter_context(nc.sbuf_tensor(name, list(shape), mybir.dt.int32))

        X = sb("x_rows", P, TT, D)
        XH = sb("normalised", P, TT * D + KT * T)
        XN = XH[:, 0:TT * D].rearrange("p (t n) -> p t n", t=TT)
        HT = XH[:, TT * D:TT * D + KT * T].rearrange("p (k t) -> p k t", k=KT)
        PR = sb("proj_rows", P, TT, 10 * NB)
        W = sb("weights", P, SLOTS, BW)
        AR = sb("arena", P, AR_END)
        GA = sb("ga_rows", P, 2, D)
        CK = sb("constants", P, C_KEEP)
        GC = sb("g_cols", P, R_END)
        BC = sb("b_ada_cols", P, 48)
        MC = sb("mod_cols", P, 4, KT)
        GM = sb("gain_cols", P, 2, KT)
        ST = sb("stats", P, 256)
        HN = sb("head_gains", P, 128 + 256 + 256 + 128)
        RB = sb("router_bias", P, NG + NE)
        WR = sb("router_weights", P, KT, NG + NE)
        WG = sb("gate_weights", P, KT, 8)
        G4 = sb("gate_bias", 4, 4)
        PS = ctx.enter_context(nc.psum_tensor("PS", [P, 8, NB], F32))

        GB = PR[:, 0, 0:D]

        def ar(at, *shape):
            n = int(np.prod(shape))
            v = AR[:, at:at + n]
            if len(shape) == 1:
                return v
            names = "abcd"[:len(shape)]
            return v.rearrange(f"p ({' '.join(names)}) -> p {' '.join(names)}",
                               **{c: k for c, k in zip(names[:-1], shape[:-1])})

        K1 = 1024
        QT, KTT, BT = ar(0, 4, T), ar(K1, 4, T), ar(2 * K1, 4, T)
        EX = [ar((3 + i) * K1, K1) for i in range(2)]
        QS = [ar((5 + i) * K1, 4, T) for i in range(2)]
        KS = [ar((7 + i) * K1, 4, T) for i in range(2)]
        SC = ar(9 * K1, 8, P)
        TMP = ar(10 * K1, K1)
        S01 = ar(11 * K1, 4, P)
        MX = ar(11 * K1 + 512, M_END)
        LB = ar(3 * K1, 3, 512)
        BO = ar(10 * K1, 512)
        LF = ar(5 * K1, 2, 512)
        RR = XN[:, :, :]
        RT = ar(0, 8, T)
        PT = ar(2 * K1, 4, 3 * P)
        HB = ar(4 * K1, 2 * K1)
        YT = ar(8 * K1, 12, T)
        CR = ar(11 * K1, 8 * (T + 3))
        CRv = CR.rearrange("p (a b) -> p a b", a=8)
        CT = ar(0, 8, T)
        HBW = ar(6 * K1, 4, 3 * P)
        GR = AR[0:4, 4 * K1:6 * K1].rearrange("p (a b) -> p a b", a=8)
        T2 = ar(0, 8, T)
        AS = ar(2 * K1, AH, 3 * P)
        APT = ar(5 * K1, 24, P)
        UT = ar(8 * K1, 4 * (T + 2))
        UTv = UT.rearrange("p (a b) -> p a b", a=4)
        BGT = ar(9 * K1 + 16, 4, T)
        YBT = ar(10 * K1 + 16, 4, T)
        YAT = ar(11 * K1 + 16, 4, T)
        YA = ar(12 * K1 + 16, 2, 512)
        MT = ar(0, 8, T)
        H1 = [ar(i * K1, 4, T) for i in range(2)]
        HR = [ar(2 * K1 + 512 * i, 2, T) for i in range(4)]
        PRF = PR[:, :, :].rearrange("p a b -> p (a b)")
        AW = [PRF[:, 2 * K1 + x * BW:2 * K1 + (x + 1) * BW].rearrange("p (k n) -> p k n", k=KT) for x in range(2)]
        AC = ar(4 * K1, ADA, NB)
        CWC = ar(5 * K1 + 256, TT, NE)
        SEL = ar(5 * K1 + 320, TT, NE)
        RK = ar(5 * K1 + 384, TT, NE)
        H2R = ar(0, TT, D)
        XG = ar(2 * K1, KT, P)
        SGU = ar(3 * K1, NB)
        HIDR = ar(3 * K1 + 512, NB)
        HIDT = ar(4 * K1, 4, P)
        SWT = ar(4 * K1 + 512, T)
        SEL1 = ar(4 * K1 + 768, TT, 2, CAP)
        SELW = ar(5 * K1, TT, 2, CAP)
        YSB = PRF[:, 2 * BW:2 * BW + D]
        ZERO = ar(5 * K1 + 448, NB)
        RNDS = sb_i("rounds", P, 1)
        CS = ST[:, 104:112]
        IDN = CK[:, C_ID:C_ID + P]
        ONE = CK[:, C_ONE:C_ONE + P]

        def colb(ap, n):
            return ap.unsqueeze(2).to_broadcast([P, ap.shape[1], n])

        def midb(ap, n):
            return ap.unsqueeze(1).to_broadcast([P, n, ap.shape[1]])

        def moe_slot(odd, c):
            s = SLOT_MOE[odd][c]
            if s < SLOTS:
                return W[:, s, :]
            if s < SLOTS + 2:
                return PRF[:, (s - SLOTS) * BW:(s - SLOTS + 1) * BW]
            if s == SLOTS + 4:
                return XH[:, 0:BW]
            at = AR_END - (SLOTS + 4 - s) * BW
            return AR[:, at:at + BW]

        def rounds(eng):
            eng.wait_ge(sem("rounds"), 1)
            return eng.value_load(RNDS[0:1, 0:1], min_val=1, max_val=T // CAP)

        def slot_of(b):
            return b % SLOTS

        def fulls(b):
            return 16 * (b // SLOTS + 1)

        def n_type(w, at):
            return w[:, bass.ds(at, NB)].rearrange("(k p) n -> p k n", p=P)

        def k_type(w, at):
            return w[bass.ds(at, NB), :].rearrange("(k p) n -> p k n", p=P)

        def wn(s):
            return W[:, s, :].rearrange("p (k n) -> p k n", k=KT)

        def wk(s):
            return W[:, s, :].rearrange("p (k n) -> p k n", k=4)

        ROW_LOADS = [(R_G + 8 * (2 * l + i), 0, A["norm_g"][l, 2 * i].rearrange("(k p) -> k p", p=P))
                     for l in range(2) for i in range(2)]
        ROW_LOADS += [
            (R_CW, 0, A["od_conv_w"][0].rearrange("j (k p) -> (j k) p", p=P)),
            (R_CB, 0, A["od_conv_b"].rearrange("a (k p) -> (a k) p", p=P)),
            (R_G1, 0, A["g_norm1_2"].rearrange("a (k p) -> (a k) p", p=P)),
            (R_G2, 0, A["g_norm2_2"].rearrange("a (k p) -> (a k) p", p=P)),
            (R_CW2, 0, A["conv_w_2"][0].rearrange("j (k p) -> (j k) p", p=P)),
            (R_CB2, 0, A["conv_b_2"].rearrange("a (k p) -> (a k) p", p=P)),
            (R_C, 0, A["c_2"].rearrange("a (k p) -> (a k) p", p=P)),
            (0, P, A["b_ada_2"].rearrange("a (k p) -> (a k) p", p=P)),
        ]

        def row_loads(queue, part):
            for at, col, src in ROW_LOADS[part::2]:
                queue.dma_start(AR[at:at + src.shape[0], col:col + P], src).then_inc(sem("rows_in"), 16)

        def small_loads(ld):
            ld("head_in", HN[:, 0:128], A["ev_hg_norm_g"][0].partition_broadcast(P))
            ld("head_in", HN[:, 128:384], A["ev_ret_norm_g"][0].partition_broadcast(P))
            ld("head_in", HN[:, 384:640], A["od_ml_norm_g"][0].partition_broadcast(P))
            ld("head_in", HN[:, 640:704], A["g_q_2"][0].partition_broadcast(P))
            ld("head_in", HN[:, 704:768], A["g_k_2"][0].partition_broadcast(P))
            ld("ga_in", GA[:, 0, :], A["b_ada_2"][0, 2 * D:3 * D].partition_broadcast(P))
            ld("ga_in", GA[:, 1, :], A["b_ada_2"][0, 5 * D:6 * D].partition_broadcast(P))
            ld("router_in", RB[:, 0:NG], A["b_rg_2"][0].partition_broadcast(P))
            ld("router_in", RB[:, NG:NG + NE], A["b_re_2"][0].partition_broadcast(P))
            ld("router_in", WR[:, :, 0:NG], A["w_rg_2"][0].rearrange("(k p) n -> p k n", p=P))
            ld("router_in", WR[:, :, NG:NG + NE], A["w_re_2"][0].rearrange("(k p) n -> p k n", p=P))
            ld("gate_in", WG[:, :, :], A["od_w_in"][0, :, 6 * NB:6 * NB + 8].rearrange("(k p) n -> p k n", p=P))
            for g in range(2):
                ld("gate_in", G4[:, g:g + 1], A["od_gate_b"][0, g].rearrange("(h a) -> h a", a=1))

        block = ctx.enter_context(nc.Block())

        @block.sync
        def _(sp):
            def load(b, src):
                s = slot_of(b)
                if b >= SLOTS:
                    sp.wait_ge(sem("block_used"), b - SLOTS + 1)
                sp.dma_start(W[:, s, :].rearrange("p (k n) -> p k n", n=src.shape[2]), src)\
                  .then_inc(sem(f"slot{s}_full"), 16)

            xv = A["x"][0].rearrange("(t p) n -> p t n", p=P)
            for tt in range(TT):
                sp.dma_start(X[:, tt, :], xv[:, tt, :]).then_inc(sem(f"x{tt}_in"), 16)
            sp.dma_start(CK[:, :], A["keep"]).then_inc(sem("const_in"), 16)

            row_loads(nc.sync, 0)

            def ld(name, dst, src):
                sp.dma_start(dst, src).then_inc(sem(name), 16)

            for b in range(EV_IN):
                load(B_EV_IN + b, n_type(A["ev_w_in"][0], b * NB))
                if b == 0:
                    ld("lb_in", LB, A["hg_lower_bound"].partition_broadcast(P))
                elif b == 1:
                    ld("mix_in", MX, A["mix"])
                elif b == 3:
                    small_loads(ld)
            for b in range(EV_OUT):
                load(B_EV_OUT + b, k_type(A["ev_w_out"][0], b * NB))

            def mlp_loads(l, base):
                w1, w2 = A["mlp_w1"][l], A["mlp_w2"][l]
                load(base, n_type(w1, 0))
                load(base + 1, n_type(w1, NB))
                load(base + 2, k_type(w2, 0))
                with sp.Fori(0, (NGRP - 2) // 2) as i:
                    for c in range(4):
                        b = base + 3 + c
                        s = slot_of(b)
                        sp.wait_ge(sem("block_used"), i * 4 + (b - SLOTS + 1))
                        g = 1 + c // 2
                        src = n_type(w1, i * (2 * NB) + (g + 1) * NB) if c % 2 == 0 else k_type(w2, i * (2 * NB) + g * NB)
                        sp.dma_start(W[:, s, :].rearrange("p (k n) -> p k n", n=src.shape[2]), src)\
                          .then_inc(sem(f"slot{s}_full"), 16)
                    for x in range(2):
                        sp.wait_ge(sem("ada_free"), i * 2 + (ADA * l + x + 1))
                        sp.dma_start(AW[x], n_type(A["w_ada_2"][0], (i * 2 + (ADA * l + x)) * NB))\
                          .then_inc(sem(f"ada{x}_full"), 16)
                load(base + MLP_B - 1, k_type(w2, (NGRP - 1) * NB))

            mlp_loads(0, B_MLP0)
            for b in range(OD_IN):
                load(B_OD_IN + b, n_type(A["od_w_in"][0], b * NB))
            for b in range(OD_OUT):
                load(B_OD_OUT + b, k_type(A["od_w_out"][0], b * NB))
            mlp_loads(1, B_MLP1)
            for b in range(8):
                load(B_IN2_AT[b], n_type(A["w_in_2"][0], b * NB))
            load(B_PA, k_type(A["w_pa_2"][0], 0))
            load(B_IN2_AT[8], n_type(A["w_in_2"][0], 8 * NB))
            load(B_PB, k_type(A["w_pb_2"][0], 0))
            load(B_IN2_AT[9], n_type(A["w_in_2"][0], 9 * NB))
            for b in range(WO):
                load(B_WO + b, k_type(A["w_o_2"][0], b * NB))

            w1f = A["w1_2"][0].rearrange("e d f -> (e d) f")
            w3f = A["w3_2"][0].rearrange("e d f -> (e d) f")
            w2f = A["w2_2"][0].rearrange("e d f -> (e d) f")

            def expert_load(i, c, odd):
                kind, x = c // 2, c % 2
                if kind < 2:
                    src = (w1f, w3f)[kind][bass.ds(i * (2 * D) + x * D, D), :].rearrange("(k p) n -> p k n", p=P)
                else:
                    src = w2f[bass.ds(i * (2 * DE) + x * DE, DE), :].rearrange("(k p) n -> p k n", p=P)
                sp.dma_start(moe_slot(odd, c).rearrange("p (k n) -> p k n", n=src.shape[2]), src)\
                  .then_inc(sem(f"slot{SLOT_MOE[odd][c]}_full"), 16)

            def first_blocks(before, i, odd):
                for c in range(2):
                    sp.wait_ge(sem("block_used"), before + i * 6 + (B_MOE + 2 - 12))
                    expert_load(i, c, odd)

            def third_block(before, i, odd):
                sp.wait_ge(sem("block_used"), before + i * 6 + (B_MOE + 4 - 12))
                expert_load(i, 2, odd)

            def last_block(before, i, odd, c):
                sp.wait_ge(sem("block_used"), before + i * 6 + (B_MOE + 2 * (c // 2 + 1) - 6))
                expert_load(i, c, odd)

            def rest_of_round(before):
                with sp.Fori(0, PAIRS // 2 - 1) as j:
                    for h in range(2):
                        i, odd = j * 2 + (1 + h), 1 - h
                        first_blocks(before, j * 2 + (2 + h), h)
                        last_block(before, i, odd, 3)
                        third_block(before, j * 2 + (2 + h), h)
                        last_block(before, i, odd, 4)
                        last_block(before, i, odd, 5)
                for c in range(3, 6):
                    last_block(before, PAIRS - 1, 1, c)

            for c in range(2):
                sp.wait_ge(sem("block_used"), B_PB + 1)
                expert_load(0, c, 0)
            sp.wait_ge(sem("block_used"), B_PB + 1)
            expert_load(0, 2, 0)
            sp.wait_ge(sem("block_used"), B_IN2_AT[9] + 1)
            expert_load(0, 3, 0)
            sp.wait_ge(sem("mg_T"), 4)
            expert_load(0, 4, 0)
            expert_load(0, 5, 0)
            for c in range(2):
                sp.wait_ge(sem("block_used"), B_WO + c + 1)
                expert_load(1, c, 1)
            sp.wait_ge(sem("h2_raw"), 4)
            expert_load(1, 2, 1)
            rest_of_round(0)
            n_rounds = rounds(sp)
            with sp.If(n_rounds > 1):
                with sp.Fori(1, n_rounds) as r:
                    before = r * (6 * PAIRS)
                    first_blocks(before, 0, 0)
                    third_block(before, 0, 0)
                    for c in range(3, 6):
                        last_block(before, 0, 0, c)
                    first_blocks(before, 1, 1)
                    third_block(before, 1, 1)
                    rest_of_round(before)

            for tt in range(TT):
                sp.wait_ge(sem("x_final"), tt + 1)
                sp.dma_start(out[0].rearrange("(t p) n -> p t n", p=P)[:, tt, :], X[:, tt, :])\
                  .then_inc(sem("out_stored"), 16)
            sp.wait_ge(sem("out_stored"), 32)

        @block.gpsimd
        def _(pool):
            powers = [0]

            def power(a, b, n, name, count):
                powers[0] += 1
                pool.wait_ge(sem(name), count)
                nc.gpsimd.tensor_scalar(ST[:, a:b], ST[:, a:b], 1.0 / n, EPS, ALU.mult, ALU.add)\
                    .then_inc(sem("mean_ready"), 1)
                pool.wait_ge(sem("mean_ready"), powers[0])
                nc.gpsimd.tensor_tensor(ST[:, a:b], ST[:, a:b], ST[:, 192:192 + b - a], ALU.pow)\
                    .then_inc(sem("rstd_ready"), 1)

            def norm_powers(n):
                for tt in range(TT):
                    power(tt, tt + 1, D, "x_sq", 2 * n + tt + 1)

            def y_powers(r):
                for tt in range(TT):
                    power(2 + tt, 3 + tt, D, "y_sq", 2 * r + tt + 1)

            def gains(r, name, count):
                pool.wait_ge(sem(name), count)
                nc.gpsimd.dma_start(GB, A["norm_g"][r // 2, 1 + 2 * (r % 2)].partition_broadcast(P))\
                    .then_inc(sem("gain_in"), 16)

            nc.gpsimd.memset(ST[:, 192:224], -0.5).then_inc(sem("half_ready"), 1)
            pool.wait_ge(sem("half_ready"), 1)
            norm_powers(0)
            pool.wait_ge(sem("hg_kT"), 2)
            pool.wait_ge(sem("mix_in"), 16)
            for n in range(8):
                pool.wait_ge(sem("hg_exp"), n + 1)
                if n >= 2:
                    pool.wait_ge(sem("hg_prod"), n)
                nc.gpsimd.tensor_tensor(KS[n % 2], KTT, EX[n % 2].rearrange("p (a b) -> p a b", a=4),
                                        ALU.mult).then_inc(sem("hg_ks"), 1)
            pool.wait_ge(sem("proj_taken"), 6)
            x = PR[:, :, 2048:3072].rearrange("p t (h x d) -> p t h x d", x=2, d=64)
            r = RR.rearrange("p t (h x d) -> p t h x d", x=2, d=64)
            t1 = PR[:, 1, 0:512].rearrange("p (h d) -> p h d", h=8)
            t2 = PR[:, 1, 512:1024].rearrange("p (h d) -> p h d", h=8)
            steps = [0]

            def rope_step(out_, in0, in1, op):
                nc.gpsimd.tensor_tensor(out_, in0, in1, op).then_inc(sem("rope_step"), 1)
                steps[0] += 1
                pool.wait_ge(sem("rope_step"), steps[0])

            for tt in range(TT):
                cos = midb(MX[:, M_CS + tt * 64:M_CS + tt * 64 + 64], 8)
                sin = midb(MX[:, M_CS + 128 + tt * 64:M_CS + 128 + tt * 64 + 64], 8)
                x1, x2 = x[:, tt, :, 0, :], x[:, tt, :, 1, :]
                rope_step(t1, x1, cos, ALU.mult)
                rope_step(t2, x2, sin, ALU.mult)
                rope_step(r[:, tt, :, 0, :], t1, t2, ALU.subtract)
                rope_step(t1, x2, cos, ALU.mult)
                rope_step(t2, x1, sin, ALU.mult)
                rope_step(r[:, tt, :, 1, :], t1, t2, ALU.add)
            pool.sem_inc(sem("rope_done"), 1)
            power(16, 24, HG_D, "sums_ready", 1)
            power(16, 24, RV_D, "sums_ready", 2)
            gains(0, "mix_T", 6)
            y_powers(0)
            norm_powers(1)
            gains(1, "res_done", 1)
            y_powers(1)
            norm_powers(2)
            power(16, 24, RV_D, "sums_ready", 3)
            gains(2, "mix_T", 10)
            y_powers(2)
            norm_powers(3)
            gains(3, "res_done", 3)
            y_powers(3)
            norm_powers(4)
            power(128, 160, AD, "sums_ready", 4)
            norm_powers(5)

        @block.tensor
        def _(pe):
            mm = nc.tensor.matmul

            def quad(bank, srcs):
                for j, s in enumerate(srcs):
                    last = nc.tensor.transpose(PS[:, bank, j * P:(j + 1) * P], s, IDN)
                return last

            def transpose_stream(n):
                for q in range(4):
                    tt, half = q // 2, q % 2
                    if half == 0:
                        pe.wait_ge(sem("xn_ready"), 2 * n + tt + 1)
                    quad(4 + q, [XN[:, tt, (4 * half + j) * P:(4 * half + j + 1) * P] for j in range(4)])\
                        .then_inc(sem("xT_ready"), 1)

            def open_rows(tt):
                for bank in range(2 * tt, 2 * tt + 2):
                    mm(PS[:, bank, :], ZERO[:, 0:P], ZERO, start=True, stop=False, skip_group_check=True)

            proj_n = [0]

            def proj_block(b, norm=None):
                s, n = slot_of(b), proj_n[0]
                pe.wait_ge(sem(f"slot{s}_full"), fulls(b))
                if n >= 2:
                    pe.wait_ge(sem("proj_taken"), n - 1)
                for tt in range(TT):
                    if norm is not None:
                        pe.wait_ge(sem("hT_ready"), 4 * norm + 2 * tt + 2)
                    for k in range(KT):
                        last = mm(PS[:, 2 * (n % 2) + tt, :], HT[:, k, tt * P:(tt + 1) * P], wn(s)[:, k, :],
                                  start=(k == 0), stop=(k == KT - 1))
                last.then_inc(sem("block_used"), 1)
                proj_n[0] += 1

            def modulation(l):
                pe.wait_ge(sem("ada_sum"), ADA * (l + 1))
                for j in range(4):
                    for n in range(4):
                        mm(PS[:, 4, 4 * j + n:4 * j + n + 1], AC[:, j, n * P:(n + 1) * P], ONE[:, 0:1],
                           start=True, stop=True)
                for j in range(2):
                    last = mm(PS[:, 6 + j, :], ONE, AC[:, 4 + j, :], start=True, stop=True)
                last.then_inc(sem("mod_raw"), 1)

            def out_block(b, lhs, k0, first, last_k, bank=0, mark=True):
                s = slot_of(b)
                pe.wait_ge(sem(f"slot{s}_full"), fulls(b))
                for tt in range(TT):
                    for kk in range(4):
                        for n in range(2):
                            last = mm(PS[:, bank + 2 * tt + n, :], lhs[:, k0 + kk, tt * P:(tt + 1) * P],
                                      wk(s)[:, kk, n * NB:(n + 1) * NB],
                                      start=(first and kk == 0), stop=(last_k and kk == 3))
                    if last_k and mark and tt == 0:
                        last.then_inc(sem("y_tile0"), 1)
                last.then_inc(sem("block_used"), 1)

            pe.wait_ge(sem("const_in"), 16)
            transpose_stream(0)
            pe.wait_ge(sem("rows_in"), 16 * len(ROW_LOADS))
            nc.tensor.transpose(PS[:, 0, 0:R_END], AR[0:R_END, 0:P], IDN[0:R_END, 0:R_END])
            nc.tensor.transpose(PS[:, 1, 0:48], AR[0:48, P:2 * P], IDN[0:48, 0:48])\
                .then_inc(sem("cols_ready"), 1)

            pe.wait_ge(sem("cols_taken"), 1)
            for b in range(2):
                proj_block(B_EV_IN + b, 0 if b == 0 else None)
            pe.wait_ge(sem("proj_taken"), 1)
            for tt in range(TT):
                last = quad(4 + tt, [PR[:, tt, h * P:(h + 1) * P] for h in range(4)])
            last.then_inc(sem("hg_qT_raw"), 1)
            proj_block(B_EV_IN + 2)
            pe.wait_ge(sem("hg_f"), 1)
            for tt in range(TT):
                last = quad(6 + tt, [PR[:, tt, NB + h * P:NB + (h + 1) * P] for h in range(4)])
            last.then_inc(sem("hg_fT_raw"), 1)
            pe.wait_ge(sem("hg_lf"), 1)
            pe.wait_ge(sem("hg_qT"), 2)
            for tt in range(TT):
                for h in range(4):
                    last = mm(PS[:, 4 + tt, h * P:(h + 1) * P], LF[:, tt, h * P:(h + 1) * P],
                              CK[:, C_TRI:C_TRI + P], start=True, stop=True)
            last.then_inc(sem("hg_b_raw"), 1)

            def level(n):
                if n == 0:
                    pe.wait_ge(sem("hg_kT"), 2)
                    q, k = QT, KTT
                    pe.wait_ge(sem("hg_bT"), 2)
                else:
                    pe.wait_ge(sem("hg_qs"), n)
                    pe.wait_ge(sem("hg_ks"), n)
                    q, k = QS[(n - 1) % 2], KS[(n - 1) % 2]
                if n >= 2:
                    pe.wait_ge(sem("hg_masked"), n - 1)
                bank = 4 + 2 * (n % 2)
                if n == 8:
                    for h in range(4):
                        last = mm(PS[:, bank, h * P:(h + 1) * P], k[:, h, 0:P], q[:, h, P:T],
                                  start=True, stop=True)
                else:
                    for tt in range(TT):
                        for h in range(4):
                            last = mm(PS[:, bank + tt, h * P:(h + 1) * P], k[:, h, tt * P:(tt + 1) * P],
                                      q[:, h, tt * P:(tt + 1) * P], start=True, stop=True)
                last.then_inc(sem("hg_prod"), 1)

            level(0)
            for b, levels in ((3, (1,)), (4, (2, 3)), (5, (4, 5)), (6, (6, 7)), (7, (8,)), (8, ())):
                proj_block(B_EV_IN + b)
                for n in levels:
                    level(n)
            pe.wait_ge(sem("hg_masked"), 8)
            pe.wait_ge(sem("hg_s01"), 1)
            for tt in range(TT):
                for h in range(4):
                    o = PS[:, 6 + tt, h * P:(h + 1) * P]
                    last = mm(o, SC[:, 4 * tt + h, :], PR[:, tt, 2 * NB + h * P:2 * NB + (h + 1) * P],
                              start=True, stop=(tt == 0))
                    if tt:
                        last = mm(o, S01[:, h, :], PR[:, 0, 2 * NB + h * P:2 * NB + (h + 1) * P],
                                  start=False, stop=True)
            last.then_inc(sem("hg_out"), 1)

            pe.wait_ge(sem("rope_done"), 1)
            for tt in range(TT):
                if tt:
                    pe.wait_ge(sem("ret_T"), 2)
                for half in range(2):
                    quad(4 + half, [RR[:, tt, (4 * half + j) * P:(4 * half + j + 1) * P] for j in range(4)])\
                        .then_inc(sem("ret_T_raw"), 1)
            proj_block(B_EV_IN + 9)

            def mixed_T(quads, ready, values_):
                for (bank, tt, col, _), value in zip(quads, values_):
                    pe.wait_ge(sem(ready), value)
                    quad(bank, [PR[:, tt, col + j * P:col + (j + 1) * P] for j in range(4)])\
                        .then_inc(sem("mix_T_raw"), 1)

            def scores(lhs, name, waits):
                for h in range(4):
                    pe.wait_ge(sem(waits[h][0]), waits[h][1])
                    mm(PS[:, 4 + h, 0:T], lhs[:, 4 + h, 0:P], lhs[:, h, 0:T], start=True, stop=True)
                    mm(PS[:, 4 + h, T:T + P], lhs[:, 4 + h, P:T], lhs[:, h, P:T], start=True, stop=True)\
                        .then_inc(sem(name), 1)

            def values(col, ready, n, dens=None):
                pe.wait_ge(sem(ready), 4)
                for tt in range(TT):
                    for h in range(4):
                        v = slice(col + h * RV_D, col + (h + 1) * RV_D)
                        o = PS[:, 4 + 2 * tt + h // 2, (h % 2) * RV_D:(h % 2 + 1) * RV_D]
                        parts = [(PT[:, h, 0:P], 0)] if tt == 0 else [(PT[:, h, P:2 * P], 0), (PT[:, h, 2 * P:3 * P], 1)]
                        for i, (left, st) in enumerate(parts):
                            last = mm(o, left, PR[:, st, v], start=(i == 0), stop=(i == len(parts) - 1))
                        if dens is not None:
                            for i, (left, st) in enumerate(parts):
                                last = mm(dens[:, 4 * tt + h:4 * tt + h + 1], left, ONE[:, 0:1],
                                          start=(i == 0), stop=(i == len(parts) - 1))
                last.then_inc(sem(n), 1)

            mixed_T(MIX_EV[:2], "ev_y_half", (1, 2))
            scores(RT, "ret_s", (("ret_T", 4), ("ret_T", 4), ("mix_T", 1), ("mix_T", 2)))
            values(3072, "ret_p", "ret_out")
            pe.wait_ge(sem("proj_taken"), EV_IN)
            out_block(B_EV_OUT, YT, 0, True, False)
            mixed_T(MIX_EV[2:], "ev_y_half", (3, 3, 4, 4))
            pe.wait_ge(sem("mix_T"), 6)
            for i in range(1, EV_OUT):
                out_block(B_EV_OUT + i, YT, 4 * i, False, i == EV_OUT - 1)

            def mlp(l, base, norm):
                transpose_stream(norm)
                pe.wait_ge(sem("hT_ready"), 4 * norm + 4)

                def up(s, full, h):
                    pe.wait_ge(sem(f"slot{s}_full"), full)
                    for j in range(4):
                        for k in range(KT):
                            last = mm(PS[:, 4 + 2 * h + j // 2, (j % 2) * T:(j % 2 + 1) * T],
                                      wn(s)[:, k, j * P:(j + 1) * P], HT[:, k, :],
                                      start=(k == 0), stop=(k == KT - 1))
                        if j == 1:
                            last.then_inc(sem("hid_raw"), 1)
                    last.then_inc(sem("block_used"), 1)

                def down(s, full, h, hid, start, stop):
                    pe.wait_ge(sem(f"slot{s}_full"), full)
                    pe.wait_ge(sem("hid_ready"), hid)
                    for tt in range(TT):
                        for kk in range(4):
                            for n in range(2):
                                last = mm(PS[:, 2 * tt + n, :], H1[h][:, kk, tt * P:(tt + 1) * P],
                                          wk(s)[:, kk, n * NB:(n + 1) * NB],
                                          start=(start and kk == 0), stop=(stop and kk == 3))
                        if stop and tt == 0:
                            last.then_inc(sem("y_tile0"), 1)
                    last.then_inc(sem("block_used"), 1)

                H0 = l * 2 * NGRP
                up(slot_of(base), fulls(base), 0)
                up(slot_of(base + 1), fulls(base + 1), 1)
                down(slot_of(base + 2), fulls(base + 2), 0, H0 + 2, True, False)
                with pe.Fori(0, (NGRP - 2) // 2) as i:
                    for g in (1, 2):
                        b = base + 1 + 2 * g
                        up(slot_of(b), i * 16 + fulls(b), (g + 1) % 2)
                        down(slot_of(b + 1), i * 16 + fulls(b + 1), g % 2, i * 4 + (H0 + 2 * g + 2), False, False)
                b = base + MLP_B - 1
                down(slot_of(b), fulls(b), (NGRP - 1) % 2, H0 + 2 * NGRP, False, True)
                modulation(l)

            mlp(0, B_MLP0, 1)

            transpose_stream(2)
            for b in range(2):
                proj_block(B_OD_IN + b, 2 if b == 0 else None)
            pe.wait_ge(sem("gate_in"), 48)
            for g in range(2):
                for k in range(KT):
                    last = mm(PS[0:4, 7, g * T:(g + 1) * T], WG[:, k, 4 * g:4 * g + 4], HT[:, k, :],
                              start=(k == 0), stop=(k == KT - 1))
            last.then_inc(sem("gates_raw"), 1)
            proj_block(B_OD_IN + 2)
            pe.wait_ge(sem("gates_taken"), 1)
            pe.wait_ge(sem("proj_taken"), EV_IN + 2)
            for q in range(4):
                tt, half = q // 2, q % 2
                quad(4 + q, [PR[:, tt, (4 * half + j) * P:(4 * half + j + 1) * P] for j in range(4)])\
                    .then_inc(sem("conv_T_raw"), 1)
            proj_block(B_OD_IN + 3)
            pe.wait_ge(sem("conv_T"), 4)
            pe.wait_ge(sem("gates_done"), 1)
            for j, row in enumerate((3, 6)):
                for tt in range(TT):
                    last = mm(PS[:, 4, 8 * j + 4 * tt:8 * j + 4 * tt + 4], GR[:, row, tt * P:(tt + 1) * P],
                              IDN[0:4, 0:4], start=True, stop=True)
            last.then_inc(sem("acol_raw"), 1)
            for h in range(4):
                last = mm(PS[:, 5 + h // 2, (h % 2) * T:(h % 2 + 1) * T], CK[0:4, C_SEL + h * P:C_SEL + (h + 1) * P],
                          GR[:, 4, :], start=True, stop=True)
            last.then_inc(sem("mrow_raw"), 1)
            proj_block(B_OD_IN + 4)
            pe.wait_ge(sem("conv_done"), 1)
            scores(CT, "ml_s", (("wexp_in", 1),) * 4)
            pe.wait_ge(sem("proj_taken"), EV_IN + 5)
            values(1024, "ml_p", "ml_out", dens=PS[:, 0, 0:8])
            proj_block(B_OD_IN + 5)
            mixed_T(MIX_OD, "od_y_half", (1, 1, 2, 2))
            pe.wait_ge(sem("proj_taken"), EV_IN + OD_IN)
            pe.wait_ge(sem("mix_T"), 10)
            for i in range(OD_OUT):
                out_block(B_OD_OUT + i, YT, 4 * i, i == 0, i == OD_OUT - 1)
            mlp(1, B_MLP1, 3)

            transpose_stream(4)
            E0 = EV_IN + OD_IN
            for b in range(4):
                proj_block(B_IN2_AT[b], 4 if b == 0 else None)
            pe.wait_ge(sem("qk_ready"), 1)
            for q in range(4):
                tt, half = q // 2, q % 2
                quad(4 + q, [PR[:, tt, (4 * half + j) * P:(4 * half + j + 1) * P] for j in range(4)])\
                    .then_inc(sem("qk_T_raw"), 1)
            proj_block(B_IN2_AT[4])
            pe.wait_ge(sem("qk_T"), 4)

            def logits(h):
                pr = slice(64 * (h % 2), 64 * (h % 2) + 64)
                bank = 4 + h % 4
                if h >= 4:
                    pe.wait_ge(sem("at_s"), h - 3)
                mm(PS[:, bank, 0:P], T2[pr, h // 2, 0:P], T2[pr, 4 + h // 2, 0:P], start=True, stop=True)
                mm(PS[:, bank, P:3 * P], T2[pr, h // 2, P:T], T2[pr, 4 + h // 2, 0:T], start=True, stop=True)\
                    .then_inc(sem("at_s_raw"), 1)

            for h in range(AH):
                logits(h)
            proj_block(B_IN2_AT[5])
            pe.wait_ge(sem("at_s"), 8)
            pe.wait_ge(sem("at_exp"), 2 * AH)
            flat = AS.rearrange("p h (x s) -> p (h x) s", x=3)
            for q in range(6):
                if q >= 4:
                    pe.wait_ge(sem("at_pT"), q - 3)
                quad(4 + q % 4, [flat[:, 4 * q + j, :] for j in range(4)]).then_inc(sem("at_pT_raw"), 1)
            proj_block(B_IN2_AT[6])
            pe.wait_ge(sem("at_pT"), 6)
            for tt in range(TT):
                for h in range(AH):
                    o = PS[:, 6 + tt, h * AD:(h + 1) * AD]
                    v = slice(1024 + h * AD, 1024 + (h + 1) * AD)
                    for st in range(tt + 1):
                        last = mm(o, APT[:, 3 * h + tt + st, :], PR[:, st, v], start=(st == 0), stop=(st == tt))
            last.then_inc(sem("at_o"), 1)
            pe.wait_ge(sem("u_ready"), 1)
            for tt in range(TT):
                quad(4 + tt, [PR[:, tt, 1536 + j * P:1536 + (j + 1) * P] for j in range(4)])\
                    .then_inc(sem("u_T_raw"), 1)
            proj_block(B_IN2_AT[7])
            pe.wait_ge(sem("u_T"), 2)
            pe.wait_ge(sem("ya_ready"), 1)
            for tt in range(TT):
                quad(4 + tt, [YA[:, tt, j * P:(j + 1) * P] for j in range(4)]).then_inc(sem("ya_T_raw"), 1)
            for tt in range(TT):
                quad(6 + tt, [PR[:, tt, 2048 + j * P:2048 + (j + 1) * P] for j in range(4)])\
                    .then_inc(sem("u_T_raw"), 1)
            pe.wait_ge(sem("ya_T"), 2)
            pe.wait_ge(sem("u_T"), 4)
            out_block(B_PA, YAT, 0, True, True, bank=4, mark=False)
            proj_block(B_IN2_AT[8])
            pe.wait_ge(sem("yb_ready"), 1)
            pe.wait_ge(sem("pa_taken"), 1)
            out_block(B_PB, YBT, 0, True, True, bank=4, mark=False)
            proj_block(B_IN2_AT[9])
            for half in range(2):
                pe.wait_ge(sem("merged"), half + 1)
                for tt in range(TT):
                    c = 3072 + half * NB
                    quad(4 + 2 * tt + half, [PR[:, tt, c + j * P:c + (j + 1) * P] for j in range(4)])\
                        .then_inc(sem("mg_T_raw"), 1)
                pe.wait_ge(sem("proj_taken"), E0 + IN2)
                pe.wait_ge(sem("mg_T"), 2 * half + 2)
                out_block(B_WO + half, MT, 4 * half, half == 0, half == 1)
            pe.wait_ge(sem("x_new"), 9)
            pe.wait_ge(sem("zeroed"), 1)
            open_rows(0)
            transpose_stream(5)
            pe.wait_ge(sem("router_in"), 64)
            for tt in range(TT):
                for k in range(KT):
                    if k % 4 == 0:
                        pe.wait_ge(sem("hT_ready"), 20 + 2 * tt + k // 4 + 1)
                    last = mm(PS[:, 4, tt * 64:tt * 64 + NG + NE], HT[:, k, tt * P:(tt + 1) * P], WR[:, k, :],
                              start=(k == 0), stop=(k == KT - 1))
            last.then_inc(sem("router_raw"), 1)
            pe.wait_ge(sem("x_new"), 10)
            open_rows(1)
            pe.wait_ge(sem("router_taken"), 1)
            for q in range(4):
                tt, half = q // 2, q % 2
                quad(4 + q, [HT[:, 4 * half + j, tt * P:(tt + 1) * P] for j in range(4)]).then_inc(sem("h2_raw"), 1)
            pe.wait_ge(sem("chosen"), 1)
            pe.wait_ge(sem("h2_rows"), 1)
            mm(PS[:, 4, 0:NE], CK[:, C_CAU:C_CAU + P], SEL[:, 0, :], start=True, stop=True)
            mm(PS[:, 4, NE:2 * NE], ONE, SEL[:, 0, :], start=True, stop=False)
            mm(PS[:, 4, NE:2 * NE], CK[:, C_CAU:C_CAU + P], SEL[:, 1, :], start=False, stop=True)
            mm(PS[:, 4, 64:64 + NE], ONE, SEL[:, 0, :], start=True, stop=False)
            mm(PS[:, 4, 64:64 + NE], ONE, SEL[:, 1, :], start=False, stop=True).then_inc(sem("places_raw"), 1)
            pe.wait_ge(sem("h2_rows"), 4)
            n_rounds = rounds(pe)

            def gather():
                for dt in range(KT):
                    for tt in range(TT):
                        last = mm(PS[:, 6 + dt // 4, (dt % 4) * P:(dt % 4 + 1) * P], H2R[:, tt, dt * P:(dt + 1) * P],
                                  SEL1[:, tt, :, :], start=(tt == 0), stop=(tt == TT - 1))
                    if dt % 4 == 3:
                        last.then_inc(sem("ex_gather"), 1)

            def scatter(last_pair=False):
                for tt in range(TT):
                    for n in range(2):
                        last = mm(PS[:, 2 * tt + n, :], SWT[:, tt * P:(tt + 1) * P], YSB[:, n * NB:(n + 1) * NB],
                                  start=False, stop=last_pair, skip_group_check=True)
                    if last_pair:
                        last.then_inc(sem(f"moe_tile{tt}"), 1)

            def pair(n, m, odd, first, last_pair):
                def arrived(c):
                    s = SLOT_MOE[odd][c]
                    times = m if c < 3 else n
                    pe.wait_ge(sem(f"slot{s}_full"), times * 16 + 16 * (ring_fulls(s) + 1))

                pe.wait_ge(sem("ex_xg0"), n + 1)
                pe.wait_ge(sem("ex_xg1"), n + 1)
                for kind in range(2):
                    arrived(2 * kind)
                    arrived(2 * kind + 1)
                    if not first:
                        pe.wait_ge(sem(("ex_hT", "ex_swT")[kind]), n)
                    for k in range(KT):
                        for x in range(2):
                            w = moe_slot(odd, 2 * kind + x).rearrange("p (k n) -> p k n", k=KT)
                            last = mm(PS[CAP * x:CAP * (x + 1), 4 + kind, :], XG[:, k, CAP * x:CAP * (x + 1)],
                                      w[:, k, :], start=(k == 0), stop=(k == KT - 1))
                    last.then_inc(sem("block_used"), 2)
                if not first:
                    pe.wait_ge(sem("ex_y0"), n)
                    pe.wait_ge(sem("ex_y1"), n)
                    scatter()
                pe.wait_ge(sem("ex_hid"), n + 1)
                for j in range(4):
                    last = nc.tensor.transpose(PS[:, 4, j * P:(j + 1) * P], HIDR[:, j * P:(j + 1) * P], IDN)
                last.then_inc(sem("ex_T"), 1)
                pe.wait_ge(sem("ex_weights"), n + 1)
                for tt in range(TT):
                    last = nc.tensor.transpose(PS[:, 5, tt * P:(tt + 1) * P],
                                               SELW[:, tt, :, :].rearrange("p e c -> p (e c)"), IDN)
                last.then_inc(sem("ex_swT_raw"), 1)
                if not last_pair:
                    pe.wait_ge(sem("ex_places"), n + 2)
                    gather()
                pe.wait_ge(sem("ex_hT"), n + 1)
                arrived(4)
                arrived(5)
                for half in range(2):
                    if not last_pair:
                        pe.wait_ge(sem(("ex_xg0", "ex_xg1")[half]), n + 2)
                    for kk in range(4):
                        for x in range(2):
                            w = moe_slot(odd, 4 + x).rearrange("p (k n) -> p k n", k=4)
                            last = mm(PS[CAP * x:CAP * (x + 1), 6 + half, :], HIDT[:, kk, CAP * x:CAP * (x + 1)],
                                      w[:, kk, half * NB:(half + 1) * NB], start=(kk == 0), stop=(kk == 3))
                    if half == 0:
                        last.then_inc(sem("ex_y_raw"), 1)
                last.then_inc(sem("block_used"), 2)

            with pe.Fori(0, n_rounds) as r:
                pe.wait_ge(sem("ex_places"), r * PAIRS + 1)
                gather()
                pair(r * PAIRS, r * (PAIRS // 2), 0, True, False)
                with pe.Fori(0, PAIRS // 2 - 1) as j:
                    pair(r * PAIRS + j * 2 + 1, r * (PAIRS // 2) + j, 1, False, False)
                    pair(r * PAIRS + j * 2 + 2, r * (PAIRS // 2) + j + 1, 0, False, False)
                pair(r * PAIRS + (PAIRS - 1), r * (PAIRS // 2) + (PAIRS // 2 - 1), 1, False, True)
                pe.wait_ge(sem("ex_y0"), r * PAIRS + PAIRS)
                pe.wait_ge(sem("ex_y1"), r * PAIRS + PAIRS)
                pe.wait_ge(sem("ex_swT"), r * PAIRS + PAIRS)
                scatter(True)

        @block.scalar
        def _(act):
            a = nc.scalar.activation
            chain = [0]

            def link(ins):
                chain[0] += 1
                ins.then_inc(sem("act_step"), 1)
                act.wait_ge(sem("act_step"), chain[0])

            n_proj = [0]

            def evac(cols, func, scale=1.0):
                n = n_proj[0]
                act.wait_ge(sem("block_used"), PROJ_BLOCKS[n] + 1)
                src = PS[:, 2 * (n % 2):2 * (n % 2) + 2, :]
                a(PR[:, :, cols:cols + NB], src, func, scale=scale).then_inc(sem("proj_taken"), 1)
                n_proj[0] += 1
                act.wait_ge(sem("proj_taken"), n + 1)

            def stream_squares(n):
                for tt in range(TT):
                    if n == 0:
                        act.wait_ge(sem(f"x{tt}_in"), 16)
                    else:
                        act.wait_ge(sem("x_new"), 2 * (n - 1) + tt + 1)
                    a(XN[:, tt, :], X[:, tt, :], ACT.Square, accum_out=ST[:, tt:tt + 1]).then_inc(sem("x_sq"), 1)

            row_loads(nc.scalar, 1)
            stream_squares(0)
            act.wait_ge(sem("cols_ready"), 1)
            link(a(GC[:, :], PS[:, 0, 0:R_END], ACT.Copy))
            a(BC[:, :], PS[:, 1, 0:48], ACT.Copy).then_inc(sem("cols_taken"), 1)
            a(CS, GC[:, R_C:R_C + 8], ACT.Silu).then_inc(sem("c_silu"), 1)
            act.wait_ge(sem("lb_shifted"), 1)
            a(LB, LB, ACT.Exp).then_inc(sem("lb_exp"), 1)
            evac(0, ACT.Silu)
            evac(NB, ACT.Sigmoid)
            act.wait_ge(sem("hg_qT_raw"), 1)
            for tt in range(TT):
                a(QT[:, :, tt * P:(tt + 1) * P], PS[:, 4 + tt, :].rearrange("p (h t) -> p h t", h=4), ACT.Copy)\
                    .then_inc(sem("hg_qT"), 1)
            evac(2 * NB, ACT.Copy)
            act.wait_ge(sem("hg_f"), 1)
            a(LF, PR[:, :, NB:2 * NB], ACT.Ln).then_inc(sem("hg_lf"), 1)
            act.wait_ge(sem("hg_b_raw"), 1)
            for tt in range(TT):
                a(BT[:, :, tt * P:(tt + 1) * P], PS[:, 4 + tt, :].rearrange("p (h t) -> p h t", h=4), ACT.Copy)\
                    .then_inc(sem("hg_bT"), 1)
            kinds = {3: (ACT.Silu, 1.0), 4: (ACT.Copy, 1.0), 5: (ACT.Copy, QK ** -0.5), 6: (ACT.Copy, 1.0),
                     7: (ACT.Copy, 1.0), 8: (ACT.Silu, 1.0), 9: (ACT.Silu, 1.0)}

            def level_exp(n):
                act.wait_ge(sem("hg_diff"), n)
                a(EX[(n - 1) % 2], EX[(n - 1) % 2], ACT.Exp).then_inc(sem("hg_exp"), 1)

            def even_evac(b):
                evac(b * NB, *kinds[b])

            for levels, b in (((1, 2), 3), ((3, 4, 5), 4), ((6, 7), 5), ((8,), 6), ((), 7)):
                for n in levels:
                    level_exp(n)
                even_evac(b)
            act.wait_ge(sem("hg_prod"), 9)
            a(S01, PS[:, 4, :].rearrange("p (h t) -> p h t", h=4), ACT.Copy).then_inc(sem("hg_s01"), 1)
            even_evac(8)

            def squares(src, dst, wait, v, name):
                act.wait_ge(sem(wait), v)
                a(dst, src, ACT.Square).then_inc(sem(name), 1)

            squares(PS[:, 6:8, :], HB[:, 0:1024].rearrange("p (a b) -> p a b", a=2), "hg_out", 1, "hg_sq")
            for q in range(4):
                tt, half = q // 2, q % 2
                act.wait_ge(sem("ret_T_raw"), q + 1)
                a(RT[:, 4 * half:4 * half + 4, tt * P:(tt + 1) * P],
                  PS[:, 4 + half, :].rearrange("p (h t) -> p h t", h=4), ACT.Copy).then_inc(sem("ret_T"), 1)
            even_evac(9)

            n_mix = [0]

            def mix_evac(quads):
                for bank, tt, _, tile0 in quads:
                    n_mix[0] += 1
                    act.wait_ge(sem("mix_T_raw"), n_mix[0])
                    a(YT[:, tile0:tile0 + 4, tt * P:(tt + 1) * P],
                      PS[:, bank, :].rearrange("p (h t) -> p h t", h=4), ACT.Copy).then_inc(sem("mix_T"), 1)

            mix_evac(MIX_EV[:2])
            squares(PS[:, 4:8, :], HB.rearrange("p (a b) -> p a b", a=4), "ret_out", 1, "ret_sq")
            mix_evac(MIX_EV[2:])

            def relus(l, base, i, g):
                h = g % 2
                for j in range(2):
                    if j == 0:
                        act.wait_ge(sem("hid_raw"), i * 2 + (NGRP * l + g + 1))
                    else:
                        act.wait_ge(sem("block_used"), i * 4 + (base + max(1, 2 * g)))
                    a(HR[2 * h + j], PS[:, 4 + 2 * h + j, :].rearrange("p (f t) -> p f t", f=2), ACT.Relu)\
                        .then_inc(sem("hid_relu"), 1)

            def mlp(l, base):
                for g in (0, 1):
                    relus(l, base, 0, g)
                with act.Fori(0, (NGRP - 2) // 2) as i:
                    for g in (2, 3):
                        relus(l, base, i, g)

            n_y = [0]

            def y_square():
                n = n_y[0]
                for tt in range(TT):
                    if tt == 0:
                        act.wait_ge(sem("y_tile0"), n + 1)
                    else:
                        act.wait_ge(sem("block_used"), Y_BLOCKS[n] + 1)
                    a(XN[:, tt, :].rearrange("p (a b) -> p a b", a=2), PS[:, 2 * tt:2 * tt + 2, :], ACT.Square,
                      accum_out=ST[:, 2 + tt:3 + tt]).then_inc(sem("y_sq"), 1)
                n_y[0] += 1
                stream_squares(n_y[0])

            y_square()
            mlp(0, B_MLP0)
            y_square()
            evac(0, ACT.Copy)
            evac(NB, ACT.Copy)
            act.wait_ge(sem("gates_raw"), 1)
            act.wait_ge(sem("gate_b"), 1)
            a(GR[:, 0, :], PS[0:4, 7, 0:T], ACT.Tanh, bias=G4[:, 2:3], scale=1.0 / GCAP).then_inc(sem("g_tanh"), 1)
            a(GR[:, 1, :], PS[0:4, 7, T:2 * T], ACT.Tanh, bias=G4[:, 3:4], scale=1.0 / GCAP)\
                .then_inc(sem("g_tanh"), 1)
            act.wait_ge(sem("g_tanh"), 2)
            act.sem_inc(sem("gates_taken"), 1)
            link(a(GR[:, 1, :], GR[:, 1, :], ACT.Exp, scale=-GCAP))
            a(GR[:, 2, :], GR[:, 1, :], ACT.Ln, bias=1.0).then_inc(sem("g_softplus"), 1)
            evac(2 * NB, ACT.Copy)
            for q in range(4):
                tt, half = q // 2, q % 2
                act.wait_ge(sem("conv_T_raw"), q + 1)
                a(CRv[:, 4 * half:4 * half + 4, 3 + tt * P:3 + (tt + 1) * P],
                  PS[:, 4 + q, :].rearrange("p (h t) -> p h t", h=4), ACT.Copy).then_inc(sem("conv_T"), 1)
            act.wait_ge(sem("g_m"), 1)
            a(GR[:, 6, :], GR[:, 5, :], ACT.Exp, scale=-1.0).then_inc(sem("gates_done"), 1)
            evac(3 * NB, ACT.Copy)
            act.wait_ge(sem("conv_sum"), 1)
            a(CT, CT, ACT.Silu).then_inc(sem("conv_done"), 1)
            act.wait_ge(sem("wexp_in"), 1)
            a(HBW, HBW, ACT.Exp, scale=-1.0).then_inc(sem("wexp"), 1)
            evac(4 * NB, ACT.Sigmoid)
            act.wait_ge(sem("ml_o"), 1)
            a(XN[:, :, :], HB.rearrange("p (a b) -> p a b", a=2), ACT.Square).then_inc(sem("ml_sq"), 1)
            evac(5 * NB, ACT.Sigmoid)
            mix_evac(MIX_OD)
            y_square()
            mlp(1, B_MLP1)
            y_square()

            for b in range(2):
                evac(b * NB, ACT.Copy)
            a(HB.rearrange("p (a b) -> p a b", a=2), PR[:, :, 0:1024], ACT.Square).then_inc(sem("qk_sq"), 1)
            for b in range(2, 4):
                evac(b * NB, ACT.Copy)
            for q in range(4):
                tt, half = q // 2, q % 2
                act.wait_ge(sem("qk_T_raw"), q + 1)
                a(T2[:, 4 * half:4 * half + 4, tt * P:(tt + 1) * P],
                  PS[:, 4 + q, :].rearrange("p (h t) -> p h t", h=4), ACT.Copy).then_inc(sem("qk_T"), 1)
            evac(4 * NB, ACT.Copy)
            act.wait_ge(sem("at_max"), 1)
            for h in range(AH):
                a(AS[:, h, 0:P], AS[:, h, 0:P], ACT.Exp, bias=ST[:, 32 + h:33 + h], scale=AD ** -0.5,
                  accum_out=ST[:, 48 + h:49 + h]).then_inc(sem("at_exp"), 1)
                a(AS[:, h, P:3 * P], AS[:, h, P:3 * P], ACT.Exp, bias=ST[:, 40 + h:41 + h], scale=AD ** -0.5,
                  accum_out=ST[:, 56 + h:57 + h]).then_inc(sem("at_exp"), 1)
            evac(5 * NB, ACT.Copy)
            for q in range(6):
                act.wait_ge(sem("at_pT_raw"), q + 1)
                a(APT[:, 4 * q:4 * q + 4, :], PS[:, 4 + q % 4, :].rearrange("p (h t) -> p h t", h=4), ACT.Copy)\
                    .then_inc(sem("at_pT"), 1)
            evac(6 * NB, ACT.Sigmoid)
            for tt in range(TT):
                act.wait_ge(sem("u_T_raw"), tt + 1)
                a(UTv[:, :, 2 + tt * P:2 + (tt + 1) * P], PS[:, 4 + tt, :].rearrange("p (h t) -> p h t", h=4),
                  ACT.Copy).then_inc(sem("u_T"), 1)
            evac(7 * NB, ACT.Sigmoid)
            for tt in range(TT):
                act.wait_ge(sem("ya_T_raw"), tt + 1)
                a(YAT[:, :, tt * P:(tt + 1) * P], PS[:, 4 + tt, :].rearrange("p (h t) -> p h t", h=4), ACT.Copy)\
                    .then_inc(sem("ya_T"), 1)
            for tt in range(TT):
                act.wait_ge(sem("u_T_raw"), tt + 3)
                a(BGT[:, :, tt * P:(tt + 1) * P], PS[:, 6 + tt, :].rearrange("p (h t) -> p h t", h=4), ACT.Copy)\
                    .then_inc(sem("u_T"), 1)
            for b in range(8, 10):
                evac(b * NB, ACT.Sigmoid)
            for half in range(2):
                for tt in range(TT):
                    act.wait_ge(sem("mg_T_raw"), 2 * half + tt + 1)
                    a(MT[:, 4 * half:4 * half + 4, tt * P:(tt + 1) * P],
                      PS[:, 4 + 2 * tt + half, :].rearrange("p (h t) -> p h t", h=4), ACT.Copy)\
                        .then_inc(sem("mg_T"), 1)
            stream_squares(5)
            for q in range(4):
                tt, half = q // 2, q % 2
                act.wait_ge(sem("h2_raw"), q + 1)
                a(H2R[:, tt, half * NB:(half + 1) * NB], PS[:, 4 + q, :], ACT.Copy).then_inc(sem("h2_rows"), 1)
            act.wait_ge(sem("r_shift"), 1)
            a(ST[:, 80:88], ST[:, 72:80], ACT.Exp).then_inc(sem("r_exp"), 1)
            act.wait_ge(sem("r_diff"), 1)
            a(ST[:, 98:100], ST[:, 96:98], ACT.Exp).then_inc(sem("r_exp"), 1)
            n_rounds = rounds(act)

            def take_gather(n):
                act.wait_ge(sem("ex_gather"), n * 2 + 1)
                a(XG[:, 0:4, :], PS[:, 6, :].rearrange("p (k t) -> p k t", k=4), ACT.Copy).then_inc(sem("ex_xg0"), 1)

            def pair(n, last_pair):
                act.wait_ge(sem("block_used"), n * 6 + (B_MOE + 2))
                a(SGU, PS[:, 4, :], ACT.Silu).then_inc(sem("ex_silu"), 1)
                act.wait_ge(sem("ex_T"), n + 1)
                a(HIDT, PS[:, 4, :].rearrange("p (k t) -> p k t", k=4), ACT.Copy).then_inc(sem("ex_hT"), 1)
                if not last_pair:
                    take_gather(n + 1)
                act.wait_ge(sem("ex_y_raw"), n + 1)
                a(YSB[:, 0:NB], PS[:, 6, :], ACT.Copy).then_inc(sem("ex_y0"), 1)

            with act.Fori(0, n_rounds) as r:
                take_gather(r * PAIRS)
                with act.Fori(0, PAIRS - 1) as i:
                    pair(r * PAIRS + i, False)
                pair(r * PAIRS + (PAIRS - 1), True)

        @block.vector
        def _(dve):
            v = nc.vector
            chain = [0]

            def link(ins):
                chain[0] += 1
                ins.then_inc(sem("dve_step"), 1)
                dve.wait_ge(sem("dve_step"), chain[0])

            def tell(ins, name, value):
                ins.then_inc(sem(name), 1)
                dve.wait_ge(sem(name), value)

            rstd_n = [0]

            def rstd():
                rstd_n[0] += 1
                dve.wait_ge(sem("rstd_ready"), rstd_n[0])

            norm_n = [0]

            def norm(gain, shift=None):
                n = norm_n[0]
                for tt in range(TT):
                    rstd()
                    v.tensor_scalar(XN[:, tt, :], X[:, tt, :], ST[:, tt:tt + 1], None, ALU.mult)\
                        .then_inc(sem("xn_ready"), 1)
                if n == 0:
                    dve.wait_ge(sem("cols_taken"), 1)
                for q in range(4):
                    tt, half = q // 2, q % 2
                    dve.wait_ge(sem("xT_ready"), 4 * n + q + 1)
                    dst = HT[:, 4 * half:4 * half + 4, tt * P:(tt + 1) * P]
                    src = PS[:, 4 + q, :].rearrange("p (k t) -> p k t", k=4)
                    if shift is None:
                        v.tensor_tensor(dst, src, colb(gain[:, 4 * half:4 * half + 4], P), ALU.mult)\
                            .then_inc(sem("hT_ready"), 1)
                    else:
                        for j in range(4):
                            k = 4 * half + j
                            last = v.tensor_scalar(dst[:, j, :], src[:, j, :], gain[:, k:k + 1], shift[:, k:k + 1],
                                                   ALU.mult, ALU.add)
                        last.then_inc(sem("hT_ready"), 1)
                norm_n[0] += 1

            def residual(r):
                dve.wait_ge(sem("gain_in"), 16 * (r + 1))
                for tt in range(TT):
                    rstd()
                    y = PS[:, 2 * tt:2 * tt + 2, :]
                    xn = XN[:, tt, :].rearrange("p (a b) -> p a b", a=2)
                    link(v.scalar_tensor_tensor(xn, y, ST[:, 2 + tt:3 + tt],
                                                GB.rearrange("p (a b) -> p a b", a=2), ALU.mult, ALU.mult))
                    tell(v.tensor_tensor(X[:, tt, :], X[:, tt, :], XN[:, tt, :], ALU.add), "x_new", 2 * r + tt + 1)
                dve.sem_inc(sem("res_done"), 1)

            def modulation(l):
                dve.wait_ge(sem("mod_raw"), l + 1)
                link(v.tensor_tensor(MC[:, 2 * l:2 * l + 2, :].rearrange("p a b -> p (a b)"), PS[:, 4, 0:16],
                                     BC[:, 24 * l:24 * l + 16], ALU.add))
                if l == 0:
                    dve.wait_ge(sem("ga_in"), 32)
                ga = GA[:, l, :].rearrange("p (a b) -> p a b", a=2)
                link(v.tensor_tensor(ga, ga, PS[:, 6:8, :], ALU.add))

            def head_norm(src, sq, groups, width, g, gate, tmp, name, value, gate_at=None):
                v.tensor_reduce(ST[:, 16:16 + groups], sq, AX.X, ALU.add).then_inc(sem("sums_ready"), 1)
                rstd()
                link(v.tensor_tensor(tmp, src, colb(ST[:, 16:16 + groups], width), ALU.mult))
                link(v.tensor_tensor(tmp, tmp, midb(g, groups), ALU.mult))
                half = groups // 2
                if gate_at is not None:
                    dve.wait_ge(sem("proj_taken"), gate_at)
                for tt in range(TT):
                    tell(v.tensor_tensor(gate[tt], gate[tt], tmp[:, tt * half:(tt + 1) * half, :], ALU.mult),
                         name + "_half", 2 * (value - 1) + tt + 1)
                dve.sem_inc(sem(name), 1)

            dve.sem_inc(sem("ada_free"), 2)
            norm(GC[:, R_G:R_G + 8])
            dve.wait_ge(sem("lb_in"), 16)
            link(v.tensor_tensor(BO, LB[:, 0, :], LB[:, 1, :], ALU.max))
            link(v.tensor_tensor(BO, BO, LB[:, 2, :], ALU.max))
            tell(v.tensor_tensor(LB, LB, midb(BO, 3), ALU.subtract), "lb_shifted", 1)
            dve.wait_ge(sem("lb_exp"), 1)
            link(v.tensor_tensor(BO, LB[:, 0, :], LB[:, 1, :], ALU.add))
            link(v.tensor_tensor(BO, BO, LB[:, 2, :], ALU.add))
            link(v.reciprocal(BO, BO))
            link(v.tensor_tensor(BO, BO, LB[:, 0, :], ALU.mult))
            link(v.tensor_scalar(LB[:, 1, :], BO, -1.0, 1.0, ALU.mult, ALU.add))
            dve.wait_ge(sem("proj_taken"), 2)
            F = PR[:, :, NB:2 * NB]
            link(v.tensor_tensor(F, F, midb(LB[:, 1, :], 2), ALU.mult))
            tell(v.tensor_tensor(F, F, midb(BO, 2), ALU.add), "hg_f", 1)
            dve.wait_ge(sem("hg_fT_raw"), 1)
            for tt in range(TT):
                tell(v.tensor_scalar(KTT[:, :, tt * P:(tt + 1) * P],
                                     PS[:, 6 + tt, :].rearrange("p (h t) -> p h t", h=4),
                                     -1.0, 1.0, ALU.mult, ALU.add), "hg_kT", tt + 1)
            dve.wait_ge(sem("hg_bT"), 2)
            dve.wait_ge(sem("hg_qT"), 2)
            dve.wait_ge(sem("mix_in"), 16)

            def diffs(n):
                ex = EX[(n - 1) % 2]
                if n >= 3:
                    dve.wait_ge(sem("hg_ks"), n - 2)
                if n <= 7:
                    m = 1 << (n - 1)
                    bv = BT.rearrange("p h (n x m) -> p (h n) x m", x=2, m=m)
                    ev = ex.rearrange("p (n x m) -> p n x m", x=2, m=m)
                    groups = 1024 // (2 * m)
                    ref = bv[:, :, 0, m - 1:m].to_broadcast([P, groups, m])
                    if n == 7:
                        link(v.tensor_copy(ev[:, :, 1, :], bv[:, :, 1, :]))
                    else:
                        link(v.tensor_tensor(ev[:, :, 1, :], bv[:, :, 1, :], ref, ALU.subtract))
                    tell(v.tensor_tensor(ev[:, :, 0, :], ref, bv[:, :, 0, :], ALU.subtract), "hg_diff", n)
                else:
                    bv = BT.rearrange("p h (c m) -> p h c m", c=4)
                    ev = ex.rearrange("p (h c m) -> p h c m", h=4, c=4)

                    def end(c):
                        return bv[:, :, c, CH - 1:CH].to_broadcast([P, 4, CH])

                    link(v.tensor_copy(ev[:, :, 2, :], bv[:, :, 2, :]))
                    link(v.tensor_tensor(ev[:, :, 3, :], bv[:, :, 3, :], end(2), ALU.add))
                    link(v.tensor_tensor(ev[:, :, 1, :], end(1), bv[:, :, 1, :], ALU.subtract))
                    link(v.tensor_tensor(ev[:, :, 0, :], end(0), bv[:, :, 0, :], ALU.subtract))
                    tell(v.tensor_tensor(ev[:, :, 0, :], ev[:, :, 0, :], end(1), ALU.add), "hg_diff", n)

            def masked(n):
                dve.wait_ge(sem("hg_prod"), n + 1)
                bank = 4 + 2 * (n % 2)
                src = PS[:, bank:bank + 2, :].rearrange("p b (h t) -> p (b h) t", h=4)
                mask = midb(MX[:, M_LEV + n * P:M_LEV + (n + 1) * P], 8)
                if n == 0:
                    tell(v.tensor_tensor(SC, src, mask, ALU.mult), "hg_masked", 1)
                else:
                    t = TMP.rearrange("p (g t) -> p g t", g=8)
                    link(v.tensor_tensor(t, src, mask, ALU.mult))
                    tell(v.tensor_tensor(SC, SC, t, ALU.add), "hg_masked", n + 1)

            diffs(1)
            diffs(2)
            masked(0)
            for n in range(1, 9):
                dve.wait_ge(sem("hg_exp"), n)
                if n >= 3:
                    dve.wait_ge(sem("hg_prod"), n - 1)
                tell(v.tensor_tensor(QS[(n - 1) % 2], QT, EX[(n - 1) % 2].rearrange("p (a b) -> p a b", a=4),
                                     ALU.mult), "hg_qs", n)
                if n + 2 <= 8:
                    diffs(n + 2)
                if n >= 2:
                    masked(n - 1)
            dve.wait_ge(sem("hg_sq"), 1)
            dve.wait_ge(sem("head_in"), 80)
            gate = [PR[:, tt, 1536:2048].rearrange("p (h d) -> p h d", h=4) for tt in range(TT)]
            dve.wait_ge(sem("proj_taken"), 4)
            head_norm(PS[:, 6:8, :].rearrange("p b (h d) -> p (b h) d", h=4),
                      HB[:, 0:1024].rearrange("p (g d) -> p g d", g=8), 8, HG_D, HN[:, 0:128], gate,
                      ar(6 * K1, 8, 128), "ev_y", 1)
            for h in range(4):
                dve.wait_ge(sem("ret_s"), h + 1)
                tell(v.tensor_tensor(PT[:, h, :], PS[:, 4 + h, 0:3 * P],
                                     MX[:, M_DEC + h * 3 * P:M_DEC + (h + 1) * 3 * P], ALU.mult), "ret_p", h + 1)

            dve.wait_ge(sem("ret_sq"), 1)
            gate = [PR[:, tt, 4096:5120].rearrange("p (h d) -> p h d", h=4) for tt in range(TT)]
            dve.wait_ge(sem("proj_taken"), 10)
            head_norm(PS[:, 4:8, :].rearrange("p b (h d) -> p (b h) d", h=2),
                      HB.rearrange("p (g d) -> p g d", g=8), 8, RV_D, HN[:, 128:384], gate,
                      ar(6 * K1, 8, 256), "ev_y", 2)
            residual(0)
            norm(GC[:, R_G + 8:R_G + 16])

            def hidden(l, i, g):
                h = g % 2
                for j in range(2):
                    dve.wait_ge(sem("hid_relu"), i * 4 + (2 * NGRP * l + 2 * g + j + 1))
                    v.tensor_tensor(H1[h][:, 2 * j:2 * j + 2, :], HR[2 * h + j], HR[2 * h + j], ALU.mult)\
                        .then_inc(sem("hid_ready"), 1)

            def ada_sums(l, i, x):
                j = i * 2 + (ADA * l + x)
                dve.wait_ge(sem(f"ada{x}_full"), i * 16 + 16 * (ADA // 2 * l + 1))
                acc = AC[:, bass.ds(i * 2 + x, 1), :].rearrange("p a b -> p (a b)")
                v.tensor_scalar(acc, AW[x][:, 0, :], CS[:, 0:1], None, ALU.mult).then_inc(sem("ada_step"), 1)
                for k in range(1, KT):
                    dve.wait_ge(sem("ada_step"), j * (KT - 1) + k)
                    v.scalar_tensor_tensor(acc, AW[x][:, k, :], CS[:, k:k + 1], acc, ALU.mult, ALU.add)\
                        .then_inc(sem("ada_step" if k < KT - 1 else "ada_sum"), 1)
                dve.wait_ge(sem("ada_sum"), j + 1)
                dve.sem_inc(sem("ada_free"), 1)

            def mlp(l):
                if l == 0:
                    dve.wait_ge(sem("c_silu"), 1)
                for g in (0, 1):
                    hidden(l, 0, g)
                with dve.Fori(0, (NGRP - 2) // 2) as i:
                    for g in (2, 3):
                        hidden(l, i, g)
                        ada_sums(l, i, g - 2)

            mlp(0)
            residual(1)
            modulation(0)
            norm(GC[:, R_G + 16:R_G + 24])
            dve.wait_ge(sem("gate_in"), 48)
            tell(v.tensor_scalar(G4[:, 2:4], G4[:, 0:2], 1.0 / GCAP, None, ALU.mult), "gate_b", 1)
            tell(v.memset(CRv[:, :, 0:3], 0.0), "pad", 1)
            dve.wait_ge(sem("g_softplus"), 1)
            link(v.memset(GR[:, 7, :], 1.0))
            link(v.tensor_tensor_scan(GR[:, 1, :], GR[:, 7, :], GR[:, 2, :], 0.0, ALU.mult, ALU.subtract))
            link(v.scalar_tensor_tensor(GR[:, 3, :], GR[:, 0, :], GCAP, GR[:, 1, :], ALU.mult, ALU.subtract))
            link(v.tensor_tensor_scan(GR[:, 4, :], GR[:, 3, :], GR[:, 3, :], 0.0, ALU.max, ALU.max))
            tell(v.tensor_tensor(GR[:, 5, :], GR[:, 1, :], GR[:, 4, :], ALU.add), "g_m", 1)
            for c in range(8):
                if c % 4 == 0:
                    dve.wait_ge(sem("conv_T"), 3 + c // 4)

                def tap(j, c=c):
                    return GC[:, R_CW + 8 * j + c:R_CW + 8 * j + c + 1]
                link(v.tensor_scalar(CT[:, c, :], CRv[:, c, 0:T], tap(0), GC[:, R_CB + c:R_CB + c + 1],
                                     ALU.mult, ALU.add))
                for j in range(1, 4):
                    link(v.scalar_tensor_tensor(CT[:, c, :], CRv[:, c, j:j + T], tap(j), CT[:, c, :],
                                                ALU.mult, ALU.add))
            dve.sem_inc(sem("conv_sum"), 1)
            dve.wait_ge(sem("acol_raw"), 1)
            link(v.tensor_copy(ST[:, 112:128], PS[:, 4, 0:16]))
            dve.wait_ge(sem("mrow_raw"), 1)
            for h in range(4):
                m = PS[:, 5 + h // 2, (h % 2) * T:(h % 2 + 1) * T]
                link(v.tensor_scalar(HBW[:, h, 0:T], m, ST[:, 112 + h:113 + h], 0.0, ALU.subtract, ALU.max))
                link(v.tensor_scalar(HBW[:, h, T:3 * P], m[:, P:T], ST[:, 116 + h:117 + h], 0.0,
                                     ALU.subtract, ALU.max))
            dve.sem_inc(sem("wexp_in"), 1)
            dve.wait_ge(sem("wexp"), 1)
            for at in (0, T):
                link(v.tensor_tensor(HBW[:, :, at:at + P], HBW[:, :, at:at + P],
                                     midb(CK[:, C_CAU:C_CAU + P], 4), ALU.mult))
            for h in range(4):
                dve.wait_ge(sem("ml_s"), h + 1)
                tell(v.scalar_tensor_tensor(PT[:, h, :], PS[:, 4 + h, 0:3 * P], QK ** -0.5, HBW[:, h, :],
                                            ALU.mult, ALU.mult), "ml_p", h + 1)
            dve.wait_ge(sem("ml_out"), 1)
            link(v.scalar_tensor_tensor(ST[:, 128:136], PS[:, 0, 0:8], -1.0, ST[:, 120:128], ALU.mult, ALU.max))
            link(v.tensor_tensor(ST[:, 128:136], PS[:, 0, 0:8], ST[:, 128:136], ALU.max))
            link(v.reciprocal(ST[:, 128:136], ST[:, 128:136]))
            tell(v.tensor_tensor(HB.rearrange("p (g d) -> p g d", g=8),
                                 PS[:, 4:8, :].rearrange("p b (h d) -> p (b h) d", h=2),
                                 colb(ST[:, 128:136], RV_D), ALU.mult), "ml_o", 1)
            dve.wait_ge(sem("ml_sq"), 1)
            gate = [PR[:, tt, 2048:3072].rearrange("p (h d) -> p h d", h=4) for tt in range(TT)]
            head_norm(HB.rearrange("p (g d) -> p g d", g=8),
                      XN[:, :, :].rearrange("p a (g d) -> p (a g) d", d=256), 8, RV_D, HN[:, 384:640], gate,
                      HB.rearrange("p (g d) -> p g d", g=8), "od_y", 1, gate_at=EV_IN + OD_IN)
            residual(2)
            norm(GC[:, R_G + 24:R_G + 32])
            mlp(1)
            residual(3)
            modulation(1)

            for i in range(2):
                link(v.scalar_tensor_tensor(GM[:, i, :], MC[:, 2 * i + 1, :], 1.0,
                                            GC[:, (R_G1, R_G2)[i]:(R_G1, R_G2)[i] + 8], ALU.add, ALU.mult))
            norm(GM[:, 0, :], MC[:, 0, :])
            dve.wait_ge(sem("qk_sq"), 1)
            v.tensor_reduce(ST[:, 128:160], HB.rearrange("p (g d) -> p g d", d=AD), AX.X, ALU.add)\
                .then_inc(sem("sums_ready"), 1)
            rstd()
            for tt in range(TT):
                qk = PR[:, tt, 0:1024].rearrange("p (g d) -> p g d", d=AD)
                link(v.tensor_tensor(qk, qk, colb(ST[:, 128 + 16 * tt:144 + 16 * tt], AD), ALU.mult))
                for i in range(2):
                    link(v.tensor_tensor(qk[:, 8 * i:8 * i + 8, :], qk[:, 8 * i:8 * i + 8, :],
                                         midb(HN[:, 640 + 64 * i:704 + 64 * i], 8), ALU.mult))
                cos = midb(CK[:, C_CS2 + tt * 8:C_CS2 + tt * 8 + 8], 16)
                sin = midb(CK[:, C_CS2 + 16 + tt * 8:C_CS2 + 24 + tt * 8], 16)
                x1, x2 = qk[:, :, 0:8], qk[:, :, 8:16]
                t = [ar(6 * K1 + 128 * i, 16, 8) for i in range(4)]
                link(v.tensor_tensor(t[0], x1, cos, ALU.mult))
                link(v.tensor_tensor(t[1], x2, sin, ALU.mult))
                link(v.tensor_tensor(t[2], x2, cos, ALU.mult))
                link(v.tensor_tensor(t[3], x1, sin, ALU.mult))
                link(v.tensor_tensor(x1, t[0], t[1], ALU.subtract))
                link(v.tensor_tensor(x2, t[2], t[3], ALU.add))
            dve.sem_inc(sem("qk_ready"), 1)
            E0 = EV_IN + OD_IN
            for h in range(AH):
                dve.wait_ge(sem("at_s_raw"), h + 1)
                tell(v.tensor_tensor(AS[:, h, :], PS[:, 4 + h % 4, 0:3 * P], CK[:, C_NEG:C_NEG + 3 * P], ALU.add),
                     "at_s", h + 1)
            link(v.tensor_reduce(ST[:, 32:40], AS[:, :, 0:P], AX.X, ALU.max))
            link(v.tensor_reduce(ST[:, 40:48], AS[:, :, P:3 * P], AX.X, ALU.max))
            tell(v.tensor_scalar(ST[:, 32:48], ST[:, 32:48], -(AD ** -0.5), None, ALU.mult), "at_max", 1)
            dve.wait_ge(sem("proj_taken"), E0 + 6)
            link(v.memset(UTv[:, :, 0:2], 0.0))
            tell(v.tensor_tensor(PR[:, :, 1536:2048], PR[:, :, 1536:2048], PR[:, :, 2560:3072], ALU.mult),
                 "u_ready", 1)
            dve.wait_ge(sem("at_exp"), 2 * AH)
            link(v.reciprocal(ST[:, 48:64], ST[:, 48:64]))
            dve.wait_ge(sem("at_o"), 1)
            tell(v.tensor_tensor(YA.rearrange("p t (h d) -> p (t h) d", h=AH),
                                 PS[:, 6:8, :].rearrange("p b (h d) -> p (b h) d", h=AH),
                                 colb(ST[:, 48:64], AD), ALU.mult), "ya_ready", 1)
            dve.wait_ge(sem("u_T"), 4)
            for c in range(4):
                def tap2(j, c=c):
                    return GC[:, R_CW2 + 4 * j + c:R_CW2 + 4 * j + c + 1]
                y = YBT[:, c, :]
                link(v.tensor_scalar(y, UTv[:, c, 0:T], tap2(0), GC[:, R_CB2 + c:R_CB2 + c + 1],
                                     ALU.mult, ALU.add))
                for j in range(1, 3):
                    link(v.scalar_tensor_tensor(y, UTv[:, c, j:j + T], tap2(j), y, ALU.mult, ALU.add))
                link(v.tensor_tensor(y, y, BGT[:, c, :], ALU.mult))
            dve.sem_inc(sem("yb_ready"), 1)
            dve.wait_ge(sem("block_used"), B_PA + 1)
            dve.wait_ge(sem("proj_taken"), E0 + 8)
            ga = [PR[:, :, 3072 + h * NB:3072 + (h + 1) * NB] for h in range(2)]
            gb = [PR[:, :, 4096 + h * NB:4096 + (h + 1) * NB] for h in range(2)]
            for half in range(2):
                for tt in range(TT):
                    link(v.tensor_tensor(ga[half][:, tt, :], ga[half][:, tt, :], PS[:, 4 + 2 * tt + half, :], ALU.mult))
            dve.sem_inc(sem("pa_taken"), 1)
            dve.wait_ge(sem("block_used"), B_PB + 1)
            for half in range(2):
                dve.wait_ge(sem("proj_taken"), E0 + 9 + half)
                for tt in range(TT):
                    link(v.tensor_tensor(gb[half][:, tt, :], gb[half][:, tt, :], PS[:, 4 + 2 * tt + half, :], ALU.mult))
                tell(v.tensor_tensor(ga[half], ga[half], gb[half], ALU.add), "merged", half + 1)

            def gated_residual(i, waits):
                for tt in range(TT):
                    dve.wait_ge(sem(waits[tt][0]), waits[tt][1])
                    y = PS[:, 2 * tt:2 * tt + 2, :].rearrange("p a b -> p (a b)")
                    gated = (XN, H2R)[i][:, tt, :]
                    link(v.tensor_tensor(gated, y, GA[:, i, :], ALU.mult))
                    tell(v.tensor_tensor(X[:, tt, :], X[:, tt, :], gated, ALU.add),
                         ("x_new", "x_final")[i], (9, 1)[i] + tt)

            v.memset(ZERO, 0.0).then_inc(sem("zeroed"), 1)
            gated_residual(0, (("y_tile0", 5), ("block_used", B_WO + WO)))
            norm(GM[:, 1, :], MC[:, 2, :])
            dve.wait_ge(sem("router_raw"), 1)
            scratch = PRF[:, 2 * BW + D:2 * BW + 2 * D]
            L = scratch[:, 0:TT * (NG + NE)].rearrange("p (t n) -> p t n", t=TT)
            link(v.tensor_tensor(L, PS[:, 4, 0:128].rearrange("p (t n) -> p t n", t=2)[:, :, 0:NG + NE],
                                 midb(RB[:, :], TT), ALU.add))
            dve.sem_inc(sem("router_taken"), 1)
            gl = L[:, :, 0:NG]
            el = L[:, :, NG:NG + NE].rearrange("p t (g e) -> p t g e", g=NG)

            def st(at, a, b, c=1):
                at += 128
                flat = scratch[:, at:at + a * b * c]
                if c == 1:
                    return flat.rearrange("p (a b) -> p a b", a=a)
                return flat.rearrange("p (a b c) -> p a b c", a=a, b=b)

            def first_max(x, width, mx, hot):
                link(v.tensor_reduce(mx, x, AX.X, ALU.max))
                link(v.tensor_tensor(hot, x, colb(mx, width), ALU.is_equal))
                link(v.tensor_tensor(hot, hot, midb(CK[:, C_FIRST:C_FIRST + width], TT), ALU.mult))
                link(v.tensor_reduce(ST[:, 140:142], hot, AX.X, ALU.max))
                link(v.tensor_tensor(hot, hot, colb(ST[:, 140:142], width), ALU.is_equal))

            hg = st(0, TT, NG)
            first_max(gl, NG, ST[:, 64:66], hg)
            tell(v.tensor_tensor(ST[:, 72:80].rearrange("p (t g) -> p t g", t=TT), gl, colb(ST[:, 64:66], NG),
                                 ALU.subtract), "r_shift", 1)
            sel = st(64, TT, EG, NG)
            for tt in range(TT):
                link(v.tensor_tensor(sel[:, tt, :, :], el[:, tt, :, :].rearrange("p g e -> p e g"),
                                     midb(hg[:, tt, :], EG), ALU.mult))
            le = st(192, TT, EG)
            link(v.tensor_reduce(le, sel, AX.X, ALU.add))
            h1, h2 = st(256, TT, EG), st(320, TT, EG)
            first_max(le, EG, ST[:, 66:68], h1)
            link(v.scalar_tensor_tensor(le, h1, -BIG, le, ALU.mult, ALU.add))
            first_max(le, EG, ST[:, 68:70], h2)
            tell(v.tensor_tensor(ST[:, 96:98], ST[:, 68:70], ST[:, 66:68], ALU.subtract), "r_diff", 1)
            link(v.tensor_tensor(st(384, TT, EG), h1, h2, ALU.add))
            for tt in range(TT):
                link(v.tensor_tensor(SEL[:, tt, :].rearrange("p (g e) -> p g e", g=NG), colb(hg[:, tt, :], EG),
                                     midb(st(384, TT, EG)[:, tt, :], NG), ALU.mult))
            dve.sem_inc(sem("chosen"), 1)
            PLACE = CK[:, C_PLACE:C_PLACE + CAP].unsqueeze(1).unsqueeze(1).to_broadcast([P, TT, 2, CAP])

            def of_pair(table, i):
                return table[:, :, bass.ds(i * 2, 2)].unsqueeze(3).to_broadcast([P, TT, 2, CAP])

            def places(i):
                v.tensor_tensor(SEL1, PLACE, of_pair(RK, i), ALU.is_equal).then_inc(sem("ex_places"), 1)

            dve.wait_ge(sem("places_raw"), 1)
            link(v.tensor_tensor(RK, PS[:, 4, 0:2 * NE].rearrange("p (t e) -> p t e", t=TT), SEL, ALU.mult))
            link(v.tensor_reduce(ST[:, 0:1], PS[:, 4, 64:64 + NE], AX.X, ALU.max))
            places(0)
            link(v.tensor_scalar(ST[:, 4:8], CK[:, C_STEP:C_STEP + T // CAP], ST[:, 0:1], None, ALU.is_lt))
            link(v.tensor_reduce(ST[:, 1:2], ST[:, 4:8], AX.X, ALU.add))
            link(v.tensor_copy(RNDS[:, :], ST[:, 1:2]))
            dve.sem_inc(sem("rounds"), 1)
            dve.wait_ge(sem("r_exp"), 2)
            link(v.tensor_reduce(ST[:, 100:102], ST[:, 80:88].rearrange("p (t g) -> p t g", t=TT), AX.X, ALU.add))
            link(v.tensor_scalar(ST[:, 102:104], ST[:, 98:100], 1.0, None, ALU.add))
            link(v.tensor_tensor(ST[:, 102:104], ST[:, 102:104], ST[:, 100:102], ALU.mult))
            link(v.reciprocal(ST[:, 102:104], ST[:, 102:104]))
            link(v.tensor_tensor(ST[:, 98:100], ST[:, 98:100], ST[:, 102:104], ALU.mult))
            link(v.tensor_tensor(h1, h1, colb(ST[:, 102:104], EG), ALU.mult))
            link(v.tensor_tensor(h2, h2, colb(ST[:, 98:100], EG), ALU.mult))
            link(v.tensor_tensor(h1, h1, h2, ALU.add))
            for tt in range(TT):
                link(v.tensor_tensor(CWC[:, tt, :].rearrange("p (g e) -> p g e", g=NG), colb(hg[:, tt, :], EG),
                                     midb(h1[:, tt, :], NG), ALU.mult))
            n_rounds = rounds(dve)

            def weights(n, i):
                dve.wait_ge(sem("ex_places"), n + 1)
                v.tensor_tensor(SELW, SEL1, of_pair(CWC, i), ALU.mult).then_inc(sem("ex_weights"), 1)

            def take_gather(n):
                dve.wait_ge(sem("ex_gather"), n * 2 + 2)
                v.tensor_copy(XG[:, 4:8, :], PS[:, 7, :].rearrange("p (k t) -> p k t", k=4))\
                    .then_inc(sem("ex_xg1"), 1)

            def pair(n, i, last_pair):
                dve.wait_ge(sem("ex_silu"), n + 1)
                dve.wait_ge(sem("block_used"), n * 6 + (B_MOE + 4))
                v.tensor_tensor(HIDR, SGU, PS[:, 5, :], ALU.mult).then_inc(sem("ex_hid"), 1)
                if not last_pair:
                    dve.wait_ge(sem("ex_weights"), n + 1)
                    places(i + 1)
                dve.wait_ge(sem("ex_swT_raw"), n + 1)
                v.tensor_copy(SWT, PS[:, 5, 0:T]).then_inc(sem("ex_swT"), 1)
                if not last_pair:
                    weights(n + 1, i + 1)
                    take_gather(n + 1)
                dve.wait_ge(sem("block_used"), n * 6 + (B_MOE + 6))
                v.tensor_copy(YSB[:, NB:D], PS[:, 7, :]).then_inc(sem("ex_y1"), 1)

            with dve.Fori(0, n_rounds) as r:
                weights(r * PAIRS, 0)
                take_gather(r * PAIRS)
                with dve.Fori(0, PAIRS - 1) as i:
                    pair(r * PAIRS + i, i, False)
                pair(r * PAIRS + (PAIRS - 1), PAIRS - 1, True)
                v.tensor_scalar(RK, RK, -float(CAP), None, ALU.add).then_inc(sem("next_places"), 1)
                dve.wait_ge(sem("next_places"), r + 1)
                places(0)
            gated_residual(1, (("moe_tile0", n_rounds), ("moe_tile1", n_rounds)))


_IN = ["x", "norm_g", "hg_lower_bound", "ev_w_in", "ev_hg_norm_g", "ev_ret_norm_g", "ev_w_out", "od_w_in",
       "od_conv_w", "od_conv_b", "od_gate_b", "od_ml_norm_g", "od_w_out", "mlp_w1", "mlp_w2", "c_2", "w_ada_2",
       "b_ada_2", "g_norm1_2", "g_norm2_2", "w_in_2", "g_q_2", "g_k_2", "conv_w_2", "conv_b_2", "w_pa_2",
       "w_pb_2", "w_o_2", "w_rg_2", "b_rg_2", "w_re_2", "b_re_2", "w1_2", "w3_2", "w2_2"]


def kernel(**inputs):
    import concourse.bacc as bacc
    from concourse.bass_utils import run_bass_kernel_spmd

    nc = bacc.Bacc("TRN2", target_bir_lowering=False, num_devices=1)
    keep, mix = shape_constants()
    arrays, A = {}, {}
    for name in _IN:
        arrays[f"in_{name}"] = np.ascontiguousarray(inputs[name])
    arrays["in_keep"], arrays["in_mix"] = keep, mix
    for name, a in arrays.items():
        A[name[3:]] = nc.dram_tensor(name, a.shape, F32, kind="ExternalInput").ap()
    out = nc.dram_tensor("out", (1, T, D), F32, kind="ExternalOutput").ap()
    block_program(nc, A, out)
    r = run_bass_kernel_spmd(nc, [arrays], core_ids=[0])
    return r.results[0]["out"]
```
